# Optimizing a Trainium2 kernel written in Bass

```python
import math
import jax
import jax.numpy as jnp
from jax import lax
import numpy as np

D_MODEL = 1024
BATCH = 1
SEQ = 512
DEPTH = 2

HEAD_DIM = 64
MIX_WIDTH = D_MODEL
A_HEADS = 4
DIFF_QK_DIM = HEAD_DIM // 2
DIFF_V_DIM = HEAD_DIM
B_HEADS = 6
C_HEADS = 6
DILATED_PATTERNS = ((128, 1), (512, 4), (2048, 16))
Q_BLOCK = 128
ROPE_THETA = 10000.0
D_FF = 2816
CONV_WIDTH = 3
NORM_EPS = 1e-6
SUBLN_EPS = 1e-5
FORGET_BIAS_INIT = 4.0

A_Q = A_HEADS * 2 * DIFF_QK_DIM
A_K = A_HEADS * 2 * DIFF_QK_DIM
A_V = A_HEADS * DIFF_V_DIM
B_W = B_HEADS * HEAD_DIM
C_W = C_HEADS * HEAD_DIM
IN_COLS = A_Q + A_K + A_V + 3 * B_W + 3 * C_W + C_HEADS


def rmsnorm(x, g, eps=NORM_EPS):
    xf = x.astype(jnp.float32)
    y = xf * lax.rsqrt(jnp.mean(xf * xf, axis=-1, keepdims=True) + eps)
    return (y * g.astype(jnp.float32)).astype(x.dtype)

def rope_tables(seq, dim):
    inv = 1.0 / (ROPE_THETA ** (jnp.arange(0, dim, 2, dtype=jnp.float32) / dim))
    ang = jnp.arange(seq, dtype=jnp.float32)[:, None] * inv[None, :]
    return jnp.cos(ang), jnp.sin(ang)

def apply_rope(x, cos, sin):
    half = x.shape[-1] // 2
    xf = x.astype(jnp.float32)
    x1, x2 = xf[..., :half], xf[..., half:]
    out = jnp.concatenate([x1 * cos - x2 * sin, x2 * cos + x1 * sin], axis=-1)
    return out.astype(x.dtype)

def diff_attention(q, k, v, lam):
    bn, h, _, t, dk = q.shape
    nb = t // Q_BLOCK
    qb = q.reshape(bn, h, 2, nb, Q_BLOCK, dk).transpose(3, 0, 1, 2, 4, 5)
    kpos = jnp.arange(t)
    scale = dk ** -0.5
    vf = v.astype(jnp.float32)

    def block(args):
        qblk, bi = args
        s = jnp.einsum('bhmqd,bhmkd->bhmqk', qblk, k).astype(jnp.float32) * scale
        qpos = bi * Q_BLOCK + jnp.arange(Q_BLOCK)
        s = jnp.where(kpos[None, :] <= qpos[:, None], s, -jnp.inf)
        p = jax.nn.softmax(s, axis=-1)
        a = p[:, :, 0] - lam * p[:, :, 1]
        return jnp.einsum('bhqk,bhkd->bhqd', a, vf)

    o = lax.map(block, (qb, jnp.arange(nb)))
    return o.transpose(1, 2, 0, 3, 4).reshape(bn, h, t, -1)

def forgetting_attention(q, k, v, cum_logf):
    bn, h, t, hd = q.shape
    nb = t // Q_BLOCK
    qb = q.reshape(bn, h, nb, Q_BLOCK, hd).transpose(2, 0, 1, 3, 4)
    fb = cum_logf.reshape(bn, h, nb, Q_BLOCK).transpose(2, 0, 1, 3)
    kpos = jnp.arange(t)
    scale = hd ** -0.5
    vf = v.astype(jnp.float32)

    def block(args):
        qblk, fq, bi = args
        s = jnp.einsum('bhqd,bhkd->bhqk', qblk, k).astype(jnp.float32) * scale
        s = s + fq[..., :, None] - cum_logf[..., None, :]
        qpos = bi * Q_BLOCK + jnp.arange(Q_BLOCK)
        s = jnp.where(kpos[None, :] <= qpos[:, None], s, -jnp.inf)
        p = jax.nn.softmax(s, axis=-1)
        return jnp.einsum('bhqk,bhkd->bhqd', p, vf)

    o = lax.map(block, (qb, fb, jnp.arange(nb)))
    return o.transpose(1, 2, 0, 3, 4).reshape(bn, h, t, hd)

def banded_window_attention(q, k, v, w):
    bn, g, l, hd = q.shape
    nb = l // w
    qb = q.reshape(bn, g, nb, w, hd)

    def with_prev(a):
        a = a.reshape(bn, g, nb, w, hd)
        prev = jnp.pad(a, ((0, 0), (0, 0), (1, 0), (0, 0), (0, 0)))[:, :, :-1]
        return jnp.concatenate([prev, a], axis=3)

    kk, vv = with_prev(k), with_prev(v)
    s = jnp.einsum('bgnqd,bgnkd->bgnqk', qb, kk).astype(jnp.float32) * (hd ** -0.5)
    dist = jnp.arange(w)[:, None] + w - jnp.arange(2 * w)[None, :]
    kidx = jnp.arange(nb)[:, None] * w + jnp.arange(2 * w)[None, :] - w
    mask = ((dist >= 0) & (dist <= w))[None, :, :] & (kidx >= 0)[:, None, :]
    s = jnp.where(mask, s, -jnp.inf)
    m = jnp.max(s, axis=-1, keepdims=True)
    p = jnp.exp(s - m)
    den = jnp.sum(p, axis=-1, keepdims=True)
    o = jnp.einsum('bgnqk,bgnkd->bgnqd', p, vv.astype(jnp.float32)) / den
    lse = (m + jnp.log(den))[..., 0]
    return o.reshape(bn, g, l, hd), lse.reshape(bn, g, l)

def dilated_mixture_attention(q, k, v):
    bn, h, t, hd = q.shape
    outs, lses = [], []
    for window, d in DILATED_PATTERNS:
        l = t // d
        w = window // d
        lp = -(-l // w) * w

        def fold(a):
            a = a.reshape(bn, h, l, d, hd).transpose(0, 1, 3, 2, 4).reshape(bn, h * d, l, hd)
            return jnp.pad(a, ((0, 0), (0, 0), (0, lp - l), (0, 0)))

        o, lse = banded_window_attention(fold(q), fold(k), fold(v), w)
        o = o[:, :, :l].reshape(bn, h, d, l, hd).transpose(0, 1, 3, 2, 4).reshape(bn, h, t, hd)
        lse = lse[:, :, :l].reshape(bn, h, d, l).transpose(0, 1, 3, 2).reshape(bn, h, t)
        outs.append(o)
        lses.append(lse)
    wts = jax.nn.softmax(jnp.stack(lses, axis=0), axis=0)
    return jnp.sum(wts[..., None] * jnp.stack(outs, axis=0), axis=0)

def causal_depthwise_conv(g, w, b):
    t = g.shape[1]
    gp = jnp.pad(g, ((0, 0), (CONV_WIDTH - 1, 0), (0, 0)))
    y = b
    for i in range(CONV_WIDTH):
        y = y + gp[:, i:i + t] * w[i]
    return y

def mixer_layer(h, w_in, w_out, lam_params, subln_g, forget_bias, lam_init, cos_a, sin_a, cos_b, sin_b):
    bn, t, _ = h.shape
    proj = h @ w_in
    cuts = np.cumsum([A_Q, A_K, A_V, B_W, B_W, B_W, C_W, C_W, C_W])
    qa, ka, va, qb, kb, vb, qc, kc, vc, fz = jnp.split(proj, cuts, axis=-1)

    qa = apply_rope(qa.reshape(bn, t, A_HEADS, 2, DIFF_QK_DIM).transpose(0, 2, 3, 1, 4), cos_a, sin_a)
    ka = apply_rope(ka.reshape(bn, t, A_HEADS, 2, DIFF_QK_DIM).transpose(0, 2, 3, 1, 4), cos_a, sin_a)
    va = va.reshape(bn, t, A_HEADS, DIFF_V_DIM).transpose(0, 2, 1, 3)
    lp = lam_params.astype(jnp.float32)
    lam = jnp.exp(jnp.sum(lp[0] * lp[1])) - jnp.exp(jnp.sum(lp[2] * lp[3])) + lam_init
    oa = diff_attention(qa, ka, va, lam)
    oa = oa * lax.rsqrt(jnp.mean(oa * oa, axis=-1, keepdims=True) + SUBLN_EPS)
    oa = oa * subln_g.astype(jnp.float32) * (1.0 - lam_init)

    def heads(a, n):
        return a.reshape(bn, t, n, HEAD_DIM).transpose(0, 2, 1, 3)
    qb = apply_rope(heads(qb, B_HEADS), cos_b, sin_b)
    kb = apply_rope(heads(kb, B_HEADS), cos_b, sin_b)
    ob = dilated_mixture_attention(qb, kb, heads(vb, B_HEADS))

    logf = jax.nn.log_sigmoid((fz + forget_bias).astype(jnp.float32))
    cum_logf = lax.cumsum(logf, axis=1).transpose(0, 2, 1)
    oc = forgetting_attention(heads(qc, C_HEADS), heads(kc, C_HEADS), heads(vc, C_HEADS), cum_logf)

    def merge(o):
        return o.transpose(0, 2, 1, 3).reshape(bn, t, -1)
    o = jnp.concatenate([merge(oa), merge(ob), merge(oc)], axis=-1).astype(h.dtype)
    return o @ w_out

def first_inputs(seed: int = 0) -> dict:
    key = jax.random.key(seed)
    ks = jax.random.split(key, 18)
    f32 = jnp.float32
    n = jax.random.normal
    return {
        'x': n(ks[0], (BATCH, SEQ, D_MODEL), f32),
        'c': n(ks[1], (BATCH, D_MODEL), f32),
        'w_mod': n(ks[2], (DEPTH, D_MODEL, 6 * D_MODEL), f32) * (0.5 * D_MODEL ** -0.5),
        'b_mod': n(ks[3], (DEPTH, 6 * D_MODEL), f32) * 0.02,
        'g_attn': 1.0 + 0.02 * n(ks[4], (DEPTH, D_MODEL), f32),
        'w_in': n(ks[5], (DEPTH, D_MODEL, IN_COLS), f32) * D_MODEL ** -0.5,
        'diff_lambda': n(ks[6], (DEPTH, 4, DIFF_QK_DIM), f32) * 0.1,
        'subln_g': 1.0 + 0.02 * n(ks[7], (DEPTH, DIFF_V_DIM), f32),
        'forget_bias': FORGET_BIAS_INIT + 0.5 * n(ks[8], (DEPTH, C_HEADS), f32),
        'w_out': n(ks[9], (DEPTH, MIX_WIDTH, D_MODEL), f32) * MIX_WIDTH ** -0.5,
        'g_mlp': 1.0 + 0.02 * n(ks[10], (DEPTH, D_MODEL), f32),
        'w_up': n(ks[11], (DEPTH, D_MODEL, 2 * D_FF), f32) * D_MODEL ** -0.5,
        'conv_w': n(ks[12], (DEPTH, CONV_WIDTH, D_FF), f32) * CONV_WIDTH ** -0.5,
        'conv_b': n(ks[13], (DEPTH, D_FF), f32) * 0.02,
        'w_down': n(ks[14], (DEPTH, D_FF, D_MODEL), f32) * D_FF ** -0.5,
        'g_final': 1.0 + 0.02 * n(ks[15], (D_MODEL,), f32),
    }

def first_block(x, c, w_mod, b_mod, g_attn, w_in, diff_lambda, subln_g, forget_bias, w_out,
              g_mlp, w_up, conv_w, conv_b, w_down, g_final):
    t = x.shape[1]
    cos_a, sin_a = rope_tables(t, DIFF_QK_DIM)
    cos_b, sin_b = rope_tables(t, HEAD_DIM)
    sc = jax.nn.silu(c)
    for layer in range(DEPTH):
        lam_init = 0.8 - 0.6 * math.exp(-0.3 * layer)
        mod = sc @ w_mod[layer] + b_mod[layer]
        shift1, scale1, gate1, shift2, scale2, gate2 = [m[:, None, :] for m in jnp.split(mod, 6, axis=-1)]

        h = rmsnorm(x, g_attn[layer]) * (1.0 + scale1) + shift1
        o = mixer_layer(h, w_in[layer], w_out[layer], diff_lambda[layer], subln_g[layer],
                        forget_bias[layer], lam_init, cos_a, sin_a, cos_b, sin_b)
        x = x + gate1 * o

        h = rmsnorm(x, g_mlp[layer]) * (1.0 + scale2) + shift2
        up = h @ w_up[layer]
        u, g = up[..., :D_FF], up[..., D_FF:]
        g = causal_depthwise_conv(g, conv_w[layer], conv_b[layer])
        x = x + gate2 * ((jax.nn.silu(g) * u) @ w_down[layer])
    return rmsnorm(x, g_final)


DEPTH_2 = 1

CHUNK = 64
N_MEM = 256
D_MIX = D_MODEL
D_RNN = D_MIX // 2
D_ATT = D_MIX - D_RNN
N_RNN_BLOCKS = 8
RNN_BLOCK = D_RNN // N_RNN_BLOCKS
CONV_WIDTH_2 = 4
RG_LRU_C = 8.0
N_ATT_HEADS = 8
ATT_HEAD_DIM = D_ATT // N_ATT_HEADS
LEFT_CHUNKS = 8
BAND = (LEFT_CHUNKS + 1) * CHUNK
REL_CLIP = 128
N_XHEADS = 4
XHEAD_DIM = D_MODEL // N_XHEADS
N_GROUPS = 4
EXPERTS_PER_GROUP = 8
N_EXPERTS = N_GROUPS * EXPERTS_PER_GROUP
TOP_K = 2
D_EXPERT = D_MODEL // 2
MOE_BLOCK = 128
D_IN_PROJ = 2 * D_RNN + 3 * D_ATT
EPS = 1e-6
NEG_INF = -1e30


def rms_norm(x, w):
    xf = x.astype(jnp.float32)
    y = xf * lax.rsqrt(jnp.mean(xf * xf, axis=-1, keepdims=True) + EPS)
    return (y * w.astype(jnp.float32)).astype(x.dtype)

def _linear_recurrence_combine(left, right):
    a1, b1 = left
    a2, b2 = right
    return a1 * a2, a2 * b1 + b2

def recurrent_group(xr, xg, conv_w, conv_b, w_a, b_a, w_x, b_x, lam):
    b, s, _ = xr.shape
    xc = lax.conv_general_dilated(
        xr, conv_w[:, None, :].astype(xr.dtype), window_strides=(1,),
        padding=[(CONV_WIDTH_2 - 1, 0)], dimension_numbers=('NWC', 'WIO', 'NWC'),
        feature_group_count=D_RNN) + conv_b
    xb = xc.reshape(b, s, N_RNN_BLOCKS, RNN_BLOCK)
    r = jax.nn.sigmoid((jnp.einsum('bsnc,ncd->bsnd', xb, w_a).reshape(b, s, D_RNN) + b_a).astype(jnp.float32))
    i = jax.nn.sigmoid((jnp.einsum('bsnc,ncd->bsnd', xb, w_x).reshape(b, s, D_RNN) + b_x).astype(jnp.float32))
    log_a = -RG_LRU_C * r * jax.nn.softplus(-lam.astype(jnp.float32))
    a = jnp.exp(log_a)
    u = jnp.sqrt(-jnp.expm1(2.0 * log_a)) * (i * xc.astype(jnp.float32))
    _, h = lax.associative_scan(_linear_recurrence_combine, (a, u), axis=1)
    return (jax.nn.gelu(xg.astype(jnp.float32)) * h).astype(xr.dtype)

def rel_bias_band(rel_bias):
    qi = np.arange(CHUNK)[:, None]
    kj = np.arange(BAND)[None, :]
    dist = LEFT_CHUNKS * CHUNK + qi - kj
    idx = np.clip(dist, -REL_CLIP, REL_CLIP) + REL_CLIP
    return rel_bias[:, idx]

def chunk_band_attention(q, k, v, rel_bias):
    b, s, _ = q.shape
    nc = s // CHUNK
    qc = q.reshape(b, nc, CHUNK, N_ATT_HEADS, ATT_HEAD_DIM)
    kc = k.reshape(b, nc, CHUNK, N_ATT_HEADS, ATT_HEAD_DIM)
    vc = v.reshape(b, nc, CHUNK, N_ATT_HEADS, ATT_HEAD_DIM)
    pad = ((0, 0), (LEFT_CHUNKS, 0), (0, 0), (0, 0), (0, 0))
    kp = jnp.pad(kc, pad)
    vp = jnp.pad(vc, pad)
    kb = jnp.concatenate([kp[:, j:j + nc] for j in range(LEFT_CHUNKS + 1)], axis=2)
    vb = jnp.concatenate([vp[:, j:j + nc] for j in range(LEFT_CHUNKS + 1)], axis=2)
    chunk_id = np.arange(nc)[:, None] - LEFT_CHUNKS + np.arange(LEFT_CHUNKS + 1)[None, :]
    valid = np.repeat(chunk_id >= 0, CHUNK, axis=1)
    scores = jnp.einsum('bnqhd,bnkhd->bhnqk', qc, kb, preferred_element_type=jnp.float32)
    scores = scores * (ATT_HEAD_DIM ** -0.5) + rel_bias_band(rel_bias).astype(jnp.float32)[None, :, None]
    scores = jnp.where(valid[None, None, :, None, :], scores, NEG_INF)
    probs = jax.nn.softmax(scores, axis=-1).astype(v.dtype)
    out = jnp.einsum('bhnqk,bnkhd->bnqhd', probs, vb)
    return out.reshape(b, s, D_ATT)

def memory_cross_attention(h, mem_n, wq, wk, wv, wo):
    b, s, _ = h.shape
    m = mem_n.shape[1]
    q = (h @ wq).reshape(b, s, N_XHEADS, XHEAD_DIM)
    k = (mem_n @ wk).reshape(b, m, N_XHEADS, XHEAD_DIM)
    v = (mem_n @ wv).reshape(b, m, N_XHEADS, XHEAD_DIM)
    scores = jnp.einsum('bshd,bmhd->bhsm', q, k, preferred_element_type=jnp.float32) * (XHEAD_DIM ** -0.5)
    probs = jax.nn.softmax(scores, axis=-1).astype(v.dtype)
    out = jnp.einsum('bhsm,bmhd->bshd', probs, v).reshape(b, s, D_MODEL)
    return out @ wo

def routed_experts(ht, expert_idx, combine_w, w_gate, w_up, w_down):
    t, d = ht.shape
    n_slots = t * TOP_K
    flat_e = expert_idx.reshape(-1)
    flat_tok = jnp.repeat(jnp.arange(t, dtype=jnp.int32), TOP_K)
    order = jnp.argsort(flat_e)
    e_sorted = flat_e[order]
    tok_sorted = flat_tok[order]
    w_sorted = combine_w.reshape(-1)[order]
    counts = jnp.bincount(flat_e, length=N_EXPERTS)
    padded = (counts + MOE_BLOCK - 1) // MOE_BLOCK * MOE_BLOCK
    pad_end = jnp.cumsum(padded)
    pad_start = pad_end - padded
    start = jnp.cumsum(counts) - counts
    dest = pad_start[e_sorted] + (jnp.arange(n_slots) - start[e_sorted])
    n_blocks = (n_slots + MOE_BLOCK - 1) // MOE_BLOCK + N_EXPERTS
    n_rows = n_blocks * MOE_BLOCK
    src_tok = jnp.full((n_rows,), t, dtype=jnp.int32).at[dest].set(tok_sorted)
    x_pad = jnp.concatenate([ht, jnp.zeros((1, d), ht.dtype)], axis=0)
    xs = x_pad[src_tok].reshape(n_blocks, MOE_BLOCK, d)
    block_expert = jnp.minimum(
        jnp.searchsorted(pad_end, jnp.arange(n_blocks) * MOE_BLOCK, side='right'), N_EXPERTS - 1)

    def expert_block(args):
        xb, e = args
        g = xb @ w_gate[e]
        u = xb @ w_up[e]
        return (jax.nn.silu(g) * u) @ w_down[e]

    ys = lax.map(expert_block, (xs, block_expert)).reshape(n_rows, d)
    contrib = (ys[dest].astype(jnp.float32) * w_sorted[:, None]).astype(ht.dtype)
    return jnp.zeros((t, d), ht.dtype).at[tok_sorted].add(contrib)

def hierarchical_moe(h, w_group, b_group, w_router, b_router, w_gate, w_up, w_down):
    b, s, d = h.shape
    t = b * s
    ht = h.reshape(t, d)
    g_logits = (ht @ w_group).astype(jnp.float32) + b_group.astype(jnp.float32)
    g_probs = jax.nn.softmax(g_logits, axis=-1)
    g_p, g_idx = lax.top_k(g_probs, 1)
    e_all = jnp.einsum('td,gde->tge', ht, w_router).astype(jnp.float32) + b_router.astype(jnp.float32)
    sel = jnp.broadcast_to(g_idx[:, :, None], (t, 1, EXPERTS_PER_GROUP))
    e_logits = jnp.take_along_axis(e_all, sel, axis=1)[:, 0]
    e_probs = jax.nn.softmax(e_logits, axis=-1)
    e_p, e_idx = lax.top_k(e_probs, TOP_K)
    e_p = e_p / jnp.sum(e_p, axis=-1, keepdims=True)
    combine_w = g_p * e_p
    expert_idx = g_idx * EXPERTS_PER_GROUP + e_idx
    y = routed_experts(ht, expert_idx, combine_w, w_gate, w_up, w_down)
    return y.reshape(b, s, d)

def second_inputs(seed: int = 0) -> dict:
    key = jax.random.key(seed)
    ks = jax.random.split(key, 32)
    f32 = jnp.float32

    def nrm(k, shape, scale):
        return jax.random.normal(k, shape, f32) * scale

    def gain(k, shape):
        return 1.0 + 0.02 * jax.random.normal(k, shape, f32)

    a0 = jax.random.uniform(ks[10], (DEPTH_2, D_RNN), f32, 0.9, 0.999)
    lam = jnp.log(a0) - jnp.log1p(-a0)
    return {
        'x': nrm(ks[0], (BATCH, SEQ, D_MODEL), 1.0),
        'mem': nrm(ks[1], (BATCH, N_MEM, D_MODEL), 1.0),
        'ln1_w': gain(ks[2], (DEPTH_2, D_MODEL)),
        'w_in': nrm(ks[3], (DEPTH_2, D_MODEL, D_IN_PROJ), D_MODEL ** -0.5),
        'conv_w': nrm(ks[4], (DEPTH_2, CONV_WIDTH_2, D_RNN), CONV_WIDTH_2 ** -0.5),
        'conv_b': nrm(ks[5], (DEPTH_2, D_RNN), 0.02),
        'rnn_wa': nrm(ks[6], (DEPTH_2, N_RNN_BLOCKS, RNN_BLOCK, RNN_BLOCK), RNN_BLOCK ** -0.5),
        'rnn_ba': nrm(ks[7], (DEPTH_2, D_RNN), 0.02),
        'rnn_wx': nrm(ks[8], (DEPTH_2, N_RNN_BLOCKS, RNN_BLOCK, RNN_BLOCK), RNN_BLOCK ** -0.5),
        'rnn_bx': nrm(ks[9], (DEPTH_2, D_RNN), 0.02),
        'rnn_lambda': lam,
        'rel_bias': nrm(ks[11], (DEPTH_2, N_ATT_HEADS, 2 * REL_CLIP + 1), 0.2),
        'gn_rnn_w': gain(ks[12], (DEPTH_2, D_RNN)),
        'gn_att_w': gain(ks[13], (DEPTH_2, D_ATT)),
        'w_out': nrm(ks[14], (DEPTH_2, D_MIX, D_MODEL), D_MIX ** -0.5),
        'ln2_w': gain(ks[15], (DEPTH_2, D_MODEL)),
        'mem_norm_w': gain(ks[16], (D_MODEL,)),
        'xq_w': nrm(ks[17], (DEPTH_2, D_MODEL, D_MODEL), D_MODEL ** -0.5),
        'xk_w': nrm(ks[18], (DEPTH_2, D_MODEL, D_MODEL), D_MODEL ** -0.5),
        'xv_w': nrm(ks[19], (DEPTH_2, D_MODEL, D_MODEL), D_MODEL ** -0.5),
        'xo_w': nrm(ks[20], (DEPTH_2, D_MODEL, D_MODEL), D_MODEL ** -0.5),
        'ln3_w': gain(ks[21], (DEPTH_2, D_MODEL)),
        'router_group_w': nrm(ks[22], (DEPTH_2, D_MODEL, N_GROUPS), D_MODEL ** -0.5),
        'router_group_b': nrm(ks[23], (DEPTH_2, N_GROUPS), 0.01),
        'router_expert_w': nrm(ks[24], (DEPTH_2, N_GROUPS, D_MODEL, EXPERTS_PER_GROUP), D_MODEL ** -0.5),
        'router_expert_b': nrm(ks[25], (DEPTH_2, N_GROUPS, EXPERTS_PER_GROUP), 0.01),
        'expert_gate_w': nrm(ks[26], (DEPTH_2, N_EXPERTS, D_MODEL, D_EXPERT), D_MODEL ** -0.5),
        'expert_up_w': nrm(ks[27], (DEPTH_2, N_EXPERTS, D_MODEL, D_EXPERT), D_MODEL ** -0.5),
        'expert_down_w': nrm(ks[28], (DEPTH_2, N_EXPERTS, D_EXPERT, D_MODEL), D_EXPERT ** -0.5),
        'final_norm_w': gain(ks[29], (D_MODEL,)),
    }

def second_block(x, mem, ln1_w, w_in, conv_w, conv_b, rnn_wa, rnn_ba, rnn_wx, rnn_bx, rnn_lambda,
              rel_bias, gn_rnn_w, gn_att_w, w_out, ln2_w, mem_norm_w, xq_w, xk_w, xv_w, xo_w,
              ln3_w, router_group_w, router_group_b, router_expert_w, router_expert_b,
              expert_gate_w, expert_up_w, expert_down_w, final_norm_w):
    mem_n = rms_norm(mem, mem_norm_w)
    for l in range(DEPTH_2):
        h = rms_norm(x, ln1_w[l])
        proj = h @ w_in[l]
        xr = proj[..., :D_RNN]
        xg = proj[..., D_RNN:2 * D_RNN]
        q = proj[..., 2 * D_RNN:2 * D_RNN + D_ATT]
        k = proj[..., 2 * D_RNN + D_ATT:2 * D_RNN + 2 * D_ATT]
        v = proj[..., 2 * D_RNN + 2 * D_ATT:]
        y_rnn = recurrent_group(xr, xg, conv_w[l], conv_b[l], rnn_wa[l], rnn_ba[l],
                                rnn_wx[l], rnn_bx[l], rnn_lambda[l])
        y_att = chunk_band_attention(q, k, v, rel_bias[l])
        mixed = jnp.concatenate([rms_norm(y_rnn, gn_rnn_w[l]), rms_norm(y_att, gn_att_w[l])], axis=-1)
        x = x + mixed @ w_out[l]
        h = rms_norm(x, ln2_w[l])
        x = x + memory_cross_attention(h, mem_n, xq_w[l], xk_w[l], xv_w[l], xo_w[l])
        h = rms_norm(x, ln3_w[l])
        x = x + hierarchical_moe(h, router_group_w[l], router_group_b[l], router_expert_w[l],
                                 router_expert_b[l], expert_gate_w[l], expert_up_w[l], expert_down_w[l])
    return rms_norm(x, final_norm_w)


def setup_inputs(seed=0):
    out = dict(first_inputs(seed))
    for name, value in second_inputs(seed + 1).items():
        if name != "x":
            out[name + "_2"] = value
    return out


def reference(
    x, c, w_mod, b_mod, g_attn, w_in, diff_lambda, subln_g, forget_bias, w_out, g_mlp, w_up,
    conv_w, conv_b, w_down, g_final, mem_2, ln1_w_2, w_in_2, conv_w_2, conv_b_2, rnn_wa_2,
    rnn_ba_2, rnn_wx_2, rnn_bx_2, rnn_lambda_2, rel_bias_2, gn_rnn_w_2, gn_att_w_2, w_out_2,
    ln2_w_2, mem_norm_w_2, xq_w_2, xk_w_2, xv_w_2, xo_w_2, ln3_w_2, router_group_w_2,
    router_group_b_2, router_expert_w_2, router_expert_b_2, expert_gate_w_2, expert_up_w_2,
    expert_down_w_2, final_norm_w_2,
):
    x = first_block(
        x, c, w_mod, b_mod, g_attn, w_in, diff_lambda, subln_g, forget_bias, w_out, g_mlp, w_up,
        conv_w, conv_b, w_down, g_final,
    )
    return second_block(
        x, mem_2, ln1_w_2, w_in_2, conv_w_2, conv_b_2, rnn_wa_2, rnn_ba_2, rnn_wx_2, rnn_bx_2,
        rnn_lambda_2, rel_bias_2, gn_rnn_w_2, gn_att_w_2, w_out_2, ln2_w_2, mem_norm_w_2,
        xq_w_2, xk_w_2, xv_w_2, xo_w_2, ln3_w_2, router_group_w_2, router_group_b_2,
        router_expert_w_2, router_expert_b_2, expert_gate_w_2, expert_up_w_2, expert_down_w_2,
        final_norm_w_2,
    )


_drawn_inputs = setup_inputs


def setup_inputs(seed=0):
    import zlib

    import numpy as np

    out = dict(_drawn_inputs(seed))
    spreads = {}
    factors = {'g_attn': 3.802,
     'subln_g': 3.404,
     'g_mlp': 3.593,
     'conv_b': 3.867,
     'rnn_ba_2': 8.0,
     'rnn_bx_2': 4.858,
     'gn_att_w_2': 3.18,
     'ln2_w_2': 8.0,
     'mem_norm_w_2': 8.0,
     'router_group_b_2': 64.0,
     'router_expert_b_2': 38.352,
     'final_norm_w_2': 7.772,
     'ln3_w_2': 8.0}
    for name, (base, spread) in spreads.items():
        noise = np.random.default_rng([zlib.crc32(name.encode()), seed]).standard_normal(out[name].shape)
        drawn = base * np.exp(spread * noise) if base else spread * noise
        out[name] = jnp.asarray(drawn.astype(out[name].dtype))
    for name, factor in factors.items():
        out[name] = (out[name] * factor).astype(out[name].dtype)
    return out
```

```python
import math
from contextlib import ExitStack

import numpy as np

import concourse.bass as bass
from concourse import mybir

P = 128
T = 512
NT = T // P
D = 1024
KD = D // P
DEPTH = 2
HD = 64
A_HEADS, B_HEADS, C_HEADS = 4, 6, 6
HEADS = A_HEADS + B_HEADS + C_HEADS
PAIRS = HEADS // 2
D_FF = 2816
FT = D_FF // P
FH = FT // 2
IN_COLS = 3 * D + C_HEADS
QUARTER = 256
RING = 5
NEG = -1.0e30
NORM_EPS, SUBLN_EPS, EPS2 = 1e-6, 1e-5, 1e-6
D_RNN = 512
CT = D_RNN // P
W_CONV2 = 4
HEADS2 = 8
XHEADS, XDIM = 4, 256
NMEM = 256
GROUPS, PER_GROUP = 4, 8
EXPERTS = GROUPS * PER_GROUP
D_EXP = 512
NR = GROUPS + EXPERTS
BLK = 128
BLOCKS = 40
ROWS = BLOCKS * BLK

IN_SLOTS, OUT_SLOTS, UP_SLOTS, DOWN_SLOTS = 12, 4, FH, (FH + 1) // 2
SLOTS = IN_SLOTS + OUT_SLOTS + 2 * (UP_SLOTS + DOWN_SLOTS)
assert SLOTS == 50 and SLOTS % RING == 0
HALVES = [2] * (IN_SLOTS + OUT_SLOTS) + ([2] * (UP_SLOTS + DOWN_SLOTS - 1) + [0]) * 2
CUM = [sum(HALVES[:i]) for i in range(SLOTS + 1)]
TILES = CUM[SLOTS]
IN2, OUT2 = 10, 4
SLOTS2 = IN2 + OUT2 + 16
MOD_CHUNKS = 6 * D // QUARTER
MOD_FIRST = 2 * D // QUARTER
MOD_PAIRS = (MOD_CHUNKS - MOD_FIRST) // 2
NEXT_PAIRS = MOD_FIRST // 2

QK_OF = {**{a: a for a in range(4)}, **{a: a - 2 for a in range(6, 12)}, **{a: a - 5 for a in range(15, 21)}}
V_OF = {4: 0, 5: 1, 12: 2, 13: 3, 14: 4, 21: 5, 22: 6, 23: 7}
ROPE = [0, 1, 2, 3, 6, 7, 8, 9, 10, 11]
QT = {"A": 0, "B": 4, "C": 10}
KT = {"A": 2, "B": 7, "C": 13}

C_GA, C_GM, C_CW, C_CB, C_SUB, C_LAM, C_MOD = 0, KD, 2 * KD, 2 * KD + 3 * FT, 2 * KD + 4 * FT, 105, 128
NPRM = 2 * KD + 4 * FT + 1
NCOL = C_MOD + 6 * KD
SH1, SC1, GT1, SH2, SC2, GT2 = (C_MOD + KD * i for i in range(6))
E_LN1, E_CW, E_CB, E_BA, E_BX, E_LAM, E_GR, E_GA, E_LN2, E_MEM, E_LN3, E_FIN = 0, 8, 24, 28, 32, 36, 40, 44, 48, 56, 64, 72
NPRM2 = 80

K_CA, K_SA, K_CB, K_SB, K_MA, K_MB = (i * T for i in range(6))
K_ID, K_ON, K_OD, K_OR, K_BO, K_RA, K_RB, K_TRI = (6 * T + P * i for i in range(8))
K_SEL = K_TRI + P
K_TOK = K_SEL + C_HEADS * P
K_EI = K_TOK + NT
K_BB = K_EI + EXPERTS
NK = K_BB + BLOCKS

ATANH = [1 / 15, 1 / 13, 1 / 11, 1 / 9, 1 / 7, 1 / 5, 1 / 3]
N_LOGSIG = 14

ALU = mybir.AluOpType
ACT = mybir.ActivationFunctionType
AX = mybir.AxisListType
F32 = mybir.dt.float32
I32 = mybir.dt.int32


def jobs_of_layer():
    out = []
    for kind, n, first in (("A", A_HEADS, 0), ("B", B_HEADS, A_HEADS), ("C", C_HEADS, A_HEADS + B_HEADS)):
        out += [(kind, h, first + h, qb) for h in range(n) for qb in range(NT)]
    return out


JOBS = jobs_of_layer()
MAPS = [2 if j[0] == "A" else 1 for j in JOBS]
UNIT0 = [sum(MAPS[:i]) for i in range(len(JOBS) + 1)]
UNITS = UNIT0[-1]
JOBS2 = [("D", h, h, qb) for h in range(HEADS2) for qb in range(NT)]
UNIT02 = list(range(len(JOBS2) + 1))
NS = 4
CH_NORM, CH_ROPE, CH_MLP = 1, 2, 2
CH_ATT = UNITS + sum(1 if m == 1 else 4 for m in MAPS)
CH_LAYER = 4 + 2 * CH_NORM + CH_ROPE * len(ROPE) + N_LOGSIG + CH_ATT + 2 + CH_MLP * FT


def build(nc, a):
    with ExitStack() as ctx:
        def sb(name, shape, dt=F32):
            return ctx.enter_context(nc.sbuf_tensor(name, shape, dt))

        def sem(name):
            return ctx.enter_context(nc.semaphore(name))

        xT = sb("xT", [P, KD, T])
        hT = sb("hT", [P, KD, T])
        arena = sb("arena", [P, 26624])
        wring = arena[:, 0:10240].rearrange("p (r k n) -> p r k n", r=RING, k=KD)
        wdown = arena[:, 0:10240].rearrange("p (r k n) -> p r k n", r=RING, k=2)
        big = arena[:, 10240:22528]
        qk = big[:, 0:16 * T].rearrange("p (i t) -> p i t", i=16)
        v = big[:, 16 * T:24 * T].rearrange("p (t c) -> p t c", t=NT)
        gated = big[:, 0:FH * T].rearrange("p (i t) -> p i t", i=FH)
        PT = arena[:, 22528:26624].rearrange("p (b k t) -> p b k t", b=2, k=NT)
        mod_w = arena[:, 22528:26624].rearrange("p (b k n) -> p b k n", b=2, k=KD)
        kc = sb("kc", [P, NK])
        ident, ones, onesD = kc[:, K_ID:K_ID + P], kc[:, K_ON:K_ON + P], kc[:, K_OD:K_OD + P]
        onesR, blk64 = kc[:, K_OR:K_OR + P], kc[:, K_BO:K_BO + P]
        S = sb("S", [P, NS, T])
        toep = sb("toep", [P, 2, T])
        modacc = toep[:, :, :].rearrange("p a (b c) -> p (a b) c", c=QUARTER)
        tmp = sb("tmp", [P, 6 * T])
        sq = tmp[:, 0:2 * T].rearrange("p (b t) -> p b t", b=2)
        hn = tmp[:, 2 * T:4 * T].rearrange("p (b t) -> p b t", b=2)
        raw, t1 = sq, hn
        rot = tmp[:, 4 * T:6 * T].rearrange("p (b t) -> p b t", b=2)
        gpad = sb("gpad", [P, 2, T + 4])
        y = sq
        sg = hn
        std = sb("std", [P, T])
        rs = sb("rs", [P, T])
        pcall = sb("pcall", [P, DEPTH, NCOL])
        pc = sb("pc", [P, NCOL])
        pc2 = sb("pc2", [P, NPRM2 + 16])
        wfz = sb("wfz", [P, KD, C_HEADS])
        fb = sb("fb", [C_HEADS, DEPTH])
        z6 = S[0:C_HEADS, :, :]
        F6 = sb("F6", [C_HEADS, T])
        one6 = sb("one6", [P, T])
        lamp = sb("lamp", [P, DEPTH, 4, 32])
        small = sb("small", [P, 64])
        mx = sb("mx", [P, 3, 8])
        epsc = sb("epsc", [P, 3])
        wgate = sb("wgate", [P, 2, CT, P])
        wrt = sb("wrt", [P, KD, NR])
        rb = sb("rb", [P, NR])
        rt = sb("rt", [P, 6, NT, EXPERTS])
        rlog = sb("rlog", [P, NT, NR])
        rg4 = sb("rg4", [P, 3, NT, GROUPS])
        rsm = sb("rsm", [P, 12, NT])
        e32 = sb("e32", [P, 6, EXPERTS])
        i32 = sb("i32", [P, 2, EXPERTS], I32)
        dest = sb("dest", [P, 2, NT], I32)
        tokid = sb("tokid", [P, NT], I32)
        src_i = sb("src_i", [BLOCKS, BLK], I32)
        src_f = sb("src_f", [BLOCKS, BLK])
        src_c = sb("src_c", [P, BLOCKS], I32)
        blkE = sb("blkE", [P, BLOCKS], I32)
        blkU = sb("blkU", [P, BLOCKS], I32)
        zero = sb("zero", [P, BLOCKS], I32)
        bank = [ctx.enter_context(nc.psum_tensor(f"bank{i}", [P, 512], F32)) for i in range(8)]
        mem_tok = S[:, :, :].rearrange("p (m a) t -> p m (a t)", m=2)
        memT = kc[:, 0:KD * NMEM].rearrange("p (k m) -> p k m", k=KD)
        xr = arena[:, 22528:22528 + CT * (T + 4)].rearrange("p (c t) -> p c t", c=CT)
        xc = qk[:, 0:CT, :]
        r_gate, i_gate, a_rec, u_tmp = hn[:, 0, :], hn[:, 1, :], rot[:, 0, :], rot[:, 1, :]
        h_rec, g_rec = gpad[:, 0, 0:T], gpad[:, 1, 0:T]
        xq = qk[:, 0:8, :]
        xk = big[:, 8 * T:12 * T].rearrange("p (k m) -> p k m", k=KD)
        xv = big[:, 12 * T:16 * T].rearrange("p (m c) -> p m c", m=2)
        ering = arena[:, 0:24576].rearrange("p (r c) -> p r c", r=6)
        xs = xT[:, 0:4, :].rearrange("p (b k) t -> p b (k t)", b=2)
        xsT = xT[:, 4:8, :].rearrange("p (b k) (j c) -> p b (k j) c", b=2, c=P)
        ysb = tmp[:, 0:4 * T].rearrange("p (b c) -> p b c", b=2)
        eg, ea, eaT = S[:, 0, :], S[:, 1, :], S[:, 2, :].rearrange("p (k c) -> p k c", k=4)
        y_got_t = ering[:, 0:2, :].rearrange("p r (i c) -> p (r i) c", c=D)
        fw = kc[:, 0:D]
        xtok = hT[:, :, :].rearrange("p (t a) c -> p t (a c)", t=NT)

        names = """consts_in x_in rows_in lam_in w6_in fb_in mod_in0 mod_in1 mod_in2 mod_in3 mod_in4
            w_in0 w_in1 w_in2 w_in3 w_in4 rows_turned cols_copied silu_c lam_exp lam2_abs lam2_exp mod_used
            mod_step next_added mod_next0 mod_next1 mod_turned x_turned x_updated table_ready setup_ready sq_ready sq_used std_ready hn_ready h_ready
            tiles_done down_done acc_copied rot_done rope_done fz_done z_abs z_exp decay_ready chain s_done
            max_ready exp_done p_ready t_done pt_ready pv_done o_copied sub_sq sub_sum sub_std sub_done
            gpad_ready conv_done silu_done act_ready toep_in0 toep_in1 mem_in mem_sq mem_std mem_scaled
            mem_turned mem_ready conv2_ready gate_in gate_done gates_ready rec_act rec_u rec_ready router_in
            h_tok_turned h_tok_ready h_tok_out x_tok_turned x_tok_ready logits_done group_shifted second_shifted
            sel_exp sel_ready count_done dest_ready src_zeroed src_scattered src_in src_float src_turned
            plan_ready xe_in0 xe_in1 xe_turned xeT_ready w_e0 w_e1 w_e2 w_e3 w_e4 w_e5 gate_e_done
            up_e_done silu_e act_e actT_turned actT_ready e_down_done y_ready y_out0 y_out1 y_got0 y_got1 y_got2
            y_got3 y_used fin_sq fin_std fw_in out_ready out_sent"""
        s = {n: sem(n) for n in names.split()}

        h_dram, ys_dram, src_dram = a["h_scratch"], a["y_scratch"], a["src_scratch"]

        def w_wait(eng, l, i):
            per = SLOTS // RING
            eng.wait_ge(s[f"w_in{i % RING}"], l * (32 * per) + 32 * (i // RING + 1))

        def next_layer(l):
            return nc.s_assert_within(l + 1, 1, DEPTH - 1, skip_runtime_bounds_check_because="the branch is taken for l < DEPTH - 1 only")

        def tiles(l, n):
            return l * TILES + TILES + n

        block = ctx.enter_context(nc.Block())

        @block.sync
        def _(sp):
            sp.dma_start(kc[:, :], a["consts"]).then_inc(s["consts_in"], 16)
            sp.dma_start(S[0:104, 0, 0:P], a["rows_mod"]).then_inc(s["rows_in"], 16)
            for l in range(DEPTH):
                sp.dma_start(S[0:NPRM, 1 + l, 0:P], a["rows_layer"][l]).then_inc(s["rows_in"], 16)
            sp.dma_start(S[0:NPRM2, 3, 0:P], a["rows_second"]).then_inc(s["rows_in"], 16)
            sp.dma_start(xtok, a["x"].rearrange("b (t p) d -> p (b t) d", p=P)).then_inc(s["x_in"], 16)
            sp.dma_start(lamp[:, :, :, :], bass.AP(a["diff_lambda"].tensor, 0, [[0, P], [P, DEPTH], [32, 4], [1, 32]])).then_inc(s["lam_in"], 16)
            sp.dma_start(fb[:, :], a["forget_bias_t"]).then_inc(s["fb_in"], 16)

            for c in range(MOD_FIRST):
                if c >= RING:
                    sp.wait_ge(s["mod_used"], c - RING + 1)
                sp.dma_start(wring[:, c % RING, :, :], a["w_mod"][0].rearrange("(k p) n -> p k n", p=P)[:, :, c * QUARTER:(c + 1) * QUARTER]).then_inc(s[f"mod_in{c % RING}"], 16)
            sp.wait_ge(s["mod_used"], MOD_FIRST)

            def load_mod(l, of, q, n):
                if q >= 2:
                    sp.wait_ge(s["mod_used"], l * MOD_CHUNKS + (MOD_FIRST + q - 1))
                w = a["w_mod"][bass.ds(of, 1)].rearrange("o (k p) n -> p (o k) n", p=P)
                sp.dma_start(mod_w[:, q % 2, :, :], w[:, :, n * QUARTER:(n + 1) * QUARTER]).then_inc(s[f"mod_next{q % 2}"], 16)

            def slot_free(l, i):
                if i >= RING:
                    j, at = i - RING, l
                    base = lambda per, c: l * per + per + c
                else:
                    j = i - RING + SLOTS
                    base = lambda per, c: l * per + c
                if HALVES[j]:
                    sp.wait_ge(s["tiles_done"], base(TILES, CUM[j + 1]))
                else:
                    sp.wait_ge(s["down_done"], base(2 * KD, KD if j < SLOTS - 1 else 2 * KD))

            def load(i, dst, src):
                n, w = dst.shape[1:]
                for h in range(2):
                    at = (slice(0, P), slice(h * n // 2, (h + 1) * n // 2)) if n > 1 else (slice(0, P), slice(0, 1), slice(h * w // 2, (h + 1) * w // 2))
                    sp.dma_start(dst[at], src[at]).then_inc(s[f"w_in{i % RING}"], 16)

            def load_up(i, w_up, f):
                for h in range(2):
                    c = h * D_FF + f * P
                    sp.dma_start(wring[:, i % RING, :, h * P:(h + 1) * P], w_up[:, :, c:c + P]).then_inc(s[f"w_in{i % RING}"], 16)

            with sp.Fori(0, DEPTH) as l:
                w_in = a["w_in"][bass.ds(l, 1)].rearrange("o (k p) n -> p (o k) n", p=P)
                w_out = a["w_out"][bass.ds(l, 1)].rearrange("o (k p) n -> p (o k) n", p=P)
                w_up = a["w_up"][bass.ds(l, 1)].rearrange("o (k p) n -> p (o k) n", p=P)
                w_down = a["w_down"][bass.ds(l, 1)].rearrange("o (f p) n -> p (o f) n", p=P)
                i = 0
                for c in range(IN_SLOTS):
                    slot_free(l, i)
                    load(i, wring[:, i % RING, :, :], w_in[:, :, c * QUARTER:(c + 1) * QUARTER])
                    if c == 0 or c >= 9:
                        pair = max(0, c - 8)
                        for q in (2 * pair, 2 * pair + 1):
                            load_mod(l, l, q, MOD_FIRST + q)
                    i += 1
                sp.wait_ge(s["fz_done"], l + 1)
                sp.dma_start(wfz[:, :, :], w_in[:, :, 3 * D:IN_COLS]).then_inc(s["w6_in"], 16)
                for c in range(OUT_SLOTS):
                    slot_free(l, i)
                    load(i, wring[:, i % RING, :, :], w_out[:, :, c * QUARTER:(c + 1) * QUARTER])
                    for q in (2 * (c + 4), 2 * (c + 4) + 1):
                        load_mod(l, l, q, MOD_FIRST + q)
                    i += 1
                for hh in range(2):
                    for f in range(hh * FH, hh * FH + FH):
                        slot_free(l, i)
                        load_up(i, w_up, f)
                        if f == 1 or 7 <= f < 6 + NEXT_PAIRS:
                            pair = max(0, f - 6)
                            with sp.If(l < DEPTH - 1):
                                for q in (2 * pair, 2 * pair + 1):
                                    load_mod(l, next_layer(l), 2 * MOD_PAIRS + q, q)
                        i += 1
                    for c in range(DOWN_SLOTS):
                        n = min(2, FH - 2 * c)
                        slot_free(l, i)
                        load(i, wdown[:, i % RING, 0:n, :], w_down[:, hh * FH + 2 * c:hh * FH + 2 * c + n, :])
                        i += 1

            sp.wait_ge(s["tiles_done"], tiles(DEPTH - 1, CUM[IN_SLOTS] + 1))
            sp.dma_start(mem_tok, a["mem_2"].rearrange("b (m p) d -> p (b m) d", p=P)).then_inc(s["mem_in"], 16)
            i = 0
            for name, n in (("w_in_2", IN2), ("w_out_2", OUT2), ("xk_w_2", 4), ("xv_w_2", 4), ("xq_w_2", 4), ("xo_w_2", 4)):
                w = a[name][0].rearrange("(k p) n -> p k n", p=P)
                for c in range(n):
                    if i < RING:
                        slot_free(DEPTH, i)
                    else:
                        sp.wait_ge(s["tiles_done"], tiles(DEPTH, 2 * (i - RING) + 2))
                    load(i, wring[:, i % RING, :, :], w[:, :, c * QUARTER:(c + 1) * QUARTER])
                    i += 1

            for t in range(NT):
                sp.wait_ge(s["h_tok_ready"], 2 * t + 2)
                sp.dma_start(h_dram[t * P:(t + 1) * P, :], big[:, t * D:(t + 1) * D]).then_inc(s["h_tok_out"], 16)
            sp.wait_ge(s["src_scattered"], 16 * 2 * NT)
            sp.dma_start(src_i[:, :], src_dram.rearrange("(b p) o -> b (p o)", p=BLK)).then_inc(s["src_in"], 16)
            sp.wait_ge(s["h_tok_out"], 16 * NT)
            sp.wait_ge(s["plan_ready"], 1)
            sp.dma_start(fw, bass.AP(a["final_norm_w_2"].tensor, 0, [[0, P], [1, D]])).then_inc(s["fw_in"], 16)
            ew = [a["expert_gate_w_2"][0], a["expert_up_w_2"][0], a["expert_down_w_2"][0]]

            def load_expert(b, par, again):
                e = sp.value_load(blkE[0:1, bass.ds(b, 1)], min_val=0, max_val=EXPERTS - 1)
                has_rows = sp.value_load(blkU[0:1, bass.ds(b, 1)], min_val=0, max_val=1)
                with sp.If(has_rows > 0):
                    for m, used in enumerate(("gate_e_done", "up_e_done", "e_down_done")):
                        if again:
                            sp.wait_ge(s[used], (b - 1) if m < 2 else (b - 1) * 2)
                        w = ew[m][bass.ds(e, 1)].rearrange("e (k p) n -> p (e k) n", p=P)
                        dst = ering[:, 3 * par + m, :].rearrange("p (k n) -> p k n", k=w.shape[1])
                        sp.dma_start(dst, w).then_inc(s[f"w_e{3 * par + m}"], 16)

            load_expert(0, 0, False)
            load_expert(1, 1, False)
            with sp.Fori(1, BLOCKS // 2) as g:
                for par in range(2):
                    load_expert(g * 2 + par, par, True)
            for t in range(NT):
                sp.wait_ge(s["out_ready"], t + 1)
                sp.dma_start(a["out"].rearrange("b (t p) d -> p (b t) d", p=P)[:, t, :], xtok[:, t, :]).then_inc(s["out_sent"], 16)
            sp.wait_ge(s["out_sent"], 16 * NT)

        @block.tensor
        def _(pe):
            mm = nc.tensor.matmul

            pe.sem_inc(s["tiles_done"], TILES)
            pe.sem_inc(s["down_done"], 2 * KD)
            pe.sem_inc(s["fz_done"], 1)
            pe.wait_ge(s["consts_in"], 16)
            pe.wait_ge(s["rows_in"], 16 * 4)
            for i, n in enumerate((104, NPRM, NPRM, NPRM2)):
                nc.tensor.transpose(bank[i][:, 0:n], S[0:n, i, 0:P], ident[0:n, 0:n]).then_inc(s["rows_turned"], 1)
            pe.wait_ge(s["x_in"], 16)
            for k in range(KD):
                b = bank[4 + k % 2]
                if k >= 2:
                    pe.wait_ge(s["x_updated"], k - 1)
                for t in range(NT):
                    ins = nc.tensor.transpose(b[:, t * P:(t + 1) * P], xtok[:, t, k * P:(k + 1) * P], ident)
                ins.then_inc(s["x_turned"], 1)

            def mod_sum(used, a4, n):
                pe.wait_ge(s["mod_used"], used)
                for j in range(2):
                    ins = mm(bank[6][:, 2 * n + j:2 * n + j + 1], modacc[:, a4, j * P:(j + 1) * P], ones[:, 0:1], start=True, stop=True)
                ins.then_inc(s["mod_turned"], 1)

            for c in range(MOD_FIRST):
                mod_sum(c + 1, c % 4, c)

            def norm(n):
                for k in range(KD):
                    pe.wait_ge(s["sq_ready"], n * KD + k + 1)
                    mm(bank[7][:, :], onesD, sq[:, k % 2, :], start=k == 0, stop=k == KD - 1).then_inc(s["sq_used"], 1)

            def feature_half(b, w, j, src, width=T):
                for k in range(KD):
                    ins = mm(b[:, 0:width], w[:, k, j * P:(j + 1) * P], src[:, k, 0:width], start=k == 0, stop=k == KD - 1)
                return ins

            def token_half(b, w, j, src, nt=NT):
                for t in range(nt):
                    for k in range(KD):
                        ins = mm(b[:, t * P:(t + 1) * P], src[:, k, t * P:(t + 1) * P], w[:, k, j * P:(j + 1) * P],
                                 start=k == 0, stop=k == KD - 1)
                return ins

            def attention(jobs, unit0, U, J, G, Q, scores):
                n = len(jobs)
                for j in range(n + 3):
                    if j < n:
                        for m in range(unit0[j + 1] - unit0[j]):
                            u = unit0[j] + m
                            if u >= NS:
                                pe.wait_ge(s["max_ready"], U + (u - NS + 1))
                            scores(jobs[j], m, bank[u % NS]).then_inc(s["s_done"], 1)
                    if 2 <= j < n + 2:
                        jj = j - 2
                        u, qb = unit0[jj + 1] - 1, jobs[jj][3]
                        pe.wait_ge(s["p_ready"], J + (jj + 1))
                        if jj >= 2:
                            pe.wait_ge(s["pt_ready"], J + (jj - 1))
                        for kb in range(qb + 1):
                            ins = nc.tensor.transpose(bank[4 + jj % 2][:, kb * P:(kb + 1) * P], S[:, u % NS, kb * P:(kb + 1) * P], ident)
                        ins.then_inc(s["t_done"], 1)
                    if j >= 3 and jobs[j - 3][3] == NT - 1:
                        g = jobs[j - 3][2]
                        pe.wait_ge(s["pt_ready"], J + (j - 2))
                        if g % 2 == 0 and g >= 4:
                            pe.wait_ge(s["o_copied"], Q + (g // 2 - 1))
                        ob = bank[6 + g // 2 % 2]
                        for kb in range(NT):
                            ins = mm(ob[HD * (g % 2):HD * (g % 2) + HD, kb * P:T], v[:, kb, g * HD:(g + 1) * HD],
                                     PT[:, g % 2, kb, kb * P:T], start=kb == 0, stop=kb == NT - 1)
                        ins.then_inc(s["pv_done"], 1)

            def layer_scores(job, m, b):
                kind, h, g, qb = job
                w = (qb + 1) * P
                p0, K = (HD * (h % 2) + 32 * m, 32) if kind == "A" else (HD * (h % 2), HD)
                ins = mm(b[:, 0:w], qk[p0:p0 + K, QT[kind] + h // 2, qb * P:(qb + 1) * P],
                         qk[p0:p0 + K, KT[kind] + h // 2, 0:w], start=True, stop=kind != "C")
                if kind == "C":
                    ins = mm(b[:, 0:w], kc[0:C_HEADS, K_SEL + h * P:K_SEL + (h + 1) * P], F6[:, 0:w], start=False, stop=True)
                return ins

            with pe.Fori(0, DEPTH) as l:
                norm(2 * l)
                for h in range(2 * IN_SLOTS + 1):
                    if h < 2 * IN_SLOTS:
                        i, j = divmod(h, 2)
                        if j == 0:
                            w_wait(pe, l, i)
                        if h == 0:
                            pe.wait_ge(s["h_ready"], 2 * l * KD + KD)
                        if h >= 2:
                            pe.wait_ge(s["acc_copied"], l * 25 + (h - 1))
                        half = feature_half if h in QK_OF else token_half
                        half(bank[h % 2], wring[:, i % RING, :, :], j, hT).then_inc(s["tiles_done"], 1)
                        if h % 2 and h // 2 >= 5:
                            for q in (2 * (h // 2 - 5), 2 * (h // 2 - 5) + 1):
                                mod_sum(l * MOD_CHUNKS + (MOD_FIRST + q + 1), q % 4, MOD_FIRST + q)
                    if h - 1 in ROPE:
                        r = ROPE.index(h - 1)
                        pe.wait_ge(s["acc_copied"], l * 25 + h)
                        if r >= 2:
                            pe.wait_ge(s["rope_done"], l * len(ROPE) + (r - 1))
                        R = K_RA if h - 1 < 4 else K_RB
                        mm(bank[2 + r % 2][:, :], kc[:, R:R + P], raw[:, r % 2, :], start=True, stop=True).then_inc(s["rot_done"], 1)
                pe.wait_ge(s["w6_in"], l * 16 + 16)
                pe.wait_ge(s["acc_copied"], l * 25 + 23)
                for k in range(KD):
                    ins = mm(bank[0][0:C_HEADS, :], wfz[:, k, :], hT[:, k, :], start=k == 0, stop=k == KD - 1)
                ins.then_inc(s["fz_done"], 1)
                for q in (2 * MOD_PAIRS - 2, 2 * MOD_PAIRS - 1):
                    mod_sum(l * MOD_CHUNKS + (MOD_FIRST + q + 1), q % 4, MOD_FIRST + q)
                pe.wait_ge(s["rope_done"], l * len(ROPE) + len(ROPE))
                pe.wait_ge(s["acc_copied"], l * 25 + 25)
                pe.wait_ge(s["decay_ready"], l + 1)
                attention(JOBS, UNIT0, l * UNITS, l * len(JOBS), l * HEADS, l * PAIRS, layer_scores)
                for t in range(2):
                    pe.wait_ge(s["sub_sq"], l * 2 + (t + 1))
                    mm(bank[2 + t][:, :], blk64, sq[:, t, :], start=True, stop=True).then_inc(s["sub_sum"], 1)
                pe.wait_ge(s["o_copied"], l * PAIRS + PAIRS)
                pe.wait_ge(s["sub_done"], l * 2 + 2)
                for d in range(KD):
                    i, j = IN_SLOTS + d // 2, d % 2
                    if j == 0:
                        w_wait(pe, l, i)
                    if d >= 2:
                        pe.wait_ge(s["x_updated"], l * 24 + (8 + d - 1))
                    feature_half(bank[d % 2], wring[:, i % RING, :, :], j, hT).then_inc(s["tiles_done"], 1)
                norm(2 * l + 1)
                i = IN_SLOTS + OUT_SLOTS
                for hh in range(2):
                    for f in range(hh * FH, hh * FH + FH):
                        w_wait(pe, l, i)
                        if f == 0:
                            pe.wait_ge(s["h_ready"], 2 * l * KD + 2 * KD)
                        if f % FH < 2:
                            if hh == 1:
                                pe.wait_ge(s["x_updated"], l * 24 + (16 + (4 if f % 2 else 2)))
                        else:
                            pe.wait_ge(s["act_ready"], l * FT + (f - 1))
                        for j in range(2):
                            feature_half(bank[4 * hh + 2 * (f % 2) + j], wring[:, i % RING, :, :], j, hT).then_inc(s["tiles_done"], 1)
                        if 3 <= f < 3 + NEXT_PAIRS:
                            with pe.If(l < DEPTH - 1):
                                for q in (2 * (f - 3), 2 * (f - 3) + 1):
                                    mod_sum(l * MOD_CHUNKS + (MOD_FIRST + 2 * MOD_PAIRS + q + 1), q % 4, q)
                        i += 1
                    for c in range(DOWN_SLOTS):
                        w_wait(pe, l, i)
                        for j in range(min(2, FH - 2 * c)):
                            f = 2 * c + j
                            pe.wait_ge(s["act_ready"], l * FT + (hh * FH + f + 1))
                            for d in range(KD):
                                if f == 0 and d == 4:
                                    pe.wait_ge(s["act_ready"], l * FT + (hh * FH + FH))
                                ins = mm(bank[(d + 4 - 4 * hh) % 8][:, :], wdown[:, i % RING, j, d * P:(d + 1) * P], gated[:, f, :],
                                         start=f == 0, stop=f == FH - 1)
                                if f == FH - 1:
                                    ins.then_inc(s["down_done"], 1)
                            if f < FH - 1:
                                ins.then_inc(s["tiles_done"], 1)
                        i += 1

            L = DEPTH
            pe.wait_ge(s["mem_scaled"], 2)
            pe.wait_ge(s["x_updated"], 56)
            for k in range(KD):
                if k >= 2:
                    pe.wait_ge(s["mem_ready"], k - 1)
                for m in range(2):
                    ins = nc.tensor.transpose(bank[k % 2][:, m * P:(m + 1) * P], mem_tok[:, m, k * P:(k + 1) * P], ident)
                ins.then_inc(s["mem_turned"], 1)
            norm(2 * L)
            norm(2 * L + 1)
            pe.wait_ge(s["h_ready"], 5 * KD)
            pe.wait_ge(s["mem_ready"], KD)
            pe.wait_ge(s["gate_in"], 64)
            for h in range(2 * IN2):
                i, j = divmod(h, 2)
                if j == 0:
                    w_wait(pe, L, i)
                if h >= 2:
                    pe.wait_ge(s["acc_copied"], L * 25 + h - 1)
                half = feature_half if h < 16 else token_half
                half(bank[h % 2], wring[:, i % RING, :, :], j, hT).then_inc(s["tiles_done"], 1)
                if 8 <= h < 12:
                    c = h - 8
                    pe.wait_ge(s["conv2_ready"], c + 1)
                    if c >= 2:
                        pe.wait_ge(s["gates_ready"], 2 * (c - 1))
                    for m in range(2):
                        mm(bank[2 + 2 * (c % 2) + m][:, :], wgate[:, m, c, :], xc[:, c, :], start=True, stop=True).then_inc(s["gate_done"], 1)
            acc2 = L * 25 + 2 * IN2
            pe.wait_ge(s["acc_copied"], acc2)
            pe.wait_ge(s["gates_ready"], 2 * CT)

            def scores2(job, m, b):
                _, h, g, qb = job
                w = (qb + 1) * P
                p0 = HD * (h % 2)
                return mm(b[:, 0:w], qk[p0:p0 + HD, 8 + h // 2, qb * P:(qb + 1) * P], qk[p0:p0 + HD, 12 + h // 2, 0:w], start=True, stop=True)

            attention(JOBS2, UNIT02, L * UNITS, L * len(JOBS), L * HEADS, L * PAIRS, scores2)
            pe.wait_ge(s["o_copied"], L * PAIRS + HEADS2 // 2)
            for grp in range(2):
                if grp:
                    pe.wait_ge(s["std_ready"], 7)
                for k in range(CT):
                    pe.wait_ge(s["sq_ready"], 6 * KD + CT * grp + k + 1)
                    mm(bank[7][:, :], onesR, sq[:, k % 2, :], start=k == 0, stop=k == CT - 1).then_inc(s["sq_used"], 1)
            pe.wait_ge(s["h_ready"], 6 * KD)

            def to_x(i0, first):
                for d in range(KD):
                    i, j = i0 + d // 2, d % 2
                    if j == 0:
                        w_wait(pe, L, i)
                    if d >= 2:
                        pe.wait_ge(s["x_updated"], first + d - 1)
                    feature_half(bank[d % 2], wring[:, i % RING, :, :], j, hT).then_inc(s["tiles_done"], 1)

            to_x(IN2, 64)
            i = IN2 + OUT2
            pe.wait_ge(s["x_updated"], 72)
            for h in range(16):
                if h % 2 == 0:
                    w_wait(pe, L, i + h // 2)
                if h >= 2:
                    pe.wait_ge(s["acc_copied"], acc2 + h - 1)
                w = wring[:, (i + h // 2) % RING, :, :]
                ins = feature_half(bank[h % 2], w, h % 2, memT, NMEM) if h < 8 else token_half(bank[h % 2], w, h % 2, memT, 2)
                ins.then_inc(s["tiles_done"], 1)
            i += 8
            norm(7)
            pe.wait_ge(s["h_ready"], 7 * KD)
            for h in range(8):
                if h % 2 == 0:
                    w_wait(pe, L, i + h // 2)
                pe.wait_ge(s["acc_copied"], acc2 + 16 + h - 1)
                feature_half(bank[h % 2], wring[:, (i + h // 2) % RING, :, :], h % 2, hT).then_inc(s["tiles_done"], 1)
            i += 4
            pe.wait_ge(s["acc_copied"], acc2 + 24)
            U, J = L * UNITS + len(JOBS2), L * len(JOBS) + len(JOBS2)
            n = XHEADS * NT
            for j in range(n + 3):
                if j < n:
                    h, qb = divmod(j, NT)
                    if j >= NS:
                        pe.wait_ge(s["exp_done"], U + j - NS + 1)
                    for kt in range(2):
                        ins = mm(bank[j % NS][:, 0:NMEM], xq[:, 2 * h + kt, qb * P:(qb + 1) * P], xk[:, 2 * h + kt, :], start=kt == 0, stop=kt == 1)
                    ins.then_inc(s["s_done"], 1)
                if 2 <= j < n + 2:
                    jj = j - 2
                    pe.wait_ge(s["p_ready"], J + jj + 1)
                    if jj >= 2:
                        pe.wait_ge(s["pt_ready"], J + jj - 1)
                    for m in range(2):
                        ins = nc.tensor.transpose(bank[4 + jj % 2][:, m * P:(m + 1) * P], S[:, jj % NS, m * P:(m + 1) * P], ident)
                    ins.then_inc(s["t_done"], 1)
                if j >= 3 and (j - 3) % NT == NT - 1:
                    g = (j - 3) // NT
                    pe.wait_ge(s["pt_ready"], J + j - 2)
                    if g >= 1:
                        pe.wait_ge(s["o_copied"], L * PAIRS + HEADS2 // 2 + 2 * g)
                    for dt in range(2):
                        for m in range(2):
                            ins = mm(bank[6 + dt][:, :], xv[:, m, (2 * g + dt) * P:(2 * g + dt + 1) * P], PT[:, g % 2, m, :], start=m == 0, stop=m == 1)
                    ins.then_inc(s["pv_done"], 1)
            pe.wait_ge(s["o_copied"], L * PAIRS + HEADS2 // 2 + 2 * XHEADS)
            to_x(i, 72)
            norm(8)
            pe.wait_ge(s["h_ready"], 8 * KD)
            pe.wait_ge(s["router_in"], 32)
            for t in range(NT):
                for k in range(KD):
                    ins = mm(bank[6][:, t * NR:(t + 1) * NR], hT[:, k, t * P:(t + 1) * P], wrt[:, k, :], start=k == 0, stop=k == KD - 1)
            ins.then_inc(s["logits_done"], 1)
            for n in range(2 * NT):
                t, c = divmod(n, 2)
                if n >= 2:
                    pe.wait_ge(s["h_tok_ready"], n - 1)
                for k in range(4):
                    ins = nc.tensor.transpose(bank[n % 2][:, k * P:(k + 1) * P], hT[:, 4 * c + k, t * P:(t + 1) * P], ident)
                ins.then_inc(s["h_tok_turned"], 1)
            for n in range(2 * NT):
                t, c = divmod(n, 2)
                if n >= 2:
                    pe.wait_ge(s["x_tok_ready"], n - 1)
                else:
                    pe.wait_ge(s["h_tok_ready"], 2 * NT - 1 + n)
                for k in range(4):
                    ins = nc.tensor.transpose(bank[n % 2][:, k * P:(k + 1) * P], xT[:, 4 * c + k, t * P:(t + 1) * P], ident)
                ins.then_inc(s["x_tok_turned"], 1)
            pe.wait_ge(s["sel_ready"], 1)
            for t in range(NT):
                for tt in range(t):
                    mm(bank[4][:, t * EXPERTS:(t + 1) * EXPERTS], ones, rt[:, 5, tt, :], start=tt == 0, stop=False)
                mm(bank[4][:, t * EXPERTS:(t + 1) * EXPERTS], kc[:, K_TRI:K_TRI + P], rt[:, 5, t, :], start=t == 0, stop=True)
            for tt in range(NT):
                ins = mm(bank[5][:, 0:EXPERTS], ones, rt[:, 5, tt, :], start=tt == 0, stop=tt == NT - 1)
            ins.then_inc(s["count_done"], 1)
            pe.wait_ge(s["src_float"], 1)
            nc.tensor.transpose(bank[6][:, 0:BLOCKS], src_f[:, :], ident[0:BLOCKS, 0:BLOCKS]).then_inc(s["src_turned"], 1)
            pe.wait_ge(s["plan_ready"], 1)

            def turn_rows(par, n):
                pe.wait_ge(s[f"xe_in{par}"], n * 16 + 16)
                for k in range(KD):
                    ins = nc.tensor.transpose(bank[4 + k // 4][:, (k % 4) * P:(k % 4 + 1) * P], xs[:, par, k * P:(k + 1) * P], ident)
                ins.then_inc(s["xe_turned"], 1)

            def expert_block(b, par, n, nxt, first=False):
                pe.wait_ge(s["xeT_ready"], b + 1)
                if not first:
                    pe.wait_ge(s["act_e"], b)
                has_rows = pe.value_load(blkU[0:1, bass.ds(b, 1)], min_val=0, max_val=1)
                with pe.If(has_rows > 0):
                    for m, done in enumerate(("gate_e_done", "up_e_done")):
                        pe.wait_ge(s[f"w_e{3 * par + m}"], n * 16 + 16)
                        w = ering[:, 3 * par + m, :].rearrange("p (k n) -> p k n", k=KD)
                        for k in range(KD):
                            ins = mm(bank[m][:, :], xsT[:, par, k, :], w[:, k, :], start=k == 0, stop=k == KD - 1)
                        ins.then_inc(s[done], 1)
                with pe.Else():
                    pe.sem_inc(s["gate_e_done"], 1)
                    pe.sem_inc(s["up_e_done"], 1)
                if nxt:
                    turn_rows(1 - par, n + par)
                pe.wait_ge(s["act_e"], b + 1)
                for k in range(4):
                    ins = nc.tensor.transpose(bank[6][:, k * P:(k + 1) * P], ea[:, k * P:(k + 1) * P], ident)
                ins.then_inc(s["actT_turned"], 1)
                pe.wait_ge(s["actT_ready"], b + 1)
                if not first:
                    pe.wait_ge(s["y_ready"], b * 2)
                with pe.If(has_rows > 0):
                    pe.wait_ge(s[f"w_e{3 * par + 2}"], n * 16 + 16)
                    w = ering[:, 3 * par + 2, :].rearrange("p (k n) -> p k n", k=4)
                    for c in range(2):
                        for k in range(4):
                            ins = mm(bank[2 + c][:, :], eaT[:, k, :], w[:, k, c * T:(c + 1) * T], start=k == 0, stop=k == 3)
                        ins.then_inc(s["e_down_done"], 1)
                with pe.Else():
                    pe.sem_inc(s["e_down_done"], 2)

            turn_rows(0, 0)
            expert_block(0, 0, 0, True, True)
            expert_block(1, 1, 0, True)
            with pe.Fori(1, BLOCKS // 2 - 1) as g:
                for par in range(2):
                    expert_block(g * 2 + par, par, g, True)
            n = BLOCKS // 2 - 1
            expert_block(2 * n, 0, n, True)
            expert_block(2 * n + 1, 1, n, False)

        @block.scalar
        def _(act):
            af = nc.scalar.activation
            act.wait_ge(s["setup_ready"], 1)
            for m, w in enumerate(("rnn_wa_2", "rnn_wx_2")):
                for half in range(2):
                    act.dma_start(wgate[HD * half:HD * half + HD, m, :, HD * half:HD * half + HD],
                                  a[w][0].rearrange("(c two) k n -> k two c n", two=2)[:, half]).then_inc(s["gate_in"], 16)
            act.dma_start(wrt[:, :, :], a["router_w"].rearrange("(k p) n -> p k n", p=P)).then_inc(s["router_in"], 16)
            act.dma_start(rb[:, :], bass.AP(a["router_b"].tensor, 0, [[0, P], [1, NR]])).then_inc(s["router_in"], 16)
            act.wait_ge(s["cols_copied"], 1)
            af(small[:, 0:KD], small[:, 8:8 + KD], ACT.Silu).then_inc(s["silu_c"], 1)
            act.wait_ge(s["cols_copied"], 2)
            af(small[:, 20:24], small[:, 16:20], ACT.Exp).then_inc(s["lam_exp"], 1)
            act.wait_ge(s["lam2_abs"], 1)
            af(small[:, 40:44], small[:, 40:44], ACT.Exp, scale=-1.0).then_inc(s["lam2_exp"], 1)

            def norm(n, before, shift):
                for k in range(KD):
                    act.wait_ge(s["x_updated"], before + (k + 1))
                    if k >= 2:
                        act.wait_ge(s["sq_used"], n * KD + (k - 1))
                    af(sq[:, k % 2, :], xT[:, k, :], ACT.Square).then_inc(s["sq_ready"], 1)
                act.wait_ge(s["sq_used"], n * KD + KD)
                af(std[:, :], bank[7][:, :], ACT.Sqrt, bias=epsc[:, 0:1]).then_inc(s["std_ready"], 1)
                if shift is not None:
                    for k in range(KD):
                        act.wait_ge(s["hn_ready"], n * KD + (k + 1))
                        af(hT[:, k, :], hn[:, k % 2, :], ACT.Identity, bias=pc[:, shift + k:shift + k + 1]).then_inc(s["h_ready"], 1)

            def attention(jobs, unit0, U, J, G, Q, scale_of, out, after=None):
                n = len(jobs)
                for j in range(n + 4):
                    if j < n:
                        for m in range(unit0[j + 1] - unit0[j]):
                            u = unit0[j] + m
                            act.wait_ge(s["max_ready"], U + (u + 1))
                            w = (jobs[j][3] + 1) * P
                            af(S[:, u % NS, 0:w], S[:, u % NS, 0:w], ACT.Exp, scale=scale_of(jobs[j]), bias=mx[:, 1, u % 8:u % 8 + 1],
                               accum_out=mx[:, 2, u % 8:u % 8 + 1]).then_inc(s["exp_done"], 1)
                        if after is not None:
                            after(jobs[j])
                    if 2 <= j < n + 2:
                        jj = j - 2
                        _, _, g, qb = jobs[jj]
                        act.wait_ge(s["t_done"], J + (jj + 1))
                        if qb == 0 and g >= 2:
                            act.wait_ge(s["pv_done"], G + (g - 1))
                        af(PT[:, g % 2, 0:qb + 1, qb * P:(qb + 1) * P],
                           bank[4 + jj % 2][:, 0:(qb + 1) * P].rearrange("p (k q) -> p k q", q=P), ACT.Copy).then_inc(s["pt_ready"], 1)
                    if j >= 4 and jobs[j - 4][3] == NT - 1 and jobs[j - 4][2] % 2:
                        g = jobs[j - 4][2]
                        act.wait_ge(s["pv_done"], G + (g + 1))
                        af(out(g // 2), bank[6 + g // 2 % 2][:, :], ACT.Copy).then_inc(s["o_copied"], 1)

            with act.Fori(0, DEPTH) as l:
                act.wait_ge(s["table_ready"], l + 1)
                norm(2 * l, l * 24, SH1)
                for h in range(2 * IN_SLOTS):
                    act.wait_ge(s["tiles_done"], tiles(l, h + 1))
                    b = bank[h % 2]
                    if h in ROPE:
                        r = ROPE.index(h)
                        if r >= 2:
                            act.wait_ge(s["rope_done"], l * len(ROPE) + (r - 1))
                        af(raw[:, r % 2, :], b[:, :], ACT.Copy).then_inc(s["acc_copied"], 1)
                    elif h in QK_OF:
                        af(qk[:, QK_OF[h], :], b[:, :], ACT.Copy).then_inc(s["acc_copied"], 1)
                    else:
                        c = V_OF[h] * P
                        af(v[:, :, c:c + P], b[:, :].rearrange("p (t c) -> p t c", t=NT), ACT.Copy).then_inc(s["acc_copied"], 1)
                act.wait_ge(s["fz_done"], l + 2)
                act.wait_ge(s["fb_in"], 16)
                af(z6[:, 0, :], bank[0][0:C_HEADS, :], ACT.Identity, bias=pc[0:C_HEADS, 106:107]).then_inc(s["acc_copied"], 1)
                act.wait_ge(s["z_abs"], l + 1)
                af(z6[:, 1, :], z6[:, 1, :], ACT.Exp, scale=-1.0).then_inc(s["z_exp"], 1)
                attention(JOBS, UNIT0, l * UNITS, l * len(JOBS), l * HEADS, l * PAIRS,
                          lambda job: (HD // 2 if job[0] == "A" else HD) ** -0.5, lambda p: hT[:, p, :])
                for t in range(2):
                    act.wait_ge(s["sub_sum"], l * 2 + (t + 1))
                    af(raw[:, t, :], bank[2 + t][:, :], ACT.Sqrt, bias=epsc[:, 1:2]).then_inc(s["sub_std"], 1)
                norm(2 * l + 1, l * 24 + 8, SH2)
                for f in range(FT):
                    hh = f // FH
                    act.wait_ge(s["tiles_done"], l * TILES + (TILES + CUM[IN_SLOTS + OUT_SLOTS + f + hh * DOWN_SLOTS] + 2))
                    if f >= 2:
                        act.wait_ge(s["conv_done"], l * FT + (f - 1))
                    af(gpad[:, f % 2, 2:T + 2], bank[4 * hh + 2 * (f % 2) + 1][:, :], ACT.Copy).then_inc(s["gpad_ready"], 1)
                    act.wait_ge(s["conv_done"], l * FT + (f + 1))
                    if f >= 2:
                        act.wait_ge(s["act_ready"], l * FT + (f - 1))
                    af(sg[:, f % 2, :], y[:, f % 2, :], ACT.Silu).then_inc(s["silu_done"], 1)

            L = DEPTH
            act.wait_ge(s["mem_in"], 16)
            act.wait_ge(s["act_ready"], L * FT)
            for m in range(2):
                if m:
                    act.wait_ge(s["mem_sq"], m)
                af(tmp[:, 2 * T:4 * T], mem_tok[:, m, :], ACT.Square, accum_out=small[:, 24 + m:25 + m]).then_inc(s["mem_sq"], 1)
            act.wait_ge(s["mem_sq"], 2)
            af(small[:, 26:28], small[:, 24:26], ACT.Sqrt, scale=1.0 / D, bias=epsc[:, 0:1]).then_inc(s["mem_std"], 1)
            for k in range(KD):
                act.wait_ge(s["mem_turned"], k + 1)
                af(memT[:, k, :], bank[k % 2][:, 0:NMEM], ACT.Copy, scale=pc2[:, E_MEM + k:E_MEM + k + 1]).then_inc(s["mem_ready"], 1)

            def load_bias(h):
                act.dma_start(toep[:, h % 2, :], a["bias_rows"][h]).then_inc(s[f"toep_in{h % 2}"], 16)

            load_bias(0)
            load_bias(1)
            norm(2 * L, 48, None)
            norm(2 * L + 1, 56, None)
            for h in range(2 * IN2):
                act.wait_ge(s["tiles_done"], tiles(L, h + 1))
                if h < 4:
                    af(xr[:, h, 3:T + 3], bank[h % 2][:, :], ACT.Copy).then_inc(s["acc_copied"], 1)
                elif h < 16:
                    af(qk[:, h, :], bank[h % 2][:, :], ACT.Copy).then_inc(s["acc_copied"], 1)
                else:
                    c = (h - 16) * P
                    af(v[:, :, c:c + P], bank[h % 2][:, :].rearrange("p (t c) -> p t c", t=NT), ACT.Copy).then_inc(s["acc_copied"], 1)
                if 8 <= h < 12:
                    c = h - 8
                    if c >= 1:
                        act.wait_ge(s["rec_ready"], c)
                    for m, g in enumerate((r_gate, i_gate)):
                        act.wait_ge(s["gate_done"], 2 * c + m + 1)
                        at = (E_BA, E_BX)[m] + c
                        af(g, bank[2 + 2 * (c % 2) + m][:, :], ACT.Sigmoid, bias=pc2[:, at:at + 1]).then_inc(s["gates_ready"], 1)
                    act.wait_ge(s["gates_ready"], 2 * c + 1)
                    af(a_rec, r_gate, ACT.Exp, scale=pc2[:, NPRM2 + c:NPRM2 + c + 1]).then_inc(s["rec_act"], 1)
                    af(u_tmp, r_gate, ACT.Tanh, scale=pc2[:, NPRM2 + 4 + c:NPRM2 + 5 + c]).then_inc(s["rec_act"], 1)
                    act.wait_ge(s["rec_u"], c + 1)
                    af(u_tmp, h_rec, ACT.Sqrt).then_inc(s["rec_act"], 1)
                    af(g_rec, qk[:, 4 + c, :], ACT.Gelu_apprx_tanh).then_inc(s["rec_act"], 1)

            def next_bias(job):
                if job[3] == NT - 1 and job[1] + 2 < HEADS2:
                    load_bias(job[1] + 2)

            attention(JOBS2, UNIT02, L * UNITS, L * len(JOBS), L * HEADS, L * PAIRS, lambda job: HD ** -0.5, lambda p: hT[:, 4 + p, :], next_bias)
            for grp in range(2):
                q0 = 6 * KD + CT * grp
                if grp:
                    act.wait_ge(s["h_ready"], 5 * KD + 1)
                for k in range(CT):
                    act.wait_ge(s["sq_used"], q0 + k - 1)
                    if grp:
                        act.wait_ge(s["o_copied"], L * PAIRS + k + 1)
                        src = hT[:, CT + k, :]
                    else:
                        act.wait_ge(s["rec_ready"], k + 1)
                        src = xc[:, k, :]
                    af(sq[:, k % 2, :], src, ACT.Square).then_inc(s["sq_ready"], 1)
                act.wait_ge(s["sq_used"], q0 + CT)
                af(std[:, :], bank[7][:, :], ACT.Sqrt, bias=epsc[:, 0:1]).then_inc(s["std_ready"], 1)
            for h in range(16):
                act.wait_ge(s["tiles_done"], tiles(L, 2 * (IN2 + OUT2) + h + 1))
                if h < 8:
                    af(xk[:, h, :], bank[h % 2][:, 0:NMEM], ACT.Copy).then_inc(s["acc_copied"], 1)
                else:
                    c = (h - 8) * P
                    af(xv[:, :, c:c + P], bank[h % 2][:, 0:2 * P].rearrange("p (t c) -> p t c", t=2), ACT.Copy).then_inc(s["acc_copied"], 1)
            norm(7, 64, None)
            for h in range(8):
                act.wait_ge(s["tiles_done"], tiles(L, 2 * (IN2 + OUT2 + 8) + h + 1))
                af(xq[:, h, :], bank[h % 2][:, :], ACT.Copy).then_inc(s["acc_copied"], 1)
            U, J, G = L * UNITS + len(JOBS2), L * len(JOBS) + len(JOBS2), L * HEADS + HEADS2
            n = XHEADS * NT
            for j in range(n + 4):
                if j < n:
                    act.wait_ge(s["max_ready"], U + j + 1)
                    if j >= NS:
                        act.wait_ge(s["t_done"], J + j - NS + 1)
                    af(S[:, j % NS, 0:NMEM], bank[j % NS][:, 0:NMEM], ACT.Exp, scale=XDIM ** -0.5, bias=mx[:, 1, j % 8:j % 8 + 1],
                       accum_out=mx[:, 2, j % 8:j % 8 + 1]).then_inc(s["exp_done"], 1)
                if 2 <= j < n + 2:
                    jj = j - 2
                    g, qb = divmod(jj, NT)
                    act.wait_ge(s["t_done"], J + jj + 1)
                    if qb == 0 and g >= 2:
                        act.wait_ge(s["pv_done"], G + g - 1)
                    af(PT[:, g % 2, 0:2, qb * P:(qb + 1) * P], bank[4 + jj % 2][:, 0:2 * P].rearrange("p (k q) -> p k q", q=P), ACT.Copy).then_inc(s["pt_ready"], 1)
                if j >= 4 and (j - 4) % NT == NT - 1:
                    g = (j - 4) // NT
                    act.wait_ge(s["pv_done"], G + g + 1)
                    for dt in range(2):
                        af(hT[:, 2 * g + dt, :], bank[6 + dt][:, :], ACT.Copy).then_inc(s["o_copied"], 1)
            norm(8, 72, None)
            for n in range(2 * NT):
                t, c = divmod(n, 2)
                act.wait_ge(s["h_tok_turned"], n + 1)
                af(big[:, t * D + c * T:t * D + (c + 1) * T], bank[n % 2][:, :], ACT.Copy).then_inc(s["h_tok_ready"], 1)
            for n in range(2 * NT):
                t, c = divmod(n, 2)
                act.wait_ge(s["x_tok_turned"], n + 1)
                af(xtok[:, t, c * T:(c + 1) * T], bank[n % 2][:, :], ACT.Copy).then_inc(s["x_tok_ready"], 1)
            act.wait_ge(s["group_shifted"], 1)
            af(rg4[:, 0, :, :], rg4[:, 0, :, :], ACT.Exp).then_inc(s["sel_exp"], 1)
            act.wait_ge(s["second_shifted"], 1)
            af(rsm[:, 4, :], rsm[:, 4, :], ACT.Exp).then_inc(s["sel_exp"], 1)

            def send_rows(b, par):
                act.wait_ge(s["y_ready"], b * 2 + 2)
                act.dma_start(ys_dram[bass.ds(b * BLK, BLK), :], ysb[:, par, :]).then_inc(s[f"y_out{par}"], 16)

            def expert_act(b, first=False):
                act.wait_ge(s["gate_e_done"], b + 1)
                if not first:
                    act.wait_ge(s["act_e"], b)
                af(eg, bank[0][:, :], ACT.Silu).then_inc(s["silu_e"], 1)
                act.wait_ge(s["actT_turned"], b + 1)
                af(eaT, bank[6][:, :].rearrange("p (k c) -> p k c", k=4), ACT.Copy).then_inc(s["actT_ready"], 1)

            expert_act(0, True)
            expert_act(1)
            send_rows(0, 0)
            with act.Fori(1, BLOCKS // 2) as g:
                expert_act(g * 2)
                send_rows(g * 2 - 1, 1)
                expert_act(g * 2 + 1)
                send_rows(g * 2, 0)
            send_rows(BLOCKS - 1, 1)
            for t in range(NT):
                act.wait_ge(s["y_used"], 2 * t + 2)
                af(ysb[:, 0, :], xtok[:, t, :], ACT.Square, accum_out=small[:, 32 + t:33 + t]).then_inc(s["fin_sq"], 1)
                act.wait_ge(s["fin_sq"], t + 1)
                af(small[:, 36 + t:37 + t], small[:, 32 + t:33 + t], ACT.Sqrt, scale=1.0 / D, bias=epsc[:, 0:1]).then_inc(s["fin_std"], 1)

        @block.vector
        def _(dve):
            vec = nc.vector
            base = [0, 0]

            def link(ins):
                base[1] += 1
                ins.then_inc(s["chain"], 1)
                dve.wait_ge(s["chain"], base[0] + base[1])

            def stt(out, in0, sc, in1, op0, op1):
                return vec.scalar_tensor_tensor(out=out, in0=in0, scalar=sc, in1=in1, op0=op0, op1=op1)

            def log_sigmoid(z, e, t, out, announce, wait_exp):
                stt(e, z, -1.0, z, ALU.mult, ALU.max).then_inc(announce, 1)
                wait_exp()
                link(vec.tensor_scalar(t, e, 2.0, None, ALU.add))
                link(vec.reciprocal(t, t))
                link(vec.tensor_tensor(e, e, t, ALU.mult))
                link(vec.tensor_tensor(t, e, e, ALU.mult))
                link(vec.tensor_scalar(out, t, ATANH[0], None, ALU.mult))
                for c in ATANH[1:]:
                    link(stt(out, out, c, t, ALU.add, ALU.mult))
                link(stt(out, out, 1.0, e, ALU.add, ALU.mult))
                link(vec.tensor_scalar(t, z, 0.0, None, ALU.min))
                link(stt(out, out, -2.0, t, ALU.mult, ALU.add))

            vec.memset(epsc[:, 0:1], NORM_EPS)
            vec.memset(epsc[:, 1:2], SUBLN_EPS)
            vec.memset(one6[:, :], 1.0)
            vec.memset(gpad[:, :, :], 0.0)
            vec.memset(pcall[:, :, :], 0.0)
            vec.memset(zero[:, :], 0)
            link(vec.memset(wgate[:, :, :, :], 0.0))
            vec.memset(small[:, :], 0.0).then_inc(s["setup_ready"], 1)
            dve.wait_ge(s["setup_ready"], 1)
            dve.wait_ge(s["rows_turned"], 4)
            link(vec.tensor_copy(small[:, 8:16], bank[0][:, 96:104]))
            vec.memset(small[:, 60:61], 0.0).then_inc(s["cols_copied"], 1)
            for l in range(DEPTH):
                vec.tensor_copy(pcall[:, l, 0:NPRM], bank[1 + l][:, 0:NPRM])
                vec.tensor_copy(pcall[:, l, C_MOD:NCOL], bank[0][:, l * 48:(l + 1) * 48])
            link(vec.tensor_copy(pc2[:, 0:NPRM2], bank[3][:, 0:NPRM2]))
            dve.wait_ge(s["fb_in"], 16)
            for l in range(DEPTH):
                link(vec.tensor_copy(pcall[0:C_HEADS, l, 106:107], fb[:, l:l + 1]))
            dve.wait_ge(s["lam_in"], 16)
            for l in range(DEPTH):
                for m in range(2):
                    link(vec.tensor_tensor(lamp[:, l, 2 * m, :], lamp[:, l, 2 * m, :], lamp[:, l, 2 * m + 1, :], ALU.mult))
                    link(vec.tensor_reduce(small[:, 16 + 2 * l + m:17 + 2 * l + m], lamp[:, l, 2 * m, :], AX.X, ALU.add))
            vec.memset(small[:, 60:61], 0.0).then_inc(s["cols_copied"], 1)
            dve.wait_ge(s["lam_exp"], 1)
            for l in range(DEPTH):
                lam_init = 0.8 - 0.6 * math.exp(-0.3 * l)
                link(vec.tensor_tensor(small[:, 28:29], small[:, 21 + 2 * l:22 + 2 * l], small[:, 20 + 2 * l:21 + 2 * l], ALU.subtract))
                link(vec.tensor_scalar(pcall[:, l, C_LAM:C_LAM + 1], small[:, 28:29], -lam_init, None, ALU.add))
                link(vec.tensor_scalar(pcall[:, l, C_SUB:C_SUB + 1], pcall[:, l, C_SUB:C_SUB + 1], 1.0 - lam_init, None, ALU.mult))
            log_sigmoid(pc2[:, E_LAM:E_LAM + CT], small[:, 40:44], small[:, 44:48], small[:, 48:52], s["lam2_abs"],
                        lambda: dve.wait_ge(s["lam2_exp"], 1))
            vec.tensor_scalar(pc2[:, NPRM2:NPRM2 + CT], small[:, 48:52], 8.0, None, ALU.mult)
            vec.tensor_scalar(pc2[:, NPRM2 + CT:NPRM2 + 2 * CT], small[:, 48:52], -8.0, None, ALU.mult)
            dve.wait_ge(s["consts_in"], 16)
            vec.tensor_copy(tokid[:, :], kc[:, K_TOK:K_TOK + NT])
            for k in range(KD):
                dve.wait_ge(s["x_turned"], k + 1)
                vec.tensor_copy(xT[:, k, :], bank[4 + k % 2][:, :]).then_inc(s["x_updated"], 1)

            def mod_acc(steps, w, acc):
                vec.tensor_scalar(acc, w[:, 0, :], small[:, 0:1], None, ALU.mult).then_inc(s["mod_step"], 1)
                for k in range(1, KD):
                    dve.wait_ge(s["mod_step"], steps + k)
                    ins = stt(acc, w[:, k, :], small[:, k:k + 1], acc, ALU.mult, ALU.add)
                    ins.then_inc(s["mod_step" if k < KD - 1 else "mod_used"], 1)

            dve.wait_ge(s["silu_c"], 1)
            for c in range(MOD_FIRST):
                dve.wait_ge(s[f"mod_in{c % RING}"], 16 * (c // RING + 1))
                if c >= 4:
                    dve.wait_ge(s["mod_turned"], c - 3)
                mod_acc(c * (KD - 1), wring[:, c % RING, :, :], modacc[:, c % 4, :])
            dve.wait_ge(s["mod_turned"], MOD_FIRST)
            link(vec.tensor_tensor(pcall[:, 0, SH1:GT1], pcall[:, 0, SH1:GT1], bank[6][:, 0:2 * KD], ALU.add))

            def mod_pair(l, pair):
                for q in (2 * pair, 2 * pair + 1):
                    dve.wait_ge(s[f"mod_next{q % 2}"], l * (8 * MOD_CHUNKS) + 16 * (q // 2 + 1))
                    if q >= 4:
                        dve.wait_ge(s["mod_turned"], l * MOD_CHUNKS + (MOD_FIRST + q - 3))
                    mod_acc((l * MOD_CHUNKS + (MOD_FIRST + q)) * (KD - 1), mod_w[:, q % 2, :, :], modacc[:, q % 4, :])

            def norm(n, g, table, shift, stds=None, out=hT, done="h_ready"):
                dve.wait_ge(s["std_ready"], (n if stds is None else stds) + 1)
                link(vec.reciprocal(rs[:, :], std[:, :]))
                for k in range(KD):
                    if shift:
                        if k >= 2:
                            dve.wait_ge(s["h_ready"], n * KD + (k - 1))
                        stt(hn[:, k % 2, :], xT[:, k, :], table[:, g + k:g + k + 1], rs[:, :], ALU.mult, ALU.mult).then_inc(s["hn_ready"], 1)
                    else:
                        stt(out[:, k, :], xT[:, k, :], table[:, g + k:g + k + 1], rs[:, :], ALU.mult, ALU.mult).then_inc(s[done], 1)

            def add_to_x(d, b, gate):
                if gate is None:
                    ins = vec.tensor_tensor(xT[:, d, :], xT[:, d, :], b[:, :], ALU.add)
                else:
                    ins = stt(xT[:, d, :], b[:, :], pc[:, gate + d:gate + d + 1], xT[:, d, :], ALU.mult, ALU.add)
                ins.then_inc(s["x_updated"], 1)

            def attention(jobs, unit0, U, J, scale_of, mask_of, before=None):
                n = len(jobs)
                job_of = [i for i in range(n) for _ in range(unit0[i + 1] - unit0[i])]
                for j in range(n + 1):
                    if j < n:
                        kind, h, g, qb = jobs[j]
                        w = (qb + 1) * P
                        if before is not None:
                            before(jobs[j])
                        for m in range(unit0[j + 1] - unit0[j]):
                            u = unit0[j] + m
                            dve.wait_ge(s["s_done"], U + (u + 1))
                            if u >= NS:
                                dve.wait_ge(s["t_done"], J + (job_of[u - NS] + 1))
                            c = u % 8
                            vec.memset(small[:, 59:60], 0.0)
                            link(vec.tensor_tensor_reduce(S[:, u % NS, 0:w], bank[u % NS][:, 0:w], mask_of(jobs[j])[:, T - w:T], 1.0, -3.0e38,
                                                          ALU.add, ALU.max, mx[:, 0, c:c + 1]))
                            vec.tensor_scalar(mx[:, 1, c:c + 1], mx[:, 0, c:c + 1], -scale_of(jobs[j]), None, ALU.mult).then_inc(s["max_ready"], 1)
                    if j >= 1:
                        jj = j - 1
                        kind, h, g, qb = jobs[jj]
                        w = (qb + 1) * P
                        u0, u1 = unit0[jj], unit0[jj + 1] - 1
                        dve.wait_ge(s["exp_done"], U + (u1 + 1))
                        for u in range(u0, u1 + 1):
                            link(vec.reciprocal(mx[:, 0, u % 8:u % 8 + 1], mx[:, 2, u % 8:u % 8 + 1]))
                        r = mx[:, 0, u0 % 8:u0 % 8 + 1]
                        if u1 == u0:
                            vec.tensor_scalar(S[:, u0 % NS, 0:w], S[:, u0 % NS, 0:w], r, None, ALU.mult).then_inc(s["p_ready"], 1)
                        else:
                            r1 = mx[:, 0, u1 % 8:u1 % 8 + 1]
                            link(vec.tensor_tensor(r1, r1, pc[:, C_LAM:C_LAM + 1], ALU.mult))
                            link(vec.tensor_scalar(S[:, u0 % NS, 0:w], S[:, u0 % NS, 0:w], r, None, ALU.mult))
                            stt(S[:, u1 % NS, 0:w], S[:, u1 % NS, 0:w], r1, S[:, u0 % NS, 0:w], ALU.mult, ALU.add).then_inc(s["p_ready"], 1)

            CH0 = base[1]
            with dve.Fori(0, DEPTH) as l:
                base[0], base[1] = l * CH_LAYER + CH0, 0
                dve.wait_ge(s["x_updated"], l * 24 + KD)
                link(vec.tensor_copy(pc[:, :].rearrange("p (o c) -> p o c", o=1), pcall[:, bass.ds(l, 1), :]))
                link(stt(pc[:, C_GA:C_GA + KD], pc[:, SC1:SC1 + KD], 1.0, pc[:, C_GA:C_GA + KD], ALU.add, ALU.mult))
                vec.tensor_copy(small[:, 61:62], pc[:, 0:1]).then_inc(s["table_ready"], 1)
                norm(2 * l, C_GA, pc, True)
                for r, h in enumerate(ROPE):
                    dve.wait_ge(s["acc_copied"], l * 25 + (h + 1))
                    co, si = (K_CA, K_SA) if h < 4 else (K_CB, K_SB)
                    link(vec.tensor_tensor(t1[:, r % 2, :], raw[:, r % 2, :], kc[:, co:co + T], ALU.mult))
                    dve.wait_ge(s["rot_done"], l * len(ROPE) + (r + 1))
                    link(vec.tensor_tensor(rot[:, r % 2, :], bank[2 + r % 2][:, :], kc[:, si:si + T], ALU.mult))
                    vec.tensor_tensor(qk[:, QK_OF[h], :], t1[:, r % 2, :], rot[:, r % 2, :], ALU.add).then_inc(s["rope_done"], 1)
                    if h in (9, 11):
                        mod_pair(l, (h - 9) // 2)
                for pair in range(2, MOD_PAIRS):
                    mod_pair(l, pair)
                dve.wait_ge(s["acc_copied"], l * 25 + 25)
                log_sigmoid(z6[:, 0, :], z6[:, 1, :], z6[:, 2, :], z6[:, 3, :], s["z_abs"], lambda: dve.wait_ge(s["z_exp"], l + 1))
                dve.wait_ge(s["mod_turned"], l * MOD_CHUNKS + (MOD_FIRST + 2 * MOD_PAIRS))
                link(vec.tensor_tensor(pc[:, GT1:NCOL], pc[:, GT1:NCOL], bank[6][:, 2 * KD:6 * KD], ALU.add))
                link(stt(pc[:, C_GM:C_GM + KD], pc[:, SC2:SC2 + KD], 1.0, pc[:, C_GM:C_GM + KD], ALU.add, ALU.mult))
                vec.tensor_tensor_scan(F6[:, :], one6[0:C_HEADS, :], z6[:, 3, :], 0.0, ALU.mult, ALU.add).then_inc(s["decay_ready"], 1)
                attention(JOBS, UNIT0, l * UNITS, l * len(JOBS), lambda job: (HD // 2 if job[0] == "A" else HD) ** -0.5,
                          lambda job: kc[:, K_MB:K_MB + T] if job[0] == "B" else kc[:, K_MA:K_MA + T])
                dve.wait_ge(s["o_copied"], l * PAIRS + 2)
                for t in range(2):
                    vec.tensor_tensor(sq[:, t, :], hT[:, t, :], hT[:, t, :], ALU.mult).then_inc(s["sub_sq"], 1)
                for t in range(2):
                    dve.wait_ge(s["sub_std"], l * 2 + (t + 1))
                    link(vec.reciprocal(hn[:, t, :], raw[:, t, :]))
                    stt(hT[:, t, :], hT[:, t, :], pc[:, C_SUB:C_SUB + 1], hn[:, t, :], ALU.mult, ALU.mult).then_inc(s["sub_done"], 1)
                for d in range(KD):
                    dve.wait_ge(s["tiles_done"], tiles(l, CUM[IN_SLOTS] + d + 1))
                    add_to_x(d, bank[d % 2], GT1)
                norm(2 * l + 1, C_GM, pc, True)
                for f in range(FT):
                    hh = f // FH
                    if f == 3 + NEXT_PAIRS:
                        with dve.If(l < DEPTH - 1):
                            dve.wait_ge(s["mod_turned"], l * MOD_CHUNKS + (MOD_CHUNKS + MOD_FIRST))
                            nxt = pcall[:, bass.ds(next_layer(l), 1), SH1:GT1]
                            vec.tensor_tensor(nxt, nxt, bank[6][:, 0:2 * KD].rearrange("p (o c) -> p o c", o=1), ALU.add).then_inc(s["next_added"], 1)
                    dve.wait_ge(s["gpad_ready"], l * FT + (f + 1))
                    col = lambda i: pc[:, C_CW + i * FT + f:C_CW + i * FT + f + 1]
                    link(vec.tensor_scalar(y[:, f % 2, :], gpad[:, f % 2, 2:T + 2], col(2), pc[:, C_CB + f:C_CB + f + 1], ALU.mult, ALU.add))
                    link(stt(y[:, f % 2, :], gpad[:, f % 2, 1:T + 1], col(1), y[:, f % 2, :], ALU.mult, ALU.add))
                    stt(y[:, f % 2, :], gpad[:, f % 2, 0:T], col(0), y[:, f % 2, :], ALU.mult, ALU.add).then_inc(s["conv_done"], 1)
                    dve.wait_ge(s["silu_done"], l * FT + (f + 1))
                    vec.tensor_tensor(gated[:, f % FH, :], sg[:, f % 2, :], bank[4 * hh + 2 * (f % 2)][:, :], ALU.mult).then_inc(s["act_ready"], 1)
                    if 2 <= f < 2 + NEXT_PAIRS:
                        with dve.If(l < DEPTH - 1):
                            mod_pair(l, MOD_PAIRS + f - 2)
                    if f % FH == FH - 1:
                        for d in range(KD):
                            dve.wait_ge(s["down_done"], l * 2 * KD + (2 * KD + KD * hh + d + 1))
                            add_to_x(d, bank[(d + 4 - 4 * hh) % 8], GT2)
                assert base[1] == CH_LAYER, (base[1], CH_LAYER)
            base[0], base[1] = CH0 + DEPTH * CH_LAYER, 0

            L = DEPTH
            vec.memset(xr[:, :, 0:3], 0.0)
            dve.wait_ge(s["mem_std"], 1)
            link(vec.reciprocal(small[:, 26:28], small[:, 26:28]))
            for m in range(2):
                vec.tensor_scalar(mem_tok[:, m, :], mem_tok[:, m, :], small[:, 26 + m:27 + m], None, ALU.mult).then_inc(s["mem_scaled"], 1)
            norm(2 * L, E_FIN, pc2, False, out=xT, done="x_updated")
            dve.wait_ge(s["x_updated"], 64)
            norm(2 * L + 1, E_LN1, pc2, False)
            for c in range(CT):
                dve.wait_ge(s["acc_copied"], L * 25 + c + 1)
                w = lambda i: pc2[:, E_CW + i * CT + c:E_CW + i * CT + c + 1]
                link(vec.tensor_scalar(xc[:, c, :], xr[:, c, 3:T + 3], w(3), pc2[:, E_CB + c:E_CB + c + 1], ALU.mult, ALU.add))
                for i in (2, 1, 0):
                    ins = stt(xc[:, c, :], xr[:, c, i:i + T], w(i), xc[:, c, :], ALU.mult, ALU.add)
                    if i:
                        link(ins)
                ins.then_inc(s["conv2_ready"], 1)
            for c in range(CT):
                dve.wait_ge(s["rec_act"], 4 * c + 2)
                link(vec.tensor_scalar(h_rec, u_tmp, 1.0, None, ALU.add))
                link(vec.reciprocal(h_rec, h_rec))
                stt(h_rec, h_rec, 2.0, u_tmp, ALU.mult, ALU.mult).then_inc(s["rec_u"], 1)
                dve.wait_ge(s["gates_ready"], 2 * c + 2)
                link(vec.tensor_tensor(xc[:, c, :], xc[:, c, :], i_gate, ALU.mult))
                dve.wait_ge(s["rec_act"], 4 * c + 4)
                link(vec.tensor_tensor(xc[:, c, :], xc[:, c, :], u_tmp, ALU.mult))
                link(vec.tensor_tensor_scan(h_rec, a_rec, xc[:, c, :], 0.0, ALU.mult, ALU.add))
                vec.tensor_tensor(xc[:, c, :], h_rec, g_rec, ALU.mult).then_inc(s["rec_ready"], 1)

            def ready_bias(job):
                if job[3] == 0:
                    h = job[1]
                    dve.wait_ge(s[f"toep_in{h % 2}"], 16 * (h // 2 + 1))
                    bias = toep[:, h % 2, :]
                    link(vec.tensor_scalar(bias, bias, float(HD) ** 0.5, None, ALU.mult))
                    link(vec.memset(toep[0:HD, h % 2, T - HD:T], NEG))

            attention(JOBS2, UNIT02, L * UNITS, L * len(JOBS), lambda job: HD ** -0.5, lambda job: toep[:, job[1] % 2, :], ready_bias)
            for grp, g in enumerate((E_GR, E_GA)):
                dve.wait_ge(s["std_ready"], 7 + grp)
                if grp:
                    dve.wait_ge(s["h_ready"], 5 * KD + CT)
                link(vec.reciprocal(rs[:, :], std[:, :]))
                for k in range(CT):
                    src = hT[:, CT + k, :] if grp else xc[:, k, :]
                    stt(hT[:, CT * grp + k, :], src, pc2[:, g + k:g + k + 1], rs[:, :], ALU.mult, ALU.mult).then_inc(s["h_ready"], 1)

            def to_x(i):
                for d in range(KD):
                    dve.wait_ge(s["tiles_done"], tiles(L, 2 * i + d + 1))
                    add_to_x(d, bank[d % 2], None)

            to_x(IN2)
            norm(7, E_LN2, pc2, False, stds=8)
            U, J = L * UNITS + len(JOBS2), L * len(JOBS) + len(JOBS2)
            n = XHEADS * NT
            for j in range(n + 1):
                if j < n:
                    c = j % 8
                    dve.wait_ge(s["s_done"], U + j + 1)
                    link(vec.tensor_reduce(mx[:, 0, c:c + 1], bank[j % NS][:, 0:NMEM], AX.X, ALU.max))
                    vec.tensor_scalar(mx[:, 1, c:c + 1], mx[:, 0, c:c + 1], -XDIM ** -0.5, None, ALU.mult).then_inc(s["max_ready"], 1)
                if j >= 1:
                    c = (j - 1) % 8
                    dve.wait_ge(s["exp_done"], U + j)
                    link(vec.reciprocal(mx[:, 0, c:c + 1], mx[:, 2, c:c + 1]))
                    buf = S[:, (j - 1) % NS, 0:NMEM]
                    vec.tensor_scalar(buf, buf, mx[:, 0, c:c + 1], None, ALU.mult).then_inc(s["p_ready"], 1)
            to_x(IN2 + OUT2 + 12)
            norm(8, E_LN3, pc2, False, stds=9)

            dve.wait_ge(s["logits_done"], 1)
            tt = vec.tensor_tensor
            link(tt(rlog[:, :, :], bank[6][:, 0:NT * NR].rearrange("p (t n) -> p t n", t=NT), rb[:, :].unsqueeze(1).to_broadcast([P, NT, NR]), ALU.add))

            def first_max(val, n, top, key, onehot):
                b = lambda x: x.unsqueeze(2).to_broadcast([P, NT, n])
                order = kc[:, K_EI:K_EI + n].unsqueeze(1).to_broadcast([P, NT, n])
                link(vec.tensor_reduce(top, val, AX.X, ALU.max))
                link(tt(key, val, b(top), ALU.is_ge))
                link(tt(key, key, order, ALU.mult))
                link(vec.tensor_reduce(rsm[:, 9, :], key, AX.X, ALU.max))
                link(tt(onehot, key, b(rsm[:, 9, :]), ALU.is_equal))

            glog = rlog[:, :, 0:GROUPS]
            first_max(glog, GROUPS, rsm[:, 0, :], rg4[:, 1, :, :], rg4[:, 2, :, :])
            tt(rg4[:, 0, :, :], glog, rsm[:, 0, :].unsqueeze(2).to_broadcast([P, NT, GROUPS]), ALU.subtract).then_inc(s["group_shifted"], 1)
            link(vec.tensor_scalar(rg4[:, 2, :, :], rg4[:, 2, :, :], 1.0, -NEG, ALU.subtract, ALU.mult))
            el = rt[:, 0, :, :]
            for t in range(NT):
                ins = tt(el[:, t, :].rearrange("p (g e) -> p g e", g=GROUPS), rlog[:, t, GROUPS:NR].rearrange("p (g e) -> p g e", g=GROUPS),
                         rg4[:, 2, t, :].unsqueeze(2).to_broadcast([P, GROUPS, PER_GROUP]), ALU.add)
            link(ins)
            first_max(el, EXPERTS, rsm[:, 1, :], rt[:, 1, :, :], rt[:, 2, :, :])
            link(stt(el, rt[:, 2, :, :], 3.0 * NEG, el, ALU.mult, ALU.add))
            first_max(el, EXPERTS, rsm[:, 2, :], rt[:, 1, :, :], rt[:, 3, :, :])
            tt(rt[:, 5, :, :], rt[:, 2, :, :], rt[:, 3, :, :], ALU.add).then_inc(s["sel_ready"], 1)
            tt(rsm[:, 4, :], rsm[:, 2, :], rsm[:, 1, :], ALU.subtract).then_inc(s["second_shifted"], 1)
            dve.wait_ge(s["sel_exp"], 1)
            link(vec.tensor_reduce(rsm[:, 5, :], rg4[:, 0, :, :], AX.X, ALU.add))
            dve.wait_ge(s["sel_exp"], 2)
            link(vec.tensor_scalar(rsm[:, 6, :], rsm[:, 4, :], 1.0, None, ALU.add))
            link(tt(rsm[:, 6, :], rsm[:, 6, :], rsm[:, 5, :], ALU.mult))
            link(vec.reciprocal(rsm[:, 7, :], rsm[:, 6, :]))
            link(tt(rsm[:, 8, :], rsm[:, 7, :], rsm[:, 4, :], ALU.mult))
            dve.wait_ge(s["count_done"], 1)
            link(vec.tensor_scalar(e32[:, 0, :], bank[5][:, 0:EXPERTS], float(BLK - 1), None, ALU.add))
            link(vec.tensor_copy(i32[:, 0, :], e32[:, 0, :]))
            shift = int(math.log2(BLK))
            link(vec.tensor_scalar(i32[:, 1, :], i32[:, 0, :], shift, shift, ALU.arith_shift_right, ALU.logical_shift_left))
            link(vec.tensor_copy(e32[:, 1, :], i32[:, 1, :]))
            link(vec.tensor_tensor_scan(e32[:, 2, :], one6[:, 0:EXPERTS], e32[:, 1, :], 0.0, ALU.mult, ALU.add))
            link(tt(e32[:, 3, :], e32[:, 2, :], e32[:, 1, :], ALU.subtract))
            pos = rt[:, 4, :, :]
            link(tt(pos, bank[4][:, 0:NT * EXPERTS].rearrange("p (t e) -> p t e", t=NT), e32[:, 3, :].unsqueeze(1).to_broadcast([P, NT, EXPERTS]), ALU.add))
            for j in range(2):
                link(tt(rt[:, 1, :, :], rt[:, 2 + j, :, :], pos, ALU.mult))
                link(vec.tensor_reduce(rsm[:, 10 + j, :], rt[:, 1, :, :], AX.X, ALU.add))
                vec.tensor_copy(dest[:, j, :], rsm[:, 10 + j, :]).then_inc(s["dest_ready"], 1)
            cmp = S[:, 0:3, :].rearrange("p a t -> p (a t)")[:, 0:BLOCKS * EXPERTS].rearrange("p (b e) -> p b e", b=BLOCKS)
            link(tt(cmp, e32[:, 2, :].unsqueeze(1).to_broadcast([P, BLOCKS, EXPERTS]), kc[:, K_BB:K_BB + BLOCKS].unsqueeze(2).to_broadcast([P, BLOCKS, EXPERTS]), ALU.is_le))
            link(vec.tensor_reduce(std[:, 0:BLOCKS], cmp, AX.X, ALU.add))
            link(vec.tensor_scalar(rs[:, 0:BLOCKS], std[:, 0:BLOCKS], float(EXPERTS), None, ALU.is_lt))
            vec.tensor_copy(blkU[:, :], rs[:, 0:BLOCKS])
            link(vec.tensor_scalar(std[:, 0:BLOCKS], std[:, 0:BLOCKS], float(EXPERTS - 1), None, ALU.min))
            vec.tensor_copy(blkE[:, :], std[:, 0:BLOCKS])
            dve.wait_ge(s["src_in"], 16)
            vec.tensor_copy(src_f[:, :], src_i[:, :]).then_inc(s["src_float"], 1)
            dve.wait_ge(s["src_turned"], 1)
            vec.tensor_copy(src_c[:, :], bank[6][:, 0:BLOCKS]).then_inc(s["plan_ready"], 1)

            def expert_dve(b, par, n, level):
                dve.wait_ge(s["xe_turned"], b + 1)
                if level == 2:
                    dve.wait_ge(s["up_e_done"], b - 1)
                vec.tensor_copy(xsT[:, par, 0:4, :], bank[4][:, :].rearrange("p (k c) -> p k c", k=4))
                vec.tensor_copy(xsT[:, par, 4:8, :], bank[5][:, :].rearrange("p (k c) -> p k c", k=4)).then_inc(s["xeT_ready"], 1)

            def expert_out(b, par, n, level):
                dve.wait_ge(s["silu_e"], b + 1)
                dve.wait_ge(s["up_e_done"], b + 1)
                if level:
                    dve.wait_ge(s["actT_turned"], b)
                tt(ea, eg, bank[1][:, :], ALU.mult).then_inc(s["act_e"], 1)

            def expert_copy(b, par, n, level):
                if level == 2:
                    dve.wait_ge(s[f"y_out{par}"], n * 16)
                for c in range(2):
                    dve.wait_ge(s["e_down_done"], b * 2 + (c + 1))
                    vec.tensor_copy(ysb[:, par, c * T:(c + 1) * T], bank[2 + c][:, :]).then_inc(s["y_ready"], 1)

            expert_dve(0, 0, 0, 0)
            for b in range(2):
                expert_dve(b + 1, 1 - b, b, 1 + b)
                expert_out(b, b, 0, b)
                expert_copy(b, b, 0, b)
            with dve.Fori(1, BLOCKS // 2 - 1) as g:
                for par in range(2):
                    b = g * 2 + par
                    expert_dve(b + 1, 1 - par, None, 2)
                    expert_out(b, par, g, 2)
                    expert_copy(b, par, g, 2)
            n = BLOCKS // 2 - 1
            for par in range(2):
                b = 2 * n + par
                if par == 0:
                    expert_dve(b + 1, 1, n, 2)
                expert_out(b, par, n, 2)
                expert_copy(b, par, n, 2)
            dve.wait_ge(s["fw_in"], 16)
            for t in range(NT):
                dve.wait_ge(s[f"y_got{t}"], 32)
                link(stt(xtok[:, t, :], y_got_t[:, 2 * t, :], rsm[:, 7, t:t + 1], xtok[:, t, :], ALU.mult, ALU.add))
                dve.wait_ge(s["x_tok_ready"], 2 * NT)
                vec.memset(small[:, 60:61], 0.0).then_inc(s["y_used"], 1)
                stt(xtok[:, t, :], y_got_t[:, 2 * t + 1, :], rsm[:, 8, t:t + 1], xtok[:, t, :], ALU.mult, ALU.add).then_inc(s["y_used"], 1)
            for t in range(NT):
                dve.wait_ge(s["fin_std"], t + 1)
                link(vec.reciprocal(small[:, 36 + t:37 + t], small[:, 36 + t:37 + t]))
                stt(xtok[:, t, :], xtok[:, t, :], small[:, 36 + t:37 + t], fw, ALU.mult, ALU.mult).then_inc(s["out_ready"], 1)

        @block.gpsimd
        def _(pool):
            pool.wait_ge(s["setup_ready"], 1)
            pool.dma_start(src_dram.rearrange("(p b) o -> p (b o)", p=P), zero[:, :]).then_inc(s["src_zeroed"], 16)
            pool.wait_ge(s["src_zeroed"], 16)
            pool.wait_ge(s["dest_ready"], 2)
            for j in range(2):
                for t in range(NT):
                    pool.indirect_dma_start(src_dram, bass.IndirectOffsetOnAxis(dest[:, j, t:t + 1], 0), tokid[:, t:t + 1], None).then_inc(s["src_scattered"], 16)
            pool.wait_ge(s["plan_ready"], 1)
            pool.wait_ge(s["h_tok_out"], 16 * NT)
            pool.wait_ge(s["x_tok_turned"], 2 * NT)

            for b in range(BLOCKS):
                if b >= 2:
                    pool.wait_ge(s["xe_turned"], b - 1)
                pool.indirect_dma_start(xs[:, b % 2, :], None, h_dram, bass.IndirectOffsetOnAxis(src_c[:, b:b + 1], 0)).then_inc(s[f"xe_in{b % 2}"], 16)
            for par in range(2):
                pool.wait_ge(s[f"y_out{par}"], 16 * (BLOCKS // 2))
            for t in range(NT):
                for j in range(2):
                    pool.indirect_dma_start(y_got_t[:, 2 * t + j, :], None, ys_dram, bass.IndirectOffsetOnAxis(dest[:, j, t:t + 1], 0)).then_inc(s[f"y_got{t}"], 16)


def constants():
    k = np.zeros((P, NK), np.float32)
    p, pos = np.arange(P), np.arange(T, dtype=np.float32)
    for at_c, at_s, at_r, dim in ((K_CA, K_SA, K_RA, HD // 2), (K_CB, K_SB, K_RB, HD)):
        inv = (1.0 / (np.float32(10000.0) ** (np.arange(0, dim, 2, dtype=np.float32) / np.float32(dim)))).astype(np.float32)
        ang = inv[(p % dim) % (dim // 2)][:, None] * pos[None, :]
        k[:, at_c:at_c + T] = np.cos(ang.astype(np.float64))
        k[:, at_s:at_s + T] = np.sin(ang.astype(np.float64))
        for m in range(P):
            low = m % dim < dim // 2
            k[m + dim // 2 if low else m - dim // 2, at_r + m] = -1.0 if low else 1.0
    dist = p[:, None] - np.arange(T)[None, :] + (T - P)
    k[:, K_MA:K_MA + T] = np.where(dist >= 0, 0.0, NEG)
    c = (dist <= 128).astype(int) + (dist % 4 == 0) + (dist % 16 == 0)
    k[:, K_MB:K_MB + T] = np.where((dist >= 0) & (c > 0), np.sqrt(float(HD)) * np.log(np.maximum(c, 1)), NEG)
    k[:, K_ID:K_ID + P] = np.eye(P)
    k[:, K_ON:K_ON + P] = 1.0
    k[:, K_OD:K_OD + P] = 1.0 / D
    k[:, K_OR:K_OR + P] = 1.0 / D_RNN
    k[:, K_BO:K_BO + P] = (p[:, None] // HD == p[None, :] // HD) / float(HD)
    k[:, K_TRI:K_TRI + P] = p[:, None] < p[None, :]
    for h in range(C_HEADS):
        k[h, K_SEL + h * P:K_SEL + (h + 1) * P] = -np.sqrt(float(HD))
    k[:, K_TOK:K_TOK + NT] = p[:, None] + P * np.arange(NT)[None, :]
    k[:, K_EI:K_EI + EXPERTS] = EXPERTS - np.arange(EXPERTS)[None, :]
    k[:, K_BB:K_BB + BLOCKS] = BLK * np.arange(BLOCKS)[None, :]
    return k


def kernel(**inputs):
    import concourse.bacc as bacc
    from concourse.bass_utils import run_bass_kernel_spmd

    arr = {n: np.ascontiguousarray(x) for n, x in inputs.items()}
    give = {n: arr[n] for n in ("x", "w_mod", "w_in", "w_out", "w_up", "w_down", "diff_lambda", "mem_2", "w_in_2",
                                "w_out_2", "xk_w_2", "xv_w_2", "xq_w_2", "xo_w_2", "rnn_wa_2", "rnn_wx_2",
                                "expert_gate_w_2", "expert_up_w_2", "expert_down_w_2", "final_norm_w_2")}
    rows = lambda x: x.reshape(-1, P)
    give["consts"] = constants()
    give["rows_mod"] = np.concatenate([rows(arr["b_mod"]), rows(arr["c"])])
    give["rows_layer"] = np.stack([np.concatenate([
        rows(arr["g_attn"][l]), rows(arr["g_mlp"][l]), rows(arr["conv_w"][l]), rows(arr["conv_b"][l]),
        np.concatenate([arr["subln_g"][l]] * 2)[None]]) for l in range(DEPTH)])
    give["rows_second"] = np.concatenate([rows(arr[n + "_2"]) for n in (
        "ln1_w", "conv_w", "conv_b", "rnn_ba", "rnn_bx", "rnn_lambda", "gn_rnn_w", "gn_att_w", "ln2_w", "mem_norm_w", "ln3_w")] + [rows(arr["g_final"])])
    give["forget_bias_t"] = np.ascontiguousarray(arr["forget_bias"].T)
    clip = (arr["rel_bias_2"].shape[-1] - 1) // 2
    give["bias_rows"] = np.ascontiguousarray(
        arr["rel_bias_2"][0][:, np.clip(T - P + np.arange(P)[:, None] - np.arange(T)[None, :], -clip, clip) + clip])
    give["router_w"] = np.concatenate([arr["router_group_w_2"][0], arr["router_expert_w_2"][0].transpose(1, 0, 2).reshape(D, EXPERTS)], axis=1)
    give["router_b"] = np.concatenate([arr["router_group_b_2"][0], arr["router_expert_b_2"][0].reshape(-1)])[None]

    nc = bacc.Bacc("TRN2", target_bir_lowering=False, num_devices=1)
    a, send = {}, {}
    for n, x in give.items():
        send["in_" + n] = x
        a[n] = nc.dram_tensor("in_" + n, x.shape, F32, kind="ExternalInput").ap()
    a["out"] = nc.dram_tensor("out", (1, T, D), F32, kind="ExternalOutput").ap()
    a["h_scratch"] = nc.dram_tensor("h_scratch", (T, D), F32, kind="Internal").ap()
    a["y_scratch"] = nc.dram_tensor("y_scratch", (ROWS, D), F32, kind="Internal").ap()
    a["src_scratch"] = nc.dram_tensor("src_scratch", (ROWS, 1), I32, kind="Internal").ap()
    build(nc, a)
    return run_bass_kernel_spmd(nc, [send], core_ids=[0]).results[0]["out"]
```

```python
import math
from contextlib import ExitStack

import numpy as np

import concourse.bass as bass
from concourse import mybir

P = 128
T = 512
NT = T // P
D = 1024
KD = D // P
DEPTH = 2
HD = 64
A_HEADS, B_HEADS, C_HEADS = 4, 6, 6
HEADS = A_HEADS + B_HEADS + C_HEADS
PAIRS = HEADS // 2
D_FF = 2816
FT = D_FF // P
FH = FT // 2
IN_COLS = 3 * D + C_HEADS
QUARTER = 256
RING = 5
NEG = -1.0e30
NORM_EPS, SUBLN_EPS, EPS2 = 1e-6, 1e-5, 1e-6
D_RNN = 512
CT = D_RNN // P
W_CONV2 = 4
HEADS2 = 8
XHEADS, XDIM = 4, 256
NMEM = 256
GROUPS, PER_GROUP = 4, 8
EXPERTS = GROUPS * PER_GROUP
D_EXP = 512
NR = GROUPS + EXPERTS
BLK = 128
BLOCKS = 40
ROWS = BLOCKS * BLK

IN_SLOTS, OUT_SLOTS, UP_SLOTS, DOWN_SLOTS = 12, 4, FH, (FH + 1) // 2
SLOTS = IN_SLOTS + OUT_SLOTS + 2 * (UP_SLOTS + DOWN_SLOTS)
assert SLOTS == 50 and SLOTS % RING == 0
HALVES = [2] * (IN_SLOTS + OUT_SLOTS) + ([2] * (UP_SLOTS + DOWN_SLOTS - 1) + [0]) * 2
CUM = [sum(HALVES[:i]) for i in range(SLOTS + 1)]
TILES = CUM[SLOTS]
IN2, OUT2 = 10, 4
SLOTS2 = IN2 + OUT2 + 16
MOD_CHUNKS = 6 * D // QUARTER
MOD_FIRST = 2 * D // QUARTER
MOD_PAIRS = (MOD_CHUNKS - MOD_FIRST) // 2
NEXT_PAIRS = MOD_FIRST // 2

QK_OF = {**{a: a for a in range(4)}, **{a: a - 2 for a in range(6, 12)}, **{a: a - 5 for a in range(15, 21)}}
V_OF = {4: 0, 5: 1, 12: 2, 13: 3, 14: 4, 21: 5, 22: 6, 23: 7}
FZ_AT = 13
ROPE = [0, 1, 2, 3, 6, 7, 8, 9, 10, 11]
QT = {"A": 0, "B": 4, "C": 10}
KT = {"A": 2, "B": 7, "C": 13}

C_GA, C_GM, C_CW, C_CB, C_SUB, C_LAM, C_MOD = 0, KD, 2 * KD, 2 * KD + 3 * FT, 2 * KD + 4 * FT, 105, 128
NPRM = 2 * KD + 4 * FT + 1
NCOL = C_MOD + 6 * KD
SH1, SC1, GT1, SH2, SC2, GT2 = (C_MOD + KD * i for i in range(6))
E_LN1, E_CW, E_CB, E_BA, E_BX, E_LAM, E_GR, E_GA, E_LN2, E_MEM, E_LN3, E_FIN = 0, 8, 24, 28, 32, 36, 40, 44, 48, 56, 64, 72
NPRM2 = 80

K_CA, K_SA, K_CB, K_SB, K_MA, K_MB = (i * T for i in range(6))
K_ID, K_ON, K_OD, K_OR, K_BO, K_RA, K_RB, K_TRI = (6 * T + P * i for i in range(8))
K_SEL = K_TRI + P
K_TOK = K_SEL + C_HEADS * P
K_EI = K_TOK + NT
K_BB = K_EI + EXPERTS
NK = K_BB + BLOCKS

ATANH = [1 / 15, 1 / 13, 1 / 11, 1 / 9, 1 / 7, 1 / 5, 1 / 3]
N_LOGSIG = 14

ALU = mybir.AluOpType
ACT = mybir.ActivationFunctionType
AX = mybir.AxisListType
F32 = mybir.dt.float32
F32R = mybir.dt.float32r
I32 = mybir.dt.int32


def jobs_of_layer():
    out = []
    for kind, n, first in (("A", A_HEADS, 0), ("B", B_HEADS, A_HEADS), ("C", C_HEADS, A_HEADS + B_HEADS)):
        out += [(kind, h, first + h, qb) for h in range(n) for qb in range(NT)]
    return out


JOBS = jobs_of_layer()
MAPS = [2 if j[0] == "A" else 1 for j in JOBS]
UNIT0 = [sum(MAPS[:i]) for i in range(len(JOBS) + 1)]
UNITS = UNIT0[-1]
JOBS2 = [("D", h, h, qb) for h in range(HEADS2) for qb in range(NT)]
UNIT02 = list(range(len(JOBS2) + 1))
NS = 4
LAG = 3
CH_NORM, CH_ROPE, CH_MLP = 1, 2, 2
MLP_SLOTS = 2 * (UP_SLOTS + DOWN_SLOTS)
PIECE = KD * QUARTER // 2
CH_ATT = UNITS + sum(1 if m == 1 else 4 for m in MAPS)
CH_LAYER = 4 + 2 * CH_NORM + CH_ROPE * len(ROPE) + N_LOGSIG + CH_ATT + 2 + CH_MLP * FT


def build(nc, a):
    with ExitStack() as ctx:
        def sb(name, shape, dt=F32):
            return ctx.enter_context(nc.sbuf_tensor(name, shape, dt))

        def sem(name):
            return ctx.enter_context(nc.semaphore(name))

        shared = {"hT": [P, KD, T], "arena": [P, 26624], "S": [P, NS, T], "tmp": [P, 6 * T]}
        with ExitStack() as twins:
            hT_r, arena_r, S_r, tmp_r = [twins.enter_context(nc.sbuf_tensor(n + "_r", shape, F32R)) for n, shape in shared.items()]
        hT, arena, S, tmp = [sb(n, shape) for n, shape in shared.items()]
        xT = sb("xT", [P, KD, T])
        wring = arena[:, 0:10240].rearrange("p (r k n) -> p r k n", r=RING, k=KD)
        wdown = arena[:, 0:10240].rearrange("p (r k n) -> p r k n", r=RING, k=2)
        big = arena[:, 10240:22528]
        qk = big[:, 0:16 * T].rearrange("p (i t) -> p i t", i=16)
        v = big[:, 16 * T:24 * T].rearrange("p (t c) -> p t c", t=NT)
        gated_full = big[:, FH * T:2 * FH * T].rearrange("p (i t) -> p i t", i=FH)
        gated_hi = arena_r[:, 10240:10240 + FH * T].rearrange("p (i t) -> p i t", i=FH)
        gated_lo = arena_r[:, 10240 + FH * T:10240 + 2 * FH * T].rearrange("p (i t) -> p i t", i=FH)
        h_lo = arena_r[:, 22528:26624].rearrange("p (k t) -> p k t", k=KD)
        PT = arena[:, 22528:26624].rearrange("p (b k t) -> p b k t", b=2, k=NT)
        mod_w = arena[:, 22528:26624].rearrange("p (b k n) -> p b k n", b=2, k=KD)
        kc = sb("kc", [P, NK])
        ident, ones, onesD = kc[:, K_ID:K_ID + P], kc[:, K_ON:K_ON + P], kc[:, K_OD:K_OD + P]
        onesR, blk64 = kc[:, K_OR:K_OR + P], kc[:, K_BO:K_BO + P]
        toep = sb("toep", [P, 2, T])
        modacc = toep[:, :, :].rearrange("p a (b c) -> p (a b) c", c=QUARTER)
        sq = tmp[:, 0:2 * T].rearrange("p (b t) -> p b t", b=2)
        hn = tmp[:, 2 * T:4 * T].rearrange("p (b t) -> p b t", b=2)
        raw, t1 = sq, hn
        rot = tmp[:, 4 * T:6 * T].rearrange("p (b t) -> p b t", b=2)
        gpad = sb("gpad", [P, 2, T + 4])
        y = sq
        sg = hn
        w_hi = [[S_r[:, 2 * i:2 * i + 2, :].rearrange("p a t -> p (a t)") for i in range(2)],
                [tmp_r[:, 4 * T:6 * T], arena_r[:, 10240 + 2 * FH * T:10240 + 2 * FH * T + PIECE]]]
        std = sb("std", [P, T])
        rs = sb("rs", [P, T])
        pcall = sb("pcall", [P, DEPTH, NCOL])
        pc = sb("pc", [P, NCOL])
        pc2 = sb("pc2", [P, NPRM2 + 16])
        wfz = sb("wfz", [P, KD, C_HEADS])
        fb = sb("fb", [C_HEADS, DEPTH])
        z6 = S[0:C_HEADS, :, :]
        F6 = sb("F6", [C_HEADS, T])
        one6 = sb("one6", [P, T])
        lamp = sb("lamp", [P, DEPTH, 4, 32])
        small = sb("small", [P, 64])
        mx = sb("mx", [P, 3, 8])
        epsc = sb("epsc", [P, 3])
        wgate = sb("wgate", [P, 2, CT, P])
        wrt = sb("wrt", [P, KD, NR])
        rb = sb("rb", [P, NR])
        rt = sb("rt", [P, 6, NT, EXPERTS])
        rlog = sb("rlog", [P, NT, NR])
        rg4 = sb("rg4", [P, 3, NT, GROUPS])
        rsm = sb("rsm", [P, 12, NT])
        e32 = sb("e32", [P, 6, EXPERTS])
        i32 = sb("i32", [P, 2, EXPERTS], I32)
        dest = sb("dest", [P, 2, NT], I32)
        tokid = sb("tokid", [P, NT], I32)
        src_i = sb("src_i", [BLOCKS, BLK], I32)
        src_f = sb("src_f", [BLOCKS, BLK])
        src_c = sb("src_c", [P, BLOCKS], I32)
        blkE = sb("blkE", [P, BLOCKS], I32)
        blkU = sb("blkU", [P, BLOCKS], I32)
        zero = sb("zero", [P, BLOCKS], I32)
        bank = [ctx.enter_context(nc.psum_tensor(f"bank{i}", [P, 512], F32)) for i in range(8)]
        mem_tok = arena[:, 24576:26624].rearrange("p (m c) -> p m c", m=2)
        memT = kc[:, 0:KD * NMEM].rearrange("p (k m) -> p k m", k=KD)
        xr = arena[:, 22528:22528 + CT * (T + 4)].rearrange("p (c t) -> p c t", c=CT)
        xc = qk[:, 0:CT, :]
        r_gate, i_gate, a_rec, u_tmp = hn[:, 0, :], hn[:, 1, :], rot[:, 0, :], rot[:, 1, :]
        h_rec, g_rec = gpad[:, 0, 0:T], gpad[:, 1, 0:T]
        xq = qk[:, 0:8, :]
        xk = big[:, 8 * T:12 * T].rearrange("p (k m) -> p k m", k=KD)
        xv = big[:, 12 * T:16 * T].rearrange("p (m c) -> p m c", m=2)
        ering = arena[:, 0:24576].rearrange("p (r c) -> p r c", r=6)
        xs = xT[:, 0:4, :].rearrange("p (b k) t -> p b (k t)", b=2)
        xsT = xT[:, 4:8, :].rearrange("p (b k) (j c) -> p b (k j) c", b=2, c=P)
        ysb = tmp[:, 0:4 * T].rearrange("p (b c) -> p b c", b=2)
        eg, ea, eaT = S[:, 0, :], S[:, 1, :], S[:, 2, :].rearrange("p (k c) -> p k c", k=4)
        y_got_t = ering[:, 0:2, :].rearrange("p r (i c) -> p (r i) c", c=D)
        fw = kc[:, 0:D]
        xtok = hT[:, :, :].rearrange("p (t a) c -> p t (a c)", t=NT)

        names = """consts_in x_in rows_in lam_in w6_in fb_in mod_in0 mod_in1 mod_in2 mod_in3 mod_in4
            w_in0 w_in1 w_in2 w_in3 w_in4 rows_turned cols_copied silu_c lam_exp lam2_abs lam2_exp mod_used
            mod_step next_added mod_next0 mod_next1 mod_turned x_turned x_updated table_ready setup_ready sq_ready sq_used std_ready hn_ready h_ready
            tiles_done down_done acc_copied rot_done rope_done fz_done z_ready z_abs z_exp decay_ready chain s_done
            max_ready exp_done p_ready t_done pt_ready pv_done o_copied sub_sq sub_sum sub_std sub_done
            hi_ready lo_ready h_lo_ready gated_hi gated_lo_ready gpad_ready conv_done silu_done act_ready toep_in0 toep_in1 mem_in mem_sq mem_std mem_scaled
            mem_turned mem_ready conv2_ready gate_in gate_done gates_ready rec_act rec_u rec_ready router_in
            h_tok_turned h_tok_ready h_tok_out x_tok_turned x_tok_ready logits_done group_shifted second_shifted
            sel_exp sel_ready count_done dest_ready src_zeroed src_scattered src_in src_float src_turned
            plan_ready xe_in0 xe_in1 xe_turned xeT_ready w_e0 w_e1 w_e2 w_e3 w_e4 w_e5 gate_e_done
            up_e_done silu_e act_e actT_turned actT_ready e_down_done y_ready y_out0 y_out1 y_got0 y_got1 y_got2
            y_got3 y_used fin_sq fin_std fw_in out_ready out_sent"""
        s = {n: sem(n) for n in names.split()}

        h_dram, ys_dram, src_dram = a["h_scratch"], a["y_scratch"], a["src_scratch"]

        def sub_tmp(t):
            return gpad[:, t, 2:T + 2]

        def sub_dev(t):
            return (std, rs)[t][:, :]

        def probs(u):
            return S[:, u % NS, :] if u % (2 * NS) < NS else tmp[:, (u % NS) * T:(u % NS + 1) * T]

        def w_wait(eng, l, i):
            per = SLOTS // RING
            eng.wait_ge(s[f"w_in{i % RING}"], l * (32 * per) + 32 * (i // RING + 1))

        def slot_read(eng, l, i):
            if HALVES[i]:
                eng.wait_ge(s["tiles_done"], tiles(l, CUM[i + 1]))
            else:
                eng.wait_ge(s["down_done"], l * 2 * KD + (2 * KD + (KD if i < SLOTS - 1 else 2 * KD)))

        def w_slot(memory, i, piece):
            at = (i % RING) * 2 * PIECE + piece * PIECE
            return memory[:, at:at + PIECE]

        def n_pieces(i):
            return 1 if HALVES[i] == 0 else 2

        def pieces(l, i):
            first = IN_SLOTS + OUT_SLOTS
            return l * sum(map(n_pieces, range(first, SLOTS))) + sum(map(n_pieces, range(first, i)))

        def next_layer(l):
            return nc.s_assert_within(l + 1, 1, DEPTH - 1, skip_runtime_bounds_check_because="the branch is taken for l < DEPTH - 1 only")

        def tiles(l, n):
            return l * TILES + TILES + n

        block = ctx.enter_context(nc.Block())

        @block.sync
        def _(sp):
            sp.dma_start(kc[:, :], a["consts"]).then_inc(s["consts_in"], 16)
            sp.dma_start(S[0:104, 0, 0:P], a["rows_mod"]).then_inc(s["rows_in"], 16)
            for l in range(DEPTH):
                sp.dma_start(S[0:NPRM, 1 + l, 0:P], a["rows_layer"][l]).then_inc(s["rows_in"], 16)
            sp.dma_start(S[0:NPRM2, 3, 0:P], a["rows_second"]).then_inc(s["rows_in"], 16)
            sp.dma_start(xtok, a["x"].rearrange("b (t p) d -> p (b t) d", p=P)).then_inc(s["x_in"], 16)
            sp.dma_start(lamp[:, :, :, :], bass.AP(a["diff_lambda"].tensor, 0, [[0, P], [P, DEPTH], [32, 4], [1, 32]])).then_inc(s["lam_in"], 16)
            sp.dma_start(fb[:, :], a["forget_bias_t"]).then_inc(s["fb_in"], 16)

            for c in range(MOD_FIRST):
                if c >= RING:
                    sp.wait_ge(s["mod_used"], c - RING + 1)
                sp.dma_start(wring[:, c % RING, :, :], a["w_mod"][0].rearrange("(k p) n -> p k n", p=P)[:, :, c * QUARTER:(c + 1) * QUARTER]).then_inc(s[f"mod_in{c % RING}"], 16)
            sp.wait_ge(s["mod_used"], MOD_FIRST)

            def load_mod(l, of, q, n):
                if q >= 2:
                    sp.wait_ge(s["mod_used"], l * MOD_CHUNKS + (MOD_FIRST + q - 1))
                w = a["w_mod"][bass.ds(of, 1)].rearrange("o (k p) n -> p (o k) n", p=P)
                sp.dma_start(mod_w[:, q % 2, :, :], w[:, :, n * QUARTER:(n + 1) * QUARTER]).then_inc(s[f"mod_next{q % 2}"], 16)

            def load_pair(l, pair):
                for q in (2 * pair, 2 * pair + 1):
                    if pair < MOD_PAIRS:
                        load_mod(l, l, q, MOD_FIRST + q)
                    else:
                        with sp.If(l < DEPTH - 1):
                            load_mod(l, next_layer(l), q, q - 2 * MOD_PAIRS)

            def slot_free(l, i):
                if i >= RING:
                    j, at = i - RING, l
                    base = lambda per, c: l * per + per + c
                else:
                    j = i - RING + SLOTS
                    base = lambda per, c: l * per + c
                if HALVES[j]:
                    sp.wait_ge(s["tiles_done"], base(TILES, CUM[j + 1]))
                else:
                    sp.wait_ge(s["down_done"], base(2 * KD, KD if j < SLOTS - 1 else 2 * KD))

            def load(i, dst, src):
                n, w = dst.shape[1:]
                for h in range(2):
                    at = (slice(0, P), slice(h * n // 2, (h + 1) * n // 2)) if n > 1 else (slice(0, P), slice(0, 1), slice(h * w // 2, (h + 1) * w // 2))
                    sp.dma_start(dst[at], src[at]).then_inc(s[f"w_in{i % RING}"], 16)

            def load_up(i, w_up, f):
                for h in range(2):
                    c = h * D_FF + f * P
                    sp.dma_start(wring[:, i % RING, :, h * P:(h + 1) * P], w_up[:, :, c:c + P]).then_inc(s[f"w_in{i % RING}"], 16)

            with sp.Fori(0, DEPTH) as l:
                w_in = a["w_in"][bass.ds(l, 1)].rearrange("o (k p) n -> p (o k) n", p=P)
                w_out = a["w_out"][bass.ds(l, 1)].rearrange("o (k p) n -> p (o k) n", p=P)
                w_up = a["w_up"][bass.ds(l, 1)].rearrange("o (k p) n -> p (o k) n", p=P)
                w_down = a["w_down"][bass.ds(l, 1)].rearrange("o (f p) n -> p (o f) n", p=P)
                i = 0
                for c in range(IN_SLOTS):
                    slot_free(l, i)
                    load(i, wring[:, i % RING, :, :], w_in[:, :, c * QUARTER:(c + 1) * QUARTER])
                    if c == 0 or c >= 5:
                        load_pair(l, max(0, c - 4))
                    if c == 1:
                        sp.wait_ge(s["fz_done"], l + 1)
                        sp.dma_start(wfz[:, :, :], w_in[:, :, 3 * D:IN_COLS]).then_inc(s["w6_in"], 16)
                    i += 1
                for c in range(OUT_SLOTS):
                    slot_free(l, i)
                    load(i, wring[:, i % RING, :, :], w_out[:, :, c * QUARTER:(c + 1) * QUARTER])
                    load_pair(l, c + 8)
                    i += 1
                for hh in range(2):
                    for f in range(hh * FH, hh * FH + FH):
                        slot_free(l, i)
                        load_up(i, w_up, f)
                        i += 1
                    for c in range(DOWN_SLOTS):
                        n = min(2, FH - 2 * c)
                        slot_free(l, i)
                        load(i, wdown[:, i % RING, 0:n, :], w_down[:, hh * FH + 2 * c:hh * FH + 2 * c + n, :])
                        i += 1

            sp.wait_ge(s["tiles_done"], tiles(DEPTH - 1, CUM[SLOTS - DOWN_SLOTS]))
            sp.dma_start(mem_tok, a["mem_2"].rearrange("b (m p) d -> p (b m) d", p=P)).then_inc(s["mem_in"], 16)
            i = 0
            for name, n in (("w_in_2", IN2), ("w_out_2", OUT2), ("xk_w_2", 4), ("xv_w_2", 4), ("xq_w_2", 4), ("xo_w_2", 4)):
                w = a[name][0].rearrange("(k p) n -> p k n", p=P)
                for c in range(n):
                    if i < RING:
                        slot_free(DEPTH, i)
                    else:
                        sp.wait_ge(s["tiles_done"], tiles(DEPTH, 2 * (i - RING) + 2))
                    load(i, wring[:, i % RING, :, :], w[:, :, c * QUARTER:(c + 1) * QUARTER])
                    i += 1

            for t in range(NT):
                sp.wait_ge(s["h_tok_ready"], 2 * t + 2)
                sp.dma_start(h_dram[t * P:(t + 1) * P, :], big[:, t * D:(t + 1) * D]).then_inc(s["h_tok_out"], 16)
            sp.wait_ge(s["src_scattered"], 16 * 2 * NT)
            sp.dma_start(src_i[:, :], src_dram.rearrange("(b p) o -> b (p o)", p=BLK)).then_inc(s["src_in"], 16)
            sp.wait_ge(s["h_tok_out"], 16 * NT)
            sp.wait_ge(s["plan_ready"], 1)
            sp.dma_start(fw, bass.AP(a["final_norm_w_2"].tensor, 0, [[0, P], [1, D]])).then_inc(s["fw_in"], 16)
            ew = [a["expert_gate_w_2"][0], a["expert_up_w_2"][0], a["expert_down_w_2"][0]]

            def load_expert(b, par, parts, again):
                e = sp.value_load(blkE[0:1, bass.ds(b, 1)], min_val=0, max_val=EXPERTS - 1)
                has_rows = sp.value_load(blkU[0:1, bass.ds(b, 1)], min_val=0, max_val=1)
                with sp.If(has_rows > 0):
                    for m in parts:
                        if again:
                            sp.wait_ge(s[("gate_e_done", "up_e_done", "e_down_done")[m]], (b - 1) if m < 2 else (b - 1) * 2)
                        w = ew[m][bass.ds(e, 1)].rearrange("e (k p) n -> p (e k) n", p=P)
                        dst = ering[:, 3 * par + m, :].rearrange("p (k n) -> p k n", k=w.shape[1])
                        sp.dma_start(dst, w).then_inc(s[f"w_e{3 * par + m}"], 16)

            for b in range(4):
                load_expert(b, b % 2, (0, 1), b >= 2)
                if b >= 1:
                    load_expert(b - 1, 1 - b % 2, (2,), b >= 3)
            with sp.Fori(2, BLOCKS // 2) as g:
                for par in range(2):
                    load_expert(g * 2 + par, par, (0, 1), True)
                    load_expert(g * 2 + (par - 1), 1 - par, (2,), True)
            load_expert(BLOCKS - 1, 1, (2,), True)
            for t in range(NT):
                sp.wait_ge(s["out_ready"], t + 1)
                sp.dma_start(a["out"].rearrange("b (t p) d -> p (b t) d", p=P)[:, t, :], xtok[:, t, :]).then_inc(s["out_sent"], 16)
            sp.wait_ge(s["out_sent"], 16 * NT)

        @block.tensor
        def _(pe):
            mm = nc.tensor.matmul

            pe.sem_inc(s["tiles_done"], TILES)
            pe.sem_inc(s["down_done"], 2 * KD)
            pe.sem_inc(s["fz_done"], 1)
            pe.wait_ge(s["consts_in"], 16)
            pe.wait_ge(s["rows_in"], 16 * 4)
            for i, n in enumerate((104, NPRM, NPRM, NPRM2)):
                nc.tensor.transpose(bank[i][:, 0:n], S[0:n, i, 0:P], ident[0:n, 0:n]).then_inc(s["rows_turned"], 1)
            pe.wait_ge(s["x_in"], 16)
            for k in range(KD):
                b = bank[4 + k % 2]
                if k >= 2:
                    pe.wait_ge(s["x_updated"], k - 1)
                for t in range(NT):
                    ins = nc.tensor.transpose(b[:, t * P:(t + 1) * P], xtok[:, t, k * P:(k + 1) * P], ident)
                ins.then_inc(s["x_turned"], 1)

            def mod_sum(used, a4, n, b=6):
                pe.wait_ge(s["mod_used"], used)
                for j in range(2):
                    ins = mm(bank[b][:, 2 * n + j:2 * n + j + 1], modacc[:, a4, j * P:(j + 1) * P], ones[:, 0:1], start=True, stop=True)
                ins.then_inc(s["mod_turned"], 1)

            for c in range(MOD_FIRST):
                mod_sum(c + 1, c % 4, c)

            def pair_sum(l, pair):
                for q in (2 * pair, 2 * pair + 1):
                    if pair < MOD_PAIRS:
                        mod_sum(l * MOD_CHUNKS + (MOD_FIRST + q + 1), q % 4, MOD_FIRST + q)
                    else:
                        with pe.If(l < DEPTH - 1):
                            mod_sum(l * MOD_CHUNKS + (MOD_FIRST + q + 1), q % 4, q - 2 * MOD_PAIRS, 5)

            def norm(n):
                for k in range(KD):
                    pe.wait_ge(s["sq_ready"], n * KD + k + 1)
                    mm(bank[7][:, :], onesD, sq[:, k % 2, :], start=k == 0, stop=k == KD - 1).then_inc(s["sq_used"], 1)

            def feature_half(b, w, j, src, width=T, before=None):
                for k in range(KD):
                    if before is not None:
                        before(k)
                    ins = mm(b[:, 0:width], w[:, k, j * P:(j + 1) * P], src[:, k, 0:width], start=k == 0, stop=k == KD - 1)
                return ins

            def token_half(b, w, j, src, nt=NT):
                for t in range(nt):
                    for k in range(KD):
                        ins = mm(b[:, t * P:(t + 1) * P], src[:, k, t * P:(t + 1) * P], w[:, k, j * P:(j + 1) * P],
                                 start=k == 0, stop=k == KD - 1)
                return ins

            def split_mm(b, i, piece, at, hi, lo, start, stop):
                w_h = w_hi[i % 2][piece][:, at:at + P]
                mm(b[:, :], w_h, hi, start=start, stop=False)
                mm(b[:, :], w_h, lo, start=False, stop=False)
                return mm(b[:, :], w_slot(arena_r, i, piece)[:, at:at + P], hi, start=False, stop=stop)

            def attention(jobs, unit0, U, J, G, Q, scores):
                n = len(jobs)
                for j in range(n + LAG + 1):
                    if j < n:
                        for m in range(unit0[j + 1] - unit0[j]):
                            u = unit0[j] + m
                            if u >= NS:
                                pe.wait_ge(s["max_ready"], U + (u - NS + 1))
                            scores(jobs[j], m, bank[u % NS]).then_inc(s["s_done"], 1)
                    if LAG <= j < n + LAG:
                        jj = j - LAG
                        u, qb = unit0[jj + 1] - 1, jobs[jj][3]
                        pe.wait_ge(s["p_ready"], J + (jj + 1))
                        if jj >= 2:
                            pe.wait_ge(s["pt_ready"], J + (jj - 1))
                        for kb in range(qb + 1):
                            ins = nc.tensor.transpose(bank[4 + jj % 2][:, kb * P:(kb + 1) * P], probs(u)[:, kb * P:(kb + 1) * P], ident)
                        ins.then_inc(s["t_done"], 1)
                    if j >= LAG + 1 and jobs[j - LAG - 1][3] == NT - 1:
                        g = jobs[j - LAG - 1][2]
                        pe.wait_ge(s["pt_ready"], J + (j - LAG))
                        if g % 2 == 0 and g >= 4:
                            pe.wait_ge(s["o_copied"], Q + (g // 2 - 1))
                        ob = bank[6 + g // 2 % 2]
                        for kb in range(NT):
                            ins = mm(ob[HD * (g % 2):HD * (g % 2) + HD, kb * P:T], v[:, kb, g * HD:(g + 1) * HD],
                                     PT[:, g % 2, kb, kb * P:T], start=kb == 0, stop=kb == NT - 1)
                        ins.then_inc(s["pv_done"], 1)

            def layer_scores(job, m, b):
                kind, h, g, qb = job
                w = (qb + 1) * P
                p0, K = (HD * (h % 2) + 32 * m, 32) if kind == "A" else (HD * (h % 2), HD)
                ins = mm(b[:, 0:w], qk[p0:p0 + K, QT[kind] + h // 2, qb * P:(qb + 1) * P],
                         qk[p0:p0 + K, KT[kind] + h // 2, 0:w], start=True, stop=kind != "C")
                if kind == "C":
                    ins = mm(b[:, 0:w], kc[0:C_HEADS, K_SEL + h * P:K_SEL + (h + 1) * P], F6[:, 0:w], start=False, stop=True)
                return ins

            with pe.Fori(0, DEPTH) as l:
                norm(2 * l)
                for h in range(2 * IN_SLOTS + 1):
                    if h < 2 * IN_SLOTS:
                        i, j = divmod(h, 2)
                        if j == 0:
                            w_wait(pe, l, i)
                        if h >= 2:
                            pe.wait_ge(s["acc_copied"], l * 24 + (h - 1))
                        if h == 0:
                            ins = feature_half(bank[0], wring[:, i % RING, :, :], j, hT, before=lambda k: pe.wait_ge(s["h_ready"], 2 * l * KD + (k + 1)))
                        else:
                            half = feature_half if h in QK_OF else token_half
                            ins = half(bank[h % 2], wring[:, i % RING, :, :], j, hT)
                        ins.then_inc(s["tiles_done"], 1)
                        if h % 2 and h >= 3:
                            pair_sum(l, h // 2 - 1)
                    if h - 1 in ROPE:
                        r = ROPE.index(h - 1)
                        pe.wait_ge(s["acc_copied"], l * 24 + h)
                        if r >= 2:
                            pe.wait_ge(s["rope_done"], l * len(ROPE) + (r - 1))
                        R = K_RA if h - 1 < 4 else K_RB
                        mm(bank[2 + r % 2][:, :], kc[:, R:R + P], raw[:, r % 2, :], start=True, stop=True).then_inc(s["rot_done"], 1)
                    if h == FZ_AT:
                        pe.wait_ge(s["w6_in"], l * 16 + 16)
                        for k in range(KD):
                            ins = mm(bank[4][0:C_HEADS, :], wfz[:, k, :], hT[:, k, :], start=k == 0, stop=k == KD - 1)
                        ins.then_inc(s["fz_done"], 1)
                pair_sum(l, MOD_PAIRS + NEXT_PAIRS - 1)
                pe.wait_ge(s["rope_done"], l * len(ROPE) + len(ROPE))
                pe.wait_ge(s["acc_copied"], l * 24 + 24)
                pe.wait_ge(s["decay_ready"], l + 1)
                attention(JOBS, UNIT0, l * UNITS, l * len(JOBS), l * HEADS, l * PAIRS, layer_scores)
                for t in range(2):
                    pe.wait_ge(s["sub_sq"], l * 2 + (t + 1))
                    mm(bank[2 + t][:, :], blk64, sub_tmp(t), start=True, stop=True).then_inc(s["sub_sum"], 1)
                pe.wait_ge(s["o_copied"], l * PAIRS + PAIRS)
                pe.wait_ge(s["sub_done"], l * 2 + 2)
                for d in range(KD):
                    i, j = IN_SLOTS + d // 2, d % 2
                    if j == 0:
                        w_wait(pe, l, i)
                    if d >= 2:
                        pe.wait_ge(s["x_updated"], l * 24 + (8 + d - 1))
                    feature_half(bank[d % 2], wring[:, i % RING, :, :], j, hT).then_inc(s["tiles_done"], 1)
                norm(2 * l + 1)
                i = IN_SLOTS + OUT_SLOTS
                for hh in range(2):
                    for f in range(hh * FH, hh * FH + FH):
                        pe.wait_ge(s["lo_ready"], pieces(l, i + 1))
                        if f % FH < 2:
                            if hh == 1:
                                pe.wait_ge(s["x_updated"], l * 24 + (16 + (4 if f % 2 else 2)))
                        else:
                            pe.wait_ge(s["act_ready"], l * FT + (f - 1))
                        for j in range(2):
                            for k in range(KD):
                                at = (k % 4) * QUARTER + j * P
                                if f == 0 and j == 0:
                                    pe.wait_ge(s["h_ready"], 2 * l * KD + (KD + k + 1))
                                    pe.wait_ge(s["h_lo_ready"], l * KD + (k + 1))
                                ins = split_mm(bank[4 * hh + 2 * (f % 2) + j], i, k // 4, at, hT_r[:, k, :], h_lo[:, k, :], k == 0, k == KD - 1)
                            ins.then_inc(s["tiles_done"], 1)
                        i += 1
                    for c in range(DOWN_SLOTS):
                        pe.wait_ge(s["lo_ready"], pieces(l, i + 1))
                        for j in range(min(2, FH - 2 * c)):
                            f = 2 * c + j
                            pe.wait_ge(s["gated_lo_ready"], l * FT + (hh * FH + f + 1))
                            for d in range(KD):
                                if f == 0 and d == 4:
                                    pe.wait_ge(s["act_ready"], l * FT + (hh * FH + FH))
                                ins = split_mm(bank[(d + 4 - 4 * hh) % 8], i, j, d * P, gated_hi[:, f, :], gated_lo[:, f, :], f == 0, f == FH - 1)
                                if f == FH - 1:
                                    ins.then_inc(s["down_done"], 1)
                            if f < FH - 1:
                                ins.then_inc(s["tiles_done"], 1)
                        i += 1

            L = DEPTH
            pe.wait_ge(s["mem_scaled"], 2)
            pe.wait_ge(s["x_updated"], 56)
            for k in range(KD):
                if k >= 2:
                    pe.wait_ge(s["mem_ready"], k - 1)
                for m in range(2):
                    ins = nc.tensor.transpose(bank[k % 2][:, m * P:(m + 1) * P], mem_tok[:, m, k * P:(k + 1) * P], ident)
                ins.then_inc(s["mem_turned"], 1)
            norm(2 * L)
            norm(2 * L + 1)
            pe.wait_ge(s["mem_ready"], KD)
            pe.wait_ge(s["gate_in"], 64)
            for h in range(2 * IN2):
                i, j = divmod(h, 2)
                if j == 0:
                    w_wait(pe, L, i)
                if h >= 2:
                    pe.wait_ge(s["acc_copied"], L * 24 + h - 1)
                if h == 0:
                    ins = feature_half(bank[0], wring[:, i % RING, :, :], j, hT, before=lambda k: pe.wait_ge(s["h_ready"], 4 * KD + k + 1))
                else:
                    half = feature_half if h < 16 else token_half
                    ins = half(bank[h % 2], wring[:, i % RING, :, :], j, hT)
                ins.then_inc(s["tiles_done"], 1)
                if 8 <= h < 12:
                    c = h - 8
                    pe.wait_ge(s["conv2_ready"], c + 1)
                    if c >= 2:
                        pe.wait_ge(s["gates_ready"], 2 * (c - 1))
                    for m in range(2):
                        mm(bank[2 + 2 * (c % 2) + m][:, :], wgate[:, m, c, :], xc[:, c, :], start=True, stop=True).then_inc(s["gate_done"], 1)
            acc2 = L * 24 + 2 * IN2
            pe.wait_ge(s["acc_copied"], acc2)
            pe.wait_ge(s["gates_ready"], 2 * CT)

            def scores2(job, m, b):
                _, h, g, qb = job
                w = (qb + 1) * P
                p0 = HD * (h % 2)
                return mm(b[:, 0:w], qk[p0:p0 + HD, 8 + h // 2, qb * P:(qb + 1) * P], qk[p0:p0 + HD, 12 + h // 2, 0:w], start=True, stop=True)

            attention(JOBS2, UNIT02, L * UNITS, L * len(JOBS), L * HEADS, L * PAIRS, scores2)
            pe.wait_ge(s["o_copied"], L * PAIRS + HEADS2 // 2)
            for grp in range(2):
                if grp:
                    pe.wait_ge(s["std_ready"], 7)
                for k in range(CT):
                    pe.wait_ge(s["sq_ready"], 6 * KD + CT * grp + k + 1)
                    mm(bank[7][:, :], onesR, sq[:, k % 2, :], start=k == 0, stop=k == CT - 1).then_inc(s["sq_used"], 1)
            pe.wait_ge(s["h_ready"], 6 * KD)

            def to_x(i0, first):
                for d in range(KD):
                    i, j = i0 + d // 2, d % 2
                    if j == 0:
                        w_wait(pe, L, i)
                    if d >= 2:
                        pe.wait_ge(s["x_updated"], first + d - 1)
                    feature_half(bank[d % 2], wring[:, i % RING, :, :], j, hT).then_inc(s["tiles_done"], 1)

            to_x(IN2, 64)
            i = IN2 + OUT2
            pe.wait_ge(s["x_updated"], 72)
            for h in range(16):
                if h % 2 == 0:
                    w_wait(pe, L, i + h // 2)
                if h >= 2:
                    pe.wait_ge(s["acc_copied"], acc2 + h - 1)
                w = wring[:, (i + h // 2) % RING, :, :]
                ins = feature_half(bank[h % 2], w, h % 2, memT, NMEM) if h < 8 else token_half(bank[h % 2], w, h % 2, memT, 2)
                ins.then_inc(s["tiles_done"], 1)
            i += 8
            norm(7)
            for h in range(8):
                if h % 2 == 0:
                    w_wait(pe, L, i + h // 2)
                pe.wait_ge(s["acc_copied"], acc2 + 16 + h - 1)
                feature_half(bank[h % 2], wring[:, (i + h // 2) % RING, :, :], h % 2, hT,
                             before=(lambda k: pe.wait_ge(s["h_ready"], 6 * KD + k + 1)) if h == 0 else None).then_inc(s["tiles_done"], 1)
            i += 4
            pe.wait_ge(s["acc_copied"], acc2 + 24)
            U, J = L * UNITS + len(JOBS2), L * len(JOBS) + len(JOBS2)
            n = XHEADS * NT
            for j in range(n + 3):
                if j < n:
                    h, qb = divmod(j, NT)
                    if j >= NS:
                        pe.wait_ge(s["exp_done"], U + j - NS + 1)
                    for kt in range(2):
                        ins = mm(bank[j % NS][:, 0:NMEM], xq[:, 2 * h + kt, qb * P:(qb + 1) * P], xk[:, 2 * h + kt, :], start=kt == 0, stop=kt == 1)
                    ins.then_inc(s["s_done"], 1)
                if 2 <= j < n + 2:
                    jj = j - 2
                    pe.wait_ge(s["p_ready"], J + jj + 1)
                    if jj >= 2:
                        pe.wait_ge(s["pt_ready"], J + jj - 1)
                    for m in range(2):
                        ins = nc.tensor.transpose(bank[4 + jj % 2][:, m * P:(m + 1) * P], S[:, jj % NS, m * P:(m + 1) * P], ident)
                    ins.then_inc(s["t_done"], 1)
                if j >= 3 and (j - 3) % NT == NT - 1:
                    g = (j - 3) // NT
                    pe.wait_ge(s["pt_ready"], J + j - 2)
                    if g >= 1:
                        pe.wait_ge(s["o_copied"], L * PAIRS + HEADS2 // 2 + 2 * g)
                    for dt in range(2):
                        for m in range(2):
                            ins = mm(bank[6 + dt][:, :], xv[:, m, (2 * g + dt) * P:(2 * g + dt + 1) * P], PT[:, g % 2, m, :], start=m == 0, stop=m == 1)
                    ins.then_inc(s["pv_done"], 1)
            pe.wait_ge(s["o_copied"], L * PAIRS + HEADS2 // 2 + 2 * XHEADS)
            to_x(i, 72)
            norm(8)
            pe.wait_ge(s["h_ready"], 8 * KD)
            pe.wait_ge(s["router_in"], 32)
            for t in range(NT):
                for k in range(KD):
                    ins = mm(bank[6][:, t * NR:(t + 1) * NR], hT[:, k, t * P:(t + 1) * P], wrt[:, k, :], start=k == 0, stop=k == KD - 1)
            ins.then_inc(s["logits_done"], 1)
            for n in range(2 * NT):
                t, c = divmod(n, 2)
                if n >= 2:
                    pe.wait_ge(s["h_tok_ready"], n - 1)
                for k in range(4):
                    ins = nc.tensor.transpose(bank[n % 2][:, k * P:(k + 1) * P], hT[:, 4 * c + k, t * P:(t + 1) * P], ident)
                ins.then_inc(s["h_tok_turned"], 1)
            for n in range(2 * NT):
                t, c = divmod(n, 2)
                if n >= 2:
                    pe.wait_ge(s["x_tok_ready"], n - 1)
                else:
                    pe.wait_ge(s["h_tok_ready"], 2 * NT - 1 + n)
                for k in range(4):
                    ins = nc.tensor.transpose(bank[n % 2][:, k * P:(k + 1) * P], xT[:, 4 * c + k, t * P:(t + 1) * P], ident)
                ins.then_inc(s["x_tok_turned"], 1)
            pe.wait_ge(s["sel_ready"], 1)
            for t in range(NT):
                for tt in range(t):
                    mm(bank[4][:, t * EXPERTS:(t + 1) * EXPERTS], ones, rt[:, 5, tt, :], start=tt == 0, stop=False)
                mm(bank[4][:, t * EXPERTS:(t + 1) * EXPERTS], kc[:, K_TRI:K_TRI + P], rt[:, 5, t, :], start=t == 0, stop=True)
            for tt in range(NT):
                ins = mm(bank[5][:, 0:EXPERTS], ones, rt[:, 5, tt, :], start=tt == 0, stop=tt == NT - 1)
            ins.then_inc(s["count_done"], 1)
            pe.wait_ge(s["src_float"], 1)
            nc.tensor.transpose(bank[6][:, 0:BLOCKS], src_f[:, :], ident[0:BLOCKS, 0:BLOCKS]).then_inc(s["src_turned"], 1)
            pe.wait_ge(s["plan_ready"], 1)

            def turn_rows(par, n):
                pe.wait_ge(s[f"xe_in{par}"], n * 16 + 16)
                for k in range(KD):
                    ins = nc.tensor.transpose(bank[4 + k // 4][:, (k % 4) * P:(k % 4 + 1) * P], xs[:, par, k * P:(k + 1) * P], ident)
                ins.then_inc(s["xe_turned"], 1)

            def turn_act(b):
                pe.wait_ge(s["act_e"], b + 1)
                for k in range(4):
                    ins = nc.tensor.transpose(bank[6][:, k * P:(k + 1) * P], ea[:, k * P:(k + 1) * P], ident)
                ins.then_inc(s["actT_turned"], 1)

            def expert_in(b, par, n, m, has_rows):
                done = ("gate_e_done", "up_e_done")[m]
                with pe.If(has_rows > 0):
                    pe.wait_ge(s[f"w_e{3 * par + m}"], n * 16 + 16)
                    w = ering[:, 3 * par + m, :].rearrange("p (k n) -> p k n", k=KD)
                    for k in range(KD):
                        ins = mm(bank[m][:, :], xsT[:, par, k, :], w[:, k, :], start=k == 0, stop=k == KD - 1)
                    ins.then_inc(s[done], 1)
                with pe.Else():
                    pe.sem_inc(s[done], 1)

            def expert_down(b, par, n, first=False):
                has_rows = pe.value_load(blkU[0:1, bass.ds(b, 1)], min_val=0, max_val=1)
                pe.wait_ge(s["actT_ready"], b + 1)
                if not first:
                    pe.wait_ge(s["y_ready"], b * 2)
                with pe.If(has_rows > 0):
                    pe.wait_ge(s[f"w_e{3 * par + 2}"], n * 16 + 16)
                    w = ering[:, 3 * par + 2, :].rearrange("p (k n) -> p k n", k=4)
                    for c in range(2):
                        for k in range(4):
                            ins = mm(bank[2 + c][:, :], eaT[:, k, :], w[:, k, c * T:(c + 1) * T], start=k == 0, stop=k == 3)
                        ins.then_inc(s["e_down_done"], 1)
                with pe.Else():
                    pe.sem_inc(s["e_down_done"], 2)

            def expert_block(b, par, n, nxt=True, level=2):
                has_rows = pe.value_load(blkU[0:1, bass.ds(b, 1)], min_val=0, max_val=1)
                pe.wait_ge(s["xeT_ready"], b + 1)
                if level:
                    pe.wait_ge(s["act_e"], b)
                expert_in(b, par, n, 0, has_rows)
                if level:
                    turn_act(b - 1)
                expert_in(b, par, n, 1, has_rows)
                if nxt:
                    turn_rows(1 - par, n + par)
                if level:
                    expert_down(b - 1, 1 - par, n + (par - 1), level == 1)

            turn_rows(0, 0)
            expert_block(0, 0, 0, level=0)
            expert_block(1, 1, 0, level=1)
            with pe.Fori(1, BLOCKS // 2 - 1) as g:
                for par in range(2):
                    expert_block(g * 2 + par, par, g)
            n = BLOCKS // 2 - 1
            expert_block(2 * n, 0, n)
            expert_block(2 * n + 1, 1, n, nxt=False)
            turn_act(BLOCKS - 1)
            expert_down(BLOCKS - 1, 1, n)

        @block.scalar
        def _(act):
            af = nc.scalar.activation
            act.wait_ge(s["setup_ready"], 1)
            for m, w in enumerate(("rnn_wa_2", "rnn_wx_2")):
                for half in range(2):
                    act.dma_start(wgate[HD * half:HD * half + HD, m, :, HD * half:HD * half + HD],
                                  a[w][0].rearrange("(c two) k n -> k two c n", two=2)[:, half]).then_inc(s["gate_in"], 16)
            act.dma_start(wrt[:, :, :], a["router_w"].rearrange("(k p) n -> p k n", p=P)).then_inc(s["router_in"], 16)
            act.dma_start(rb[:, :], bass.AP(a["router_b"].tensor, 0, [[0, P], [1, NR]])).then_inc(s["router_in"], 16)
            act.wait_ge(s["cols_copied"], 1)
            af(small[:, 0:KD], small[:, 8:8 + KD], ACT.Silu).then_inc(s["silu_c"], 1)
            act.wait_ge(s["cols_copied"], 2)
            af(small[:, 20:24], small[:, 16:20], ACT.Exp).then_inc(s["lam_exp"], 1)
            act.wait_ge(s["lam2_abs"], 1)
            af(small[:, 40:44], small[:, 40:44], ACT.Exp, scale=-1.0).then_inc(s["lam2_exp"], 1)

            def norm(n, before, shift, split=False):
                for k in range(KD):
                    act.wait_ge(s["x_updated"], before + (k + 1))
                    if k >= 2:
                        act.wait_ge(s["sq_used"], n * KD + (k - 1))
                    af(sq[:, k % 2, :], xT[:, k, :], ACT.Square).then_inc(s["sq_ready"], 1)
                act.wait_ge(s["sq_used"], n * KD + KD)
                af(std[:, :], bank[7][:, :], ACT.Sqrt, bias=epsc[:, 0:1]).then_inc(s["std_ready"], 1)
                if shift is not None:
                    for k in range(KD):
                        act.wait_ge(s["hn_ready"], n * KD + (k + 1))
                        af((hT_r if split else hT)[:, k, :], hn[:, k % 2, :], ACT.Identity, bias=pc[:, shift + k:shift + k + 1]).then_inc(s["h_ready"], 1)

            def attention(jobs, unit0, U, J, G, Q, scale_of, out, after=None):
                n = len(jobs)
                for j in range(n + LAG + 2):
                    if j < n:
                        for m in range(unit0[j + 1] - unit0[j]):
                            u = unit0[j] + m
                            act.wait_ge(s["max_ready"], U + (u + 1))
                            w = (jobs[j][3] + 1) * P
                            af(probs(u)[:, 0:w], probs(u)[:, 0:w], ACT.Exp, scale=scale_of(jobs[j]), bias=mx[:, 1, u % 8:u % 8 + 1],
                               accum_out=mx[:, 2, u % 8:u % 8 + 1]).then_inc(s["exp_done"], 1)
                        if after is not None:
                            after(jobs[j])
                    if LAG <= j < n + LAG:
                        jj = j - LAG
                        _, _, g, qb = jobs[jj]
                        act.wait_ge(s["t_done"], J + (jj + 1))
                        if qb == 0 and g >= 2:
                            act.wait_ge(s["pv_done"], G + (g - 1))
                        af(PT[:, g % 2, 0:qb + 1, qb * P:(qb + 1) * P],
                           bank[4 + jj % 2][:, 0:(qb + 1) * P].rearrange("p (k q) -> p k q", q=P), ACT.Copy).then_inc(s["pt_ready"], 1)
                    if j >= LAG + 2 and jobs[j - LAG - 2][3] == NT - 1 and jobs[j - LAG - 2][2] % 2:
                        g = jobs[j - LAG - 2][2]
                        act.wait_ge(s["pv_done"], G + (g + 1))
                        af(out(g // 2), bank[6 + g // 2 % 2][:, :], ACT.Copy).then_inc(s["o_copied"], 1)

            def split_hi(l, n):
                i = IN_SLOTS + OUT_SLOTS + n
                w_wait(act, l, i)
                if n >= 2:
                    slot_read(act, l, i - 2)
                for piece in range(n_pieces(i)):
                    af(w_hi[i % 2][piece], w_slot(arena, i, piece), ACT.Copy).then_inc(s["hi_ready"], 1)

            def gated_split_hi(l, f):
                act.wait_ge(s["act_ready"], l * FT + (f + 1))
                af(gated_hi[:, f % FH, :], gated_full[:, f % FH, :], ACT.Copy).then_inc(s["gated_hi"], 1)

            with act.Fori(0, DEPTH) as l:
                act.wait_ge(s["table_ready"], l + 1)
                norm(2 * l, l * 24, SH1)
                for h in range(2 * IN_SLOTS):
                    act.wait_ge(s["tiles_done"], tiles(l, h + 1))
                    b = bank[h % 2]
                    if h in ROPE:
                        r = ROPE.index(h)
                        if r >= 2:
                            act.wait_ge(s["rope_done"], l * len(ROPE) + (r - 1))
                        af(raw[:, r % 2, :], b[:, :], ACT.Copy).then_inc(s["acc_copied"], 1)
                    elif h in QK_OF:
                        af(qk[:, QK_OF[h], :], b[:, :], ACT.Copy).then_inc(s["acc_copied"], 1)
                    else:
                        c = V_OF[h] * P
                        af(v[:, :, c:c + P], b[:, :].rearrange("p (t c) -> p t c", t=NT), ACT.Copy).then_inc(s["acc_copied"], 1)
                    if h == FZ_AT:
                        act.wait_ge(s["fz_done"], l + 2)
                        act.wait_ge(s["fb_in"], 16)
                        af(z6[:, 0, :], bank[4][0:C_HEADS, :], ACT.Identity, bias=pc[0:C_HEADS, 106:107]).then_inc(s["z_ready"], 1)
                    if h == FZ_AT + 2:
                        act.wait_ge(s["z_abs"], l + 1)
                        af(z6[:, 1, :], z6[:, 1, :], ACT.Exp, scale=-1.0).then_inc(s["z_exp"], 1)
                attention(JOBS, UNIT0, l * UNITS, l * len(JOBS), l * HEADS, l * PAIRS,
                          lambda job: (HD // 2 if job[0] == "A" else HD) ** -0.5, lambda p: hT[:, p, :])
                for t in range(2):
                    act.wait_ge(s["sub_sum"], l * 2 + (t + 1))
                    af(sub_dev(t), bank[2 + t][:, :], ACT.Sqrt, bias=epsc[:, 1:2]).then_inc(s["sub_std"], 1)
                split_hi(l, 0)
                norm(2 * l + 1, l * 24 + 8, SH2, True)
                for n in range(MLP_SLOTS):
                    if n + 1 < MLP_SLOTS:
                        split_hi(l, n + 1)
                    hh, f = divmod(n, UP_SLOTS + DOWN_SLOTS)
                    if f >= UP_SLOTS:
                        continue
                    f += hh * FH
                    if f % FH:
                        gated_split_hi(l, f - 1)
                    act.wait_ge(s["tiles_done"], l * TILES + (TILES + CUM[IN_SLOTS + OUT_SLOTS + n] + 2))
                    if f >= 2:
                        act.wait_ge(s["conv_done"], l * FT + (f - 1))
                    af(gpad[:, f % 2, 2:T + 2], bank[4 * hh + 2 * (f % 2) + 1][:, :], ACT.Copy).then_inc(s["gpad_ready"], 1)
                    act.wait_ge(s["conv_done"], l * FT + (f + 1))
                    if f >= 2:
                        act.wait_ge(s["act_ready"], l * FT + (f - 1))
                    af(sg[:, f % 2, :], y[:, f % 2, :], ACT.Silu).then_inc(s["silu_done"], 1)
                    if f % FH == FH - 1:
                        gated_split_hi(l, f)

            L = DEPTH
            act.wait_ge(s["mem_in"], 16)
            act.wait_ge(s["act_ready"], L * FT)
            for m in range(2):
                if m:
                    act.wait_ge(s["mem_sq"], m)
                af(tmp[:, 2 * T:4 * T], mem_tok[:, m, :], ACT.Square, accum_out=small[:, 24 + m:25 + m]).then_inc(s["mem_sq"], 1)
            act.wait_ge(s["mem_sq"], 2)
            af(small[:, 26:28], small[:, 24:26], ACT.Sqrt, scale=1.0 / D, bias=epsc[:, 0:1]).then_inc(s["mem_std"], 1)
            for k in range(KD):
                act.wait_ge(s["mem_turned"], k + 1)
                af(memT[:, k, :], bank[k % 2][:, 0:NMEM], ACT.Copy, scale=pc2[:, E_MEM + k:E_MEM + k + 1]).then_inc(s["mem_ready"], 1)

            def load_bias(h):
                act.dma_start(toep[:, h % 2, :], a["bias_rows"][h]).then_inc(s[f"toep_in{h % 2}"], 16)

            load_bias(0)
            load_bias(1)
            norm(2 * L, 48, None)
            norm(2 * L + 1, 56, None)
            for h in range(2 * IN2):
                act.wait_ge(s["tiles_done"], tiles(L, h + 1))
                if h < 4:
                    af(xr[:, h, 3:T + 3], bank[h % 2][:, :], ACT.Copy).then_inc(s["acc_copied"], 1)
                elif h < 16:
                    af(qk[:, h, :], bank[h % 2][:, :], ACT.Copy).then_inc(s["acc_copied"], 1)
                else:
                    c = (h - 16) * P
                    af(v[:, :, c:c + P], bank[h % 2][:, :].rearrange("p (t c) -> p t c", t=NT), ACT.Copy).then_inc(s["acc_copied"], 1)
                if 8 <= h < 12:
                    c = h - 8
                    if c >= 1:
                        act.wait_ge(s["rec_ready"], c)
                    for m, g in enumerate((r_gate, i_gate)):
                        act.wait_ge(s["gate_done"], 2 * c + m + 1)
                        at = (E_BA, E_BX)[m] + c
                        af(g, bank[2 + 2 * (c % 2) + m][:, :], ACT.Sigmoid, bias=pc2[:, at:at + 1]).then_inc(s["gates_ready"], 1)
                    act.wait_ge(s["gates_ready"], 2 * c + 1)
                    af(a_rec, r_gate, ACT.Exp, scale=pc2[:, NPRM2 + c:NPRM2 + c + 1]).then_inc(s["rec_act"], 1)
                    af(u_tmp, r_gate, ACT.Tanh, scale=pc2[:, NPRM2 + 4 + c:NPRM2 + 5 + c]).then_inc(s["rec_act"], 1)
                    act.wait_ge(s["rec_u"], c + 1)
                    af(u_tmp, h_rec, ACT.Sqrt).then_inc(s["rec_act"], 1)
                    af(g_rec, qk[:, 4 + c, :], ACT.Gelu_apprx_tanh).then_inc(s["rec_act"], 1)

            def next_bias(job):
                if job[3] == NT - 1 and job[1] + 2 < HEADS2:
                    load_bias(job[1] + 2)

            attention(JOBS2, UNIT02, L * UNITS, L * len(JOBS), L * HEADS, L * PAIRS, lambda job: HD ** -0.5, lambda p: hT[:, 4 + p, :], next_bias)
            for grp in range(2):
                q0 = 6 * KD + CT * grp
                if grp:
                    act.wait_ge(s["h_ready"], 5 * KD + 1)
                for k in range(CT):
                    act.wait_ge(s["sq_used"], q0 + k - 1)
                    if grp:
                        act.wait_ge(s["o_copied"], L * PAIRS + k + 1)
                        src = hT[:, CT + k, :]
                    else:
                        act.wait_ge(s["rec_ready"], k + 1)
                        src = xc[:, k, :]
                    af(sq[:, k % 2, :], src, ACT.Square).then_inc(s["sq_ready"], 1)
                act.wait_ge(s["sq_used"], q0 + CT)
                af(std[:, :], bank[7][:, :], ACT.Sqrt, bias=epsc[:, 0:1]).then_inc(s["std_ready"], 1)
            for h in range(16):
                act.wait_ge(s["tiles_done"], tiles(L, 2 * (IN2 + OUT2) + h + 1))
                if h < 8:
                    af(xk[:, h, :], bank[h % 2][:, 0:NMEM], ACT.Copy).then_inc(s["acc_copied"], 1)
                else:
                    c = (h - 8) * P
                    af(xv[:, :, c:c + P], bank[h % 2][:, 0:2 * P].rearrange("p (t c) -> p t c", t=2), ACT.Copy).then_inc(s["acc_copied"], 1)
            norm(7, 64, None)
            for h in range(8):
                act.wait_ge(s["tiles_done"], tiles(L, 2 * (IN2 + OUT2 + 8) + h + 1))
                af(xq[:, h, :], bank[h % 2][:, :], ACT.Copy).then_inc(s["acc_copied"], 1)
            U, J, G = L * UNITS + len(JOBS2), L * len(JOBS) + len(JOBS2), L * HEADS + HEADS2
            n = XHEADS * NT
            for j in range(n + 4):
                if j < n:
                    act.wait_ge(s["max_ready"], U + j + 1)
                    if j >= NS:
                        act.wait_ge(s["t_done"], J + j - NS + 1)
                    af(S[:, j % NS, 0:NMEM], bank[j % NS][:, 0:NMEM], ACT.Exp, scale=XDIM ** -0.5, bias=mx[:, 1, j % 8:j % 8 + 1],
                       accum_out=mx[:, 2, j % 8:j % 8 + 1]).then_inc(s["exp_done"], 1)
                if 2 <= j < n + 2:
                    jj = j - 2
                    g, qb = divmod(jj, NT)
                    act.wait_ge(s["t_done"], J + jj + 1)
                    if qb == 0 and g >= 2:
                        act.wait_ge(s["pv_done"], G + g - 1)
                    af(PT[:, g % 2, 0:2, qb * P:(qb + 1) * P], bank[4 + jj % 2][:, 0:2 * P].rearrange("p (k q) -> p k q", q=P), ACT.Copy).then_inc(s["pt_ready"], 1)
                if j >= 4 and (j - 4) % NT == NT - 1:
                    g = (j - 4) // NT
                    act.wait_ge(s["pv_done"], G + g + 1)
                    for dt in range(2):
                        af(hT[:, 2 * g + dt, :], bank[6 + dt][:, :], ACT.Copy).then_inc(s["o_copied"], 1)
            norm(8, 72, None)
            for n in range(2 * NT):
                t, c = divmod(n, 2)
                act.wait_ge(s["h_tok_turned"], n + 1)
                af(big[:, t * D + c * T:t * D + (c + 1) * T], bank[n % 2][:, :], ACT.Copy).then_inc(s["h_tok_ready"], 1)
            for n in range(2 * NT):
                t, c = divmod(n, 2)
                act.wait_ge(s["x_tok_turned"], n + 1)
                af(xtok[:, t, c * T:(c + 1) * T], bank[n % 2][:, :], ACT.Copy).then_inc(s["x_tok_ready"], 1)
            act.wait_ge(s["group_shifted"], 1)
            af(rg4[:, 0, :, :], rg4[:, 0, :, :], ACT.Exp).then_inc(s["sel_exp"], 1)
            act.wait_ge(s["second_shifted"], 1)
            af(rsm[:, 4, :], rsm[:, 4, :], ACT.Exp).then_inc(s["sel_exp"], 1)

            def send_rows(b, par):
                act.wait_ge(s["y_ready"], b * 2 + 2)
                act.dma_start(ys_dram[bass.ds(b * BLK, BLK), :], ysb[:, par, :]).then_inc(s[f"y_out{par}"], 16)

            def expert_silu(b, first=False):
                act.wait_ge(s["gate_e_done"], b + 1)
                if not first:
                    act.wait_ge(s["act_e"], b)
                af(eg, bank[0][:, :], ACT.Silu).then_inc(s["silu_e"], 1)

            def copy_act(b):
                act.wait_ge(s["actT_turned"], b + 1)
                af(eaT, bank[6][:, :].rearrange("p (k c) -> p k c", k=4), ACT.Copy).then_inc(s["actT_ready"], 1)

            expert_silu(0, True)
            expert_silu(1)
            copy_act(0)
            with act.Fori(1, BLOCKS // 2) as g:
                for par in range(2):
                    expert_silu(g * 2 + par)
                    copy_act(g * 2 + (par - 1))
                    send_rows(g * 2 + (par - 2), par)
            copy_act(BLOCKS - 1)
            send_rows(BLOCKS - 2, 0)
            send_rows(BLOCKS - 1, 1)
            for t in range(NT):
                act.wait_ge(s["y_used"], 2 * t + 2)
                af(ysb[:, 0, :], xtok[:, t, :], ACT.Square, accum_out=small[:, 32 + t:33 + t]).then_inc(s["fin_sq"], 1)
                act.wait_ge(s["fin_sq"], t + 1)
                af(small[:, 36 + t:37 + t], small[:, 32 + t:33 + t], ACT.Sqrt, scale=1.0 / D, bias=epsc[:, 0:1]).then_inc(s["fin_std"], 1)

        @block.vector
        def _(dve):
            vec = nc.vector
            base = [0, 0]

            def link(ins):
                base[1] += 1
                ins.then_inc(s["chain"], 1)
                dve.wait_ge(s["chain"], base[0] + base[1])

            def stt(out, in0, sc, in1, op0, op1):
                return vec.scalar_tensor_tensor(out=out, in0=in0, scalar=sc, in1=in1, op0=op0, op1=op1)

            def log_sigmoid(z, e, t, out, announce, wait_exp):
                stt(e, z, -1.0, z, ALU.mult, ALU.max).then_inc(announce, 1)
                wait_exp()
                link(vec.tensor_scalar(t, e, 2.0, None, ALU.add))
                link(vec.reciprocal(t, t))
                link(vec.tensor_tensor(e, e, t, ALU.mult))
                link(vec.tensor_tensor(t, e, e, ALU.mult))
                link(vec.tensor_scalar(out, t, ATANH[0], None, ALU.mult))
                for c in ATANH[1:]:
                    link(stt(out, out, c, t, ALU.add, ALU.mult))
                link(stt(out, out, 1.0, e, ALU.add, ALU.mult))
                link(vec.tensor_scalar(t, z, 0.0, None, ALU.min))
                link(stt(out, out, -2.0, t, ALU.mult, ALU.add))

            vec.memset(epsc[:, 0:1], NORM_EPS)
            vec.memset(epsc[:, 1:2], SUBLN_EPS)
            vec.memset(one6[:, :], 1.0)
            vec.memset(gpad[:, :, :], 0.0)
            vec.memset(pcall[:, :, :], 0.0)
            vec.memset(zero[:, :], 0)
            link(vec.memset(wgate[:, :, :, :], 0.0))
            vec.memset(small[:, :], 0.0).then_inc(s["setup_ready"], 1)
            dve.wait_ge(s["setup_ready"], 1)
            dve.wait_ge(s["rows_turned"], 4)
            link(vec.tensor_copy(small[:, 8:16], bank[0][:, 96:104]))
            vec.memset(small[:, 60:61], 0.0).then_inc(s["cols_copied"], 1)
            for l in range(DEPTH):
                vec.tensor_copy(pcall[:, l, 0:NPRM], bank[1 + l][:, 0:NPRM])
                vec.tensor_copy(pcall[:, l, C_MOD:NCOL], bank[0][:, l * 48:(l + 1) * 48])
            link(vec.tensor_copy(pc2[:, 0:NPRM2], bank[3][:, 0:NPRM2]))
            dve.wait_ge(s["fb_in"], 16)
            for l in range(DEPTH):
                link(vec.tensor_copy(pcall[0:C_HEADS, l, 106:107], fb[:, l:l + 1]))
            dve.wait_ge(s["lam_in"], 16)
            for l in range(DEPTH):
                for m in range(2):
                    link(vec.tensor_tensor(lamp[:, l, 2 * m, :], lamp[:, l, 2 * m, :], lamp[:, l, 2 * m + 1, :], ALU.mult))
                    link(vec.tensor_reduce(small[:, 16 + 2 * l + m:17 + 2 * l + m], lamp[:, l, 2 * m, :], AX.X, ALU.add))
            vec.memset(small[:, 60:61], 0.0).then_inc(s["cols_copied"], 1)
            dve.wait_ge(s["lam_exp"], 1)
            for l in range(DEPTH):
                lam_init = 0.8 - 0.6 * math.exp(-0.3 * l)
                link(vec.tensor_tensor(small[:, 28:29], small[:, 21 + 2 * l:22 + 2 * l], small[:, 20 + 2 * l:21 + 2 * l], ALU.subtract))
                link(vec.tensor_scalar(pcall[:, l, C_LAM:C_LAM + 1], small[:, 28:29], -lam_init, None, ALU.add))
                link(vec.tensor_scalar(pcall[:, l, C_SUB:C_SUB + 1], pcall[:, l, C_SUB:C_SUB + 1], 1.0 - lam_init, None, ALU.mult))
            log_sigmoid(pc2[:, E_LAM:E_LAM + CT], small[:, 40:44], small[:, 44:48], small[:, 48:52], s["lam2_abs"],
                        lambda: dve.wait_ge(s["lam2_exp"], 1))
            vec.tensor_scalar(pc2[:, NPRM2:NPRM2 + CT], small[:, 48:52], 8.0, None, ALU.mult)
            vec.tensor_scalar(pc2[:, NPRM2 + CT:NPRM2 + 2 * CT], small[:, 48:52], -8.0, None, ALU.mult)
            dve.wait_ge(s["consts_in"], 16)
            vec.tensor_copy(tokid[:, :], kc[:, K_TOK:K_TOK + NT])
            for k in range(KD):
                dve.wait_ge(s["x_turned"], k + 1)
                vec.tensor_copy(xT[:, k, :], bank[4 + k % 2][:, :]).then_inc(s["x_updated"], 1)

            def mod_acc(steps, w, acc):
                vec.tensor_scalar(acc, w[:, 0, :], small[:, 0:1], None, ALU.mult).then_inc(s["mod_step"], 1)
                for k in range(1, KD):
                    dve.wait_ge(s["mod_step"], steps + k)
                    ins = stt(acc, w[:, k, :], small[:, k:k + 1], acc, ALU.mult, ALU.add)
                    ins.then_inc(s["mod_step" if k < KD - 1 else "mod_used"], 1)

            dve.wait_ge(s["silu_c"], 1)
            for c in range(MOD_FIRST):
                dve.wait_ge(s[f"mod_in{c % RING}"], 16 * (c // RING + 1))
                if c >= 4:
                    dve.wait_ge(s["mod_turned"], c - 3)
                mod_acc(c * (KD - 1), wring[:, c % RING, :, :], modacc[:, c % 4, :])
            dve.wait_ge(s["mod_turned"], MOD_FIRST)
            link(vec.tensor_tensor(pcall[:, 0, SH1:GT1], pcall[:, 0, SH1:GT1], bank[6][:, 0:2 * KD], ALU.add))

            def mod_pair(l, pair):
                for q in (2 * pair, 2 * pair + 1):
                    dve.wait_ge(s[f"mod_next{q % 2}"], l * (8 * MOD_CHUNKS) + 16 * (q // 2 + 1))
                    if q >= 4:
                        dve.wait_ge(s["mod_turned"], l * MOD_CHUNKS + (MOD_FIRST + q - 3))
                    mod_acc((l * MOD_CHUNKS + (MOD_FIRST + q)) * (KD - 1), mod_w[:, q % 2, :, :], modacc[:, q % 4, :])

            def norm(n, g, table, shift, stds=None, out=hT, done="h_ready", split=None):
                dve.wait_ge(s["std_ready"], (n if stds is None else stds) + 1)
                link(vec.reciprocal(rs[:, :], std[:, :]))
                for k in range(KD):
                    if shift:
                        if k >= 1 and split is not None:
                            h_rest(split, n, k - 1)
                        if k >= 2:
                            dve.wait_ge(s["h_ready"], n * KD + (k - 1))
                            if split is not None:
                                dve.wait_ge(s["h_lo_ready"], split * KD + (k - 1))
                        stt(hn[:, k % 2, :], xT[:, k, :], table[:, g + k:g + k + 1], rs[:, :], ALU.mult, ALU.mult).then_inc(s["hn_ready"], 1)
                    else:
                        stt(out[:, k, :], xT[:, k, :], table[:, g + k:g + k + 1], rs[:, :], ALU.mult, ALU.mult).then_inc(s[done], 1)

            def h_rest(l, n, k):
                dve.wait_ge(s["h_ready"], n * KD + (k + 1))
                stt(h_lo[:, k, :], hn[:, k % 2, :], pc[:, SH2 + k:SH2 + k + 1], hT_r[:, k, :], ALU.add, ALU.subtract).then_inc(s["h_lo_ready"], 1)

            def split_lo(l, n):
                i = IN_SLOTS + OUT_SLOTS + n
                for piece in range(n_pieces(i)):
                    dve.wait_ge(s["hi_ready"], pieces(l, i) + (piece + 1))
                    vec.tensor_tensor(w_slot(arena_r, i, piece), w_slot(arena, i, piece), w_hi[i % 2][piece], ALU.subtract).then_inc(s["lo_ready"], 1)

            def gated_split_lo(l, f):
                dve.wait_ge(s["gated_hi"], l * FT + (f + 1))
                vec.tensor_tensor(gated_lo[:, f % FH, :], gated_full[:, f % FH, :], gated_hi[:, f % FH, :], ALU.subtract).then_inc(s["gated_lo_ready"], 1)

            def add_to_x(d, b, gate):
                if gate is None:
                    ins = vec.tensor_tensor(xT[:, d, :], xT[:, d, :], b[:, :], ALU.add)
                else:
                    ins = stt(xT[:, d, :], b[:, :], pc[:, gate + d:gate + d + 1], xT[:, d, :], ALU.mult, ALU.add)
                ins.then_inc(s["x_updated"], 1)

            def attention(jobs, unit0, U, J, scale_of, mask_of, before=None):
                n = len(jobs)
                job_of = [i for i in range(n) for _ in range(unit0[i + 1] - unit0[i])]
                for j in range(n + 1):
                    if j < n:
                        kind, h, g, qb = jobs[j]
                        w = (qb + 1) * P
                        if before is not None:
                            before(jobs[j])
                        for m in range(unit0[j + 1] - unit0[j]):
                            u = unit0[j] + m
                            dve.wait_ge(s["s_done"], U + (u + 1))
                            if u >= 2 * NS:
                                dve.wait_ge(s["t_done"], J + (job_of[u - 2 * NS] + 1))
                            c = u % 8
                            vec.memset(small[:, 59:60], 0.0)
                            link(vec.tensor_tensor_reduce(probs(u)[:, 0:w], bank[u % NS][:, 0:w], mask_of(jobs[j])[:, T - w:T], 1.0, -3.0e38,
                                                          ALU.add, ALU.max, mx[:, 0, c:c + 1]))
                            vec.tensor_scalar(mx[:, 1, c:c + 1], mx[:, 0, c:c + 1], -scale_of(jobs[j]), None, ALU.mult).then_inc(s["max_ready"], 1)
                    if j >= 1:
                        jj = j - 1
                        kind, h, g, qb = jobs[jj]
                        w = (qb + 1) * P
                        u0, u1 = unit0[jj], unit0[jj + 1] - 1
                        dve.wait_ge(s["exp_done"], U + (u1 + 1))
                        for u in range(u0, u1 + 1):
                            link(vec.reciprocal(mx[:, 0, u % 8:u % 8 + 1], mx[:, 2, u % 8:u % 8 + 1]))
                        r = mx[:, 0, u0 % 8:u0 % 8 + 1]
                        if u1 == u0:
                            vec.tensor_scalar(probs(u0)[:, 0:w], probs(u0)[:, 0:w], r, None, ALU.mult).then_inc(s["p_ready"], 1)
                        else:
                            r1 = mx[:, 0, u1 % 8:u1 % 8 + 1]
                            link(vec.tensor_tensor(r1, r1, pc[:, C_LAM:C_LAM + 1], ALU.mult))
                            link(vec.tensor_scalar(probs(u0)[:, 0:w], probs(u0)[:, 0:w], r, None, ALU.mult))
                            stt(probs(u1)[:, 0:w], probs(u1)[:, 0:w], r1, probs(u0)[:, 0:w], ALU.mult, ALU.add).then_inc(s["p_ready"], 1)

            CH0 = base[1]
            with dve.Fori(0, DEPTH) as l:
                base[0], base[1] = l * CH_LAYER + CH0, 0
                dve.wait_ge(s["x_updated"], l * 24 + KD)
                link(vec.tensor_copy(pc[:, :].rearrange("p (o c) -> p o c", o=1), pcall[:, bass.ds(l, 1), :]))
                link(stt(pc[:, C_GA:C_GA + KD], pc[:, SC1:SC1 + KD], 1.0, pc[:, C_GA:C_GA + KD], ALU.add, ALU.mult))
                vec.tensor_copy(small[:, 61:62], pc[:, 0:1]).then_inc(s["table_ready"], 1)
                norm(2 * l, C_GA, pc, True)
                for r, h in enumerate(ROPE):
                    dve.wait_ge(s["acc_copied"], l * 24 + (h + 1))
                    co, si = (K_CA, K_SA) if h < 4 else (K_CB, K_SB)
                    link(vec.tensor_tensor(t1[:, r % 2, :], raw[:, r % 2, :], kc[:, co:co + T], ALU.mult))
                    dve.wait_ge(s["rot_done"], l * len(ROPE) + (r + 1))
                    link(vec.tensor_tensor(rot[:, r % 2, :], bank[2 + r % 2][:, :], kc[:, si:si + T], ALU.mult))
                    vec.tensor_tensor(qk[:, QK_OF[h], :], t1[:, r % 2, :], rot[:, r % 2, :], ALU.add).then_inc(s["rope_done"], 1)
                    if h % 2:
                        mod_pair(l, h // 2)
                    if h == 3:
                        mod_pair(l, 2)
                mod_pair(l, 6)
                dve.wait_ge(s["z_ready"], l + 1)
                log_sigmoid(z6[:, 0, :], z6[:, 1, :], z6[:, 2, :], z6[:, 3, :], s["z_abs"],
                            lambda: (mod_pair(l, 7), dve.wait_ge(s["z_exp"], l + 1)))
                vec.tensor_tensor_scan(F6[:, :], one6[0:C_HEADS, :], z6[:, 3, :], 0.0, ALU.mult, ALU.add).then_inc(s["decay_ready"], 1)
                with dve.If(l < DEPTH - 1):
                    for pair in range(MOD_PAIRS, MOD_PAIRS + NEXT_PAIRS):
                        mod_pair(l, pair)
                    dve.wait_ge(s["mod_turned"], l * MOD_CHUNKS + (MOD_CHUNKS + MOD_FIRST))
                    nxt = pcall[:, bass.ds(next_layer(l), 1), SH1:GT1]
                    vec.tensor_tensor(nxt, nxt, bank[5][:, 0:2 * KD].rearrange("p (o c) -> p o c", o=1), ALU.add).then_inc(s["next_added"], 1)
                dve.wait_ge(s["mod_turned"], l * MOD_CHUNKS + (MOD_FIRST + 2 * MOD_PAIRS))
                link(vec.tensor_tensor(pc[:, GT1:NCOL], pc[:, GT1:NCOL], bank[6][:, 2 * KD:6 * KD], ALU.add))
                link(stt(pc[:, C_GM:C_GM + KD], pc[:, SC2:SC2 + KD], 1.0, pc[:, C_GM:C_GM + KD], ALU.add, ALU.mult))
                attention(JOBS, UNIT0, l * UNITS, l * len(JOBS), lambda job: (HD // 2 if job[0] == "A" else HD) ** -0.5,
                          lambda job: kc[:, K_MB:K_MB + T] if job[0] == "B" else kc[:, K_MA:K_MA + T])
                dve.wait_ge(s["o_copied"], l * PAIRS + 2)
                for t in range(2):
                    vec.tensor_tensor(sub_tmp(t), hT[:, t, :], hT[:, t, :], ALU.mult).then_inc(s["sub_sq"], 1)
                for t in range(2):
                    dve.wait_ge(s["sub_std"], l * 2 + (t + 1))
                    link(vec.reciprocal(sub_tmp(t), sub_dev(t)))
                    stt(hT[:, t, :], hT[:, t, :], pc[:, C_SUB:C_SUB + 1], sub_tmp(t), ALU.mult, ALU.mult).then_inc(s["sub_done"], 1)
                for d in range(KD):
                    dve.wait_ge(s["tiles_done"], tiles(l, CUM[IN_SLOTS] + d + 1))
                    add_to_x(d, bank[d % 2], GT1)
                split_lo(l, 0)
                norm(2 * l + 1, C_GM, pc, True, split=l)
                h_rest(l, 2 * l + 1, KD - 1)
                for n in range(MLP_SLOTS):
                    if n + 1 < MLP_SLOTS:
                        split_lo(l, n + 1)
                    hh, f = divmod(n, UP_SLOTS + DOWN_SLOTS)
                    if f < UP_SLOTS:
                        f += hh * FH
                        if f % FH:
                            gated_split_lo(l, f - 1)
                        dve.wait_ge(s["gpad_ready"], l * FT + (f + 1))
                        col = lambda i: pc[:, C_CW + i * FT + f:C_CW + i * FT + f + 1]
                        link(vec.tensor_scalar(y[:, f % 2, :], gpad[:, f % 2, 2:T + 2], col(2), pc[:, C_CB + f:C_CB + f + 1], ALU.mult, ALU.add))
                        link(stt(y[:, f % 2, :], gpad[:, f % 2, 1:T + 1], col(1), y[:, f % 2, :], ALU.mult, ALU.add))
                        stt(y[:, f % 2, :], gpad[:, f % 2, 0:T], col(0), y[:, f % 2, :], ALU.mult, ALU.add).then_inc(s["conv_done"], 1)
                        dve.wait_ge(s["silu_done"], l * FT + (f + 1))
                        vec.tensor_tensor(gated_full[:, f % FH, :], sg[:, f % 2, :], bank[4 * hh + 2 * (f % 2)][:, :], ALU.mult).then_inc(s["act_ready"], 1)
                        if f % FH == FH - 1:
                            gated_split_lo(l, f)
                    elif f == UP_SLOTS + DOWN_SLOTS - 1:
                        for d in range(KD):
                            dve.wait_ge(s["down_done"], l * 2 * KD + (2 * KD + KD * hh + d + 1))
                            add_to_x(d, bank[(d + 4 - 4 * hh) % 8], GT2)
                assert base[1] == CH_LAYER, (base[1], CH_LAYER)
            base[0], base[1] = CH0 + DEPTH * CH_LAYER, 0

            L = DEPTH
            vec.memset(xr[:, :, 0:3], 0.0)
            dve.wait_ge(s["mem_std"], 1)
            link(vec.reciprocal(small[:, 26:28], small[:, 26:28]))
            for m in range(2):
                vec.tensor_scalar(mem_tok[:, m, :], mem_tok[:, m, :], small[:, 26 + m:27 + m], None, ALU.mult).then_inc(s["mem_scaled"], 1)
            norm(2 * L, E_FIN, pc2, False, out=xT, done="x_updated")
            dve.wait_ge(s["x_updated"], 64)
            norm(2 * L + 1, E_LN1, pc2, False)
            for c in range(CT):
                dve.wait_ge(s["acc_copied"], L * 24 + c + 1)
                w = lambda i: pc2[:, E_CW + i * CT + c:E_CW + i * CT + c + 1]
                link(vec.tensor_scalar(xc[:, c, :], xr[:, c, 3:T + 3], w(3), pc2[:, E_CB + c:E_CB + c + 1], ALU.mult, ALU.add))
                for i in (2, 1, 0):
                    ins = stt(xc[:, c, :], xr[:, c, i:i + T], w(i), xc[:, c, :], ALU.mult, ALU.add)
                    if i:
                        link(ins)
                ins.then_inc(s["conv2_ready"], 1)
            for c in range(CT):
                dve.wait_ge(s["rec_act"], 4 * c + 2)
                link(vec.tensor_scalar(h_rec, u_tmp, 1.0, None, ALU.add))
                link(vec.reciprocal(h_rec, h_rec))
                stt(h_rec, h_rec, 2.0, u_tmp, ALU.mult, ALU.mult).then_inc(s["rec_u"], 1)
                dve.wait_ge(s["gates_ready"], 2 * c + 2)
                link(vec.tensor_tensor(xc[:, c, :], xc[:, c, :], i_gate, ALU.mult))
                dve.wait_ge(s["rec_act"], 4 * c + 4)
                link(vec.tensor_tensor(xc[:, c, :], xc[:, c, :], u_tmp, ALU.mult))
                link(vec.tensor_tensor_scan(h_rec, a_rec, xc[:, c, :], 0.0, ALU.mult, ALU.add))
                vec.tensor_tensor(xc[:, c, :], h_rec, g_rec, ALU.mult).then_inc(s["rec_ready"], 1)

            def ready_bias(job):
                if job[3] == 0:
                    h = job[1]
                    dve.wait_ge(s[f"toep_in{h % 2}"], 16 * (h // 2 + 1))
                    bias = toep[:, h % 2, :]
                    link(vec.tensor_scalar(bias, bias, float(HD) ** 0.5, None, ALU.mult))
                    link(vec.memset(toep[0:HD, h % 2, T - HD:T], NEG))

            attention(JOBS2, UNIT02, L * UNITS, L * len(JOBS), lambda job: HD ** -0.5, lambda job: toep[:, job[1] % 2, :], ready_bias)
            for grp, g in enumerate((E_GR, E_GA)):
                dve.wait_ge(s["std_ready"], 7 + grp)
                if grp:
                    dve.wait_ge(s["h_ready"], 5 * KD + CT)
                link(vec.reciprocal(rs[:, :], std[:, :]))
                for k in range(CT):
                    src = hT[:, CT + k, :] if grp else xc[:, k, :]
                    stt(hT[:, CT * grp + k, :], src, pc2[:, g + k:g + k + 1], rs[:, :], ALU.mult, ALU.mult).then_inc(s["h_ready"], 1)

            def to_x(i):
                for d in range(KD):
                    dve.wait_ge(s["tiles_done"], tiles(L, 2 * i + d + 1))
                    add_to_x(d, bank[d % 2], None)

            to_x(IN2)
            norm(7, E_LN2, pc2, False, stds=8)
            U, J = L * UNITS + len(JOBS2), L * len(JOBS) + len(JOBS2)
            n = XHEADS * NT
            for j in range(n + 1):
                if j < n:
                    c = j % 8
                    dve.wait_ge(s["s_done"], U + j + 1)
                    link(vec.tensor_reduce(mx[:, 0, c:c + 1], bank[j % NS][:, 0:NMEM], AX.X, ALU.max))
                    vec.tensor_scalar(mx[:, 1, c:c + 1], mx[:, 0, c:c + 1], -XDIM ** -0.5, None, ALU.mult).then_inc(s["max_ready"], 1)
                if j >= 1:
                    c = (j - 1) % 8
                    dve.wait_ge(s["exp_done"], U + j)
                    link(vec.reciprocal(mx[:, 0, c:c + 1], mx[:, 2, c:c + 1]))
                    buf = S[:, (j - 1) % NS, 0:NMEM]
                    vec.tensor_scalar(buf, buf, mx[:, 0, c:c + 1], None, ALU.mult).then_inc(s["p_ready"], 1)
            to_x(IN2 + OUT2 + 12)
            norm(8, E_LN3, pc2, False, stds=9)

            dve.wait_ge(s["logits_done"], 1)
            tt = vec.tensor_tensor
            link(tt(rlog[:, :, :], bank[6][:, 0:NT * NR].rearrange("p (t n) -> p t n", t=NT), rb[:, :].unsqueeze(1).to_broadcast([P, NT, NR]), ALU.add))

            def first_max(val, n, top, key, onehot):
                b = lambda x: x.unsqueeze(2).to_broadcast([P, NT, n])
                order = kc[:, K_EI:K_EI + n].unsqueeze(1).to_broadcast([P, NT, n])
                link(vec.tensor_reduce(top, val, AX.X, ALU.max))
                link(tt(key, val, b(top), ALU.is_ge))
                link(tt(key, key, order, ALU.mult))
                link(vec.tensor_reduce(rsm[:, 9, :], key, AX.X, ALU.max))
                link(tt(onehot, key, b(rsm[:, 9, :]), ALU.is_equal))

            glog = rlog[:, :, 0:GROUPS]
            first_max(glog, GROUPS, rsm[:, 0, :], rg4[:, 1, :, :], rg4[:, 2, :, :])
            tt(rg4[:, 0, :, :], glog, rsm[:, 0, :].unsqueeze(2).to_broadcast([P, NT, GROUPS]), ALU.subtract).then_inc(s["group_shifted"], 1)
            link(vec.tensor_scalar(rg4[:, 2, :, :], rg4[:, 2, :, :], 1.0, -NEG, ALU.subtract, ALU.mult))
            el = rt[:, 0, :, :]
            for t in range(NT):
                ins = tt(el[:, t, :].rearrange("p (g e) -> p g e", g=GROUPS), rlog[:, t, GROUPS:NR].rearrange("p (g e) -> p g e", g=GROUPS),
                         rg4[:, 2, t, :].unsqueeze(2).to_broadcast([P, GROUPS, PER_GROUP]), ALU.add)
            link(ins)
            first_max(el, EXPERTS, rsm[:, 1, :], rt[:, 1, :, :], rt[:, 2, :, :])
            link(stt(el, rt[:, 2, :, :], 3.0 * NEG, el, ALU.mult, ALU.add))
            first_max(el, EXPERTS, rsm[:, 2, :], rt[:, 1, :, :], rt[:, 3, :, :])
            tt(rt[:, 5, :, :], rt[:, 2, :, :], rt[:, 3, :, :], ALU.add).then_inc(s["sel_ready"], 1)
            tt(rsm[:, 4, :], rsm[:, 2, :], rsm[:, 1, :], ALU.subtract).then_inc(s["second_shifted"], 1)
            dve.wait_ge(s["sel_exp"], 1)
            link(vec.tensor_reduce(rsm[:, 5, :], rg4[:, 0, :, :], AX.X, ALU.add))
            dve.wait_ge(s["sel_exp"], 2)
            link(vec.tensor_scalar(rsm[:, 6, :], rsm[:, 4, :], 1.0, None, ALU.add))
            link(tt(rsm[:, 6, :], rsm[:, 6, :], rsm[:, 5, :], ALU.mult))
            link(vec.reciprocal(rsm[:, 7, :], rsm[:, 6, :]))
            link(tt(rsm[:, 8, :], rsm[:, 7, :], rsm[:, 4, :], ALU.mult))
            dve.wait_ge(s["count_done"], 1)
            link(vec.tensor_scalar(e32[:, 0, :], bank[5][:, 0:EXPERTS], float(BLK - 1), None, ALU.add))
            link(vec.tensor_copy(i32[:, 0, :], e32[:, 0, :]))
            shift = int(math.log2(BLK))
            link(vec.tensor_scalar(i32[:, 1, :], i32[:, 0, :], shift, shift, ALU.arith_shift_right, ALU.logical_shift_left))
            link(vec.tensor_copy(e32[:, 1, :], i32[:, 1, :]))
            link(vec.tensor_tensor_scan(e32[:, 2, :], one6[:, 0:EXPERTS], e32[:, 1, :], 0.0, ALU.mult, ALU.add))
            link(tt(e32[:, 3, :], e32[:, 2, :], e32[:, 1, :], ALU.subtract))
            pos = rt[:, 4, :, :]
            link(tt(pos, bank[4][:, 0:NT * EXPERTS].rearrange("p (t e) -> p t e", t=NT), e32[:, 3, :].unsqueeze(1).to_broadcast([P, NT, EXPERTS]), ALU.add))
            for j in range(2):
                link(tt(rt[:, 1, :, :], rt[:, 2 + j, :, :], pos, ALU.mult))
                link(vec.tensor_reduce(rsm[:, 10 + j, :], rt[:, 1, :, :], AX.X, ALU.add))
                vec.tensor_copy(dest[:, j, :], rsm[:, 10 + j, :]).then_inc(s["dest_ready"], 1)
            cmp = S[:, 0:3, :].rearrange("p a t -> p (a t)")[:, 0:BLOCKS * EXPERTS].rearrange("p (b e) -> p b e", b=BLOCKS)
            link(tt(cmp, e32[:, 2, :].unsqueeze(1).to_broadcast([P, BLOCKS, EXPERTS]), kc[:, K_BB:K_BB + BLOCKS].unsqueeze(2).to_broadcast([P, BLOCKS, EXPERTS]), ALU.is_le))
            link(vec.tensor_reduce(std[:, 0:BLOCKS], cmp, AX.X, ALU.add))
            link(vec.tensor_scalar(rs[:, 0:BLOCKS], std[:, 0:BLOCKS], float(EXPERTS), None, ALU.is_lt))
            vec.tensor_copy(blkU[:, :], rs[:, 0:BLOCKS])
            link(vec.tensor_scalar(std[:, 0:BLOCKS], std[:, 0:BLOCKS], float(EXPERTS - 1), None, ALU.min))
            vec.tensor_copy(blkE[:, :], std[:, 0:BLOCKS])
            dve.wait_ge(s["src_in"], 16)
            vec.tensor_copy(src_f[:, :], src_i[:, :]).then_inc(s["src_float"], 1)
            dve.wait_ge(s["src_turned"], 1)
            vec.tensor_copy(src_c[:, :], bank[6][:, 0:BLOCKS]).then_inc(s["plan_ready"], 1)

            def expert_dve(b, par, n, level):
                dve.wait_ge(s["xe_turned"], b + 1)
                if level == 2:
                    dve.wait_ge(s["up_e_done"], b - 1)
                vec.tensor_copy(xsT[:, par, 0:4, :], bank[4][:, :].rearrange("p (k c) -> p k c", k=4))
                vec.tensor_copy(xsT[:, par, 4:8, :], bank[5][:, :].rearrange("p (k c) -> p k c", k=4)).then_inc(s["xeT_ready"], 1)

            def expert_out(b, par, n, level):
                dve.wait_ge(s["silu_e"], b + 1)
                dve.wait_ge(s["up_e_done"], b + 1)
                if level:
                    dve.wait_ge(s["actT_turned"], b)
                tt(ea, eg, bank[1][:, :], ALU.mult).then_inc(s["act_e"], 1)

            def expert_copy(b, par, n, level):
                if level == 2:
                    dve.wait_ge(s[f"y_out{par}"], n * 16)
                for c in range(2):
                    dve.wait_ge(s["e_down_done"], b * 2 + (c + 1))
                    vec.tensor_copy(ysb[:, par, c * T:(c + 1) * T], bank[2 + c][:, :]).then_inc(s["y_ready"], 1)

            expert_dve(0, 0, 0, 0)
            expert_out(0, 0, 0, 0)
            expert_dve(1, 1, 0, 1)
            expert_out(1, 1, 0, 1)
            expert_dve(2, 0, 1, 2)
            expert_copy(0, 0, 0, 0)
            expert_out(2, 0, 1, 2)
            expert_dve(3, 1, 1, 2)
            expert_copy(1, 1, 0, 1)
            expert_out(3, 1, 1, 2)
            expert_dve(4, 0, 2, 2)
            expert_copy(2, 0, 1, 2)
            with dve.Fori(2, BLOCKS // 2 - 1) as g:
                for par in range(2):
                    expert_out(g * 2 + par, par, g, 2)
                    expert_dve(g * 2 + (par + 1), 1 - par, None, 2)
                    expert_copy(g * 2 + (par - 1), 1 - par, g + (par - 1), 2)
            n = BLOCKS // 2 - 1
            expert_out(2 * n, 0, n, 2)
            expert_dve(2 * n + 1, 1, n, 2)
            expert_copy(2 * n - 1, 1, n - 1, 2)
            expert_out(2 * n + 1, 1, n, 2)
            expert_copy(2 * n, 0, n, 2)
            expert_copy(2 * n + 1, 1, n, 2)
            dve.wait_ge(s["fw_in"], 16)
            for t in range(NT):
                dve.wait_ge(s[f"y_got{t}"], 32)
                link(stt(xtok[:, t, :], y_got_t[:, 2 * t, :], rsm[:, 7, t:t + 1], xtok[:, t, :], ALU.mult, ALU.add))
                dve.wait_ge(s["x_tok_ready"], 2 * NT)
                vec.memset(small[:, 60:61], 0.0).then_inc(s["y_used"], 1)
                stt(xtok[:, t, :], y_got_t[:, 2 * t + 1, :], rsm[:, 8, t:t + 1], xtok[:, t, :], ALU.mult, ALU.add).then_inc(s["y_used"], 1)
            for t in range(NT):
                dve.wait_ge(s["fin_std"], t + 1)
                link(vec.reciprocal(small[:, 36 + t:37 + t], small[:, 36 + t:37 + t]))
                stt(xtok[:, t, :], xtok[:, t, :], small[:, 36 + t:37 + t], fw, ALU.mult, ALU.mult).then_inc(s["out_ready"], 1)

        @block.gpsimd
        def _(pool):
            pool.wait_ge(s["setup_ready"], 1)
            pool.dma_start(src_dram.rearrange("(p b) o -> p (b o)", p=P), zero[:, :]).then_inc(s["src_zeroed"], 16)
            pool.wait_ge(s["src_zeroed"], 16)
            pool.wait_ge(s["dest_ready"], 2)
            for j in range(2):
                for t in range(NT):
                    pool.indirect_dma_start(src_dram, bass.IndirectOffsetOnAxis(dest[:, j, t:t + 1], 0), tokid[:, t:t + 1], None).then_inc(s["src_scattered"], 16)
            pool.wait_ge(s["plan_ready"], 1)
            pool.wait_ge(s["h_tok_out"], 16 * NT)
            pool.wait_ge(s["x_tok_turned"], 2 * NT)

            for b in range(BLOCKS):
                if b >= 2:
                    pool.wait_ge(s["xe_turned"], b - 1)
                pool.indirect_dma_start(xs[:, b % 2, :], None, h_dram, bass.IndirectOffsetOnAxis(src_c[:, b:b + 1], 0)).then_inc(s[f"xe_in{b % 2}"], 16)
            for par in range(2):
                pool.wait_ge(s[f"y_out{par}"], 16 * (BLOCKS // 2))
            for t in range(NT):
                for j in range(2):
                    pool.indirect_dma_start(y_got_t[:, 2 * t + j, :], None, ys_dram, bass.IndirectOffsetOnAxis(dest[:, j, t:t + 1], 0)).then_inc(s[f"y_got{t}"], 16)


def constants():
    k = np.zeros((P, NK), np.float32)
    p, pos = np.arange(P), np.arange(T, dtype=np.float32)
    for at_c, at_s, at_r, dim in ((K_CA, K_SA, K_RA, HD // 2), (K_CB, K_SB, K_RB, HD)):
        inv = (1.0 / (np.float32(10000.0) ** (np.arange(0, dim, 2, dtype=np.float32) / np.float32(dim)))).astype(np.float32)
        ang = inv[(p % dim) % (dim // 2)][:, None] * pos[None, :]
        k[:, at_c:at_c + T] = np.cos(ang.astype(np.float64))
        k[:, at_s:at_s + T] = np.sin(ang.astype(np.float64))
        for m in range(P):
            low = m % dim < dim // 2
            k[m + dim // 2 if low else m - dim // 2, at_r + m] = -1.0 if low else 1.0
    dist = p[:, None] - np.arange(T)[None, :] + (T - P)
    k[:, K_MA:K_MA + T] = np.where(dist >= 0, 0.0, NEG)
    c = (dist <= 128).astype(int) + (dist % 4 == 0) + (dist % 16 == 0)
    k[:, K_MB:K_MB + T] = np.where((dist >= 0) & (c > 0), np.sqrt(float(HD)) * np.log(np.maximum(c, 1)), NEG)
    k[:, K_ID:K_ID + P] = np.eye(P)
    k[:, K_ON:K_ON + P] = 1.0
    k[:, K_OD:K_OD + P] = 1.0 / D
    k[:, K_OR:K_OR + P] = 1.0 / D_RNN
    k[:, K_BO:K_BO + P] = (p[:, None] // HD == p[None, :] // HD) / float(HD)
    k[:, K_TRI:K_TRI + P] = p[:, None] < p[None, :]
    for h in range(C_HEADS):
        k[h, K_SEL + h * P:K_SEL + (h + 1) * P] = -np.sqrt(float(HD))
    k[:, K_TOK:K_TOK + NT] = p[:, None] + P * np.arange(NT)[None, :]
    k[:, K_EI:K_EI + EXPERTS] = EXPERTS - np.arange(EXPERTS)[None, :]
    k[:, K_BB:K_BB + BLOCKS] = BLK * np.arange(BLOCKS)[None, :]
    return k


def kernel(**inputs):
    import concourse.bacc as bacc
    from concourse.bass_utils import run_bass_kernel_spmd

    arr = {n: np.ascontiguousarray(x) for n, x in inputs.items()}
    give = {n: arr[n] for n in ("x", "w_mod", "w_in", "w_out", "w_up", "w_down", "diff_lambda", "mem_2", "w_in_2",
                                "w_out_2", "xk_w_2", "xv_w_2", "xq_w_2", "xo_w_2", "rnn_wa_2", "rnn_wx_2",
                                "expert_gate_w_2", "expert_up_w_2", "expert_down_w_2", "final_norm_w_2")}
    rows = lambda x: x.reshape(-1, P)
    give["consts"] = constants()
    give["rows_mod"] = np.concatenate([rows(arr["b_mod"]), rows(arr["c"])])
    give["rows_layer"] = np.stack([np.concatenate([
        rows(arr["g_attn"][l]), rows(arr["g_mlp"][l]), rows(arr["conv_w"][l]), rows(arr["conv_b"][l]),
        np.concatenate([arr["subln_g"][l]] * 2)[None]]) for l in range(DEPTH)])
    give["rows_second"] = np.concatenate([rows(arr[n + "_2"]) for n in (
        "ln1_w", "conv_w", "conv_b", "rnn_ba", "rnn_bx", "rnn_lambda", "gn_rnn_w", "gn_att_w", "ln2_w", "mem_norm_w", "ln3_w")] + [rows(arr["g_final"])])
    give["forget_bias_t"] = np.ascontiguousarray(arr["forget_bias"].T)
    clip = (arr["rel_bias_2"].shape[-1] - 1) // 2
    give["bias_rows"] = np.ascontiguousarray(
        arr["rel_bias_2"][0][:, np.clip(T - P + np.arange(P)[:, None] - np.arange(T)[None, :], -clip, clip) + clip])
    give["router_w"] = np.concatenate([arr["router_group_w_2"][0], arr["router_expert_w_2"][0].transpose(1, 0, 2).reshape(D, EXPERTS)], axis=1)
    give["router_b"] = np.concatenate([arr["router_group_b_2"][0], arr["router_expert_b_2"][0].reshape(-1)])[None]

    nc = bacc.Bacc("TRN2", target_bir_lowering=False, num_devices=1)
    a, send = {}, {}
    for n, x in give.items():
        send["in_" + n] = x
        a[n] = nc.dram_tensor("in_" + n, x.shape, F32, kind="ExternalInput").ap()
    a["out"] = nc.dram_tensor("out", (1, T, D), F32, kind="ExternalOutput").ap()
    a["h_scratch"] = nc.dram_tensor("h_scratch", (T, D), F32, kind="Internal").ap()
    a["y_scratch"] = nc.dram_tensor("y_scratch", (ROWS, D), F32, kind="Internal").ap()
    a["src_scratch"] = nc.dram_tensor("src_scratch", (ROWS, 1), I32, kind="Internal").ap()
    build(nc, a)
    return run_bass_kernel_spmd(nc, [send], core_ids=[0]).results[0]["out"]
```
